# Optimizing a Trainium2 kernel written in Bass

```python
import math
import jax, jax.numpy as jnp
from jax import lax
import numpy as np
import jax
import jax.numpy as jnp

D_MODEL = 1024
BATCH = 1
SEQ = 512
DEPTH = 1

HEAD_DIM = 64
N_HEADS_A = 8
N_KV_A = 2
GROUP_A = N_HEADS_A // N_KV_A
WINDOW_A = 128
N_HEADS_B = 8
DILATED_PATTERNS = ((128, 1), (512, 4), (2048, 16))
WIDTH_A = N_HEADS_A * HEAD_DIM
WIDTH_B = N_HEADS_B * HEAD_DIM
D_MIX = WIDTH_A + WIDTH_B
KV_WIDTH_A = N_KV_A * HEAD_DIM
D_IN_PROJ = WIDTH_A + 2 * KV_WIDTH_A + 3 * WIDTH_B
N_BIAS_HEADS = N_HEADS_A + N_HEADS_B
NUM_BUCKETS = 32
MAX_DISTANCE = 1024
D_FF = 4 * D_MODEL
PLE_DIM = 256
EPS = 1e-6
NEG = -1e30


def rmsnorm(x, g):
    xf = x.astype(jnp.float32)
    y = xf * lax.rsqrt(jnp.mean(xf * xf, axis=-1, keepdims=True) + EPS)
    return (y * g.astype(jnp.float32)).astype(x.dtype)

def t5_bucket(rel):
    half = NUM_BUCKETS // 2
    max_exact = half // 2
    sign = jnp.where(rel > 0, half, 0)
    n = jnp.abs(rel)
    nf = jnp.maximum(n, 1).astype(jnp.float32)
    large = max_exact + (jnp.log(nf / max_exact) / math.log(MAX_DISTANCE / max_exact)
                         * (half - max_exact)).astype(jnp.int32)
    large = jnp.minimum(large, half - 1)
    return sign + jnp.where(n < max_exact, n, large)

def band_rel(block):
    qi = jnp.arange(block)[:, None]
    ki = jnp.arange(3 * block)[None, :]
    return ki - block - qi

def banded_attention(q, k, v, bias, half_window, block, sink):
    b_, hk, g, L, dh = q.shape
    nb = -(-L // block)
    lp = nb * block
    q = jnp.pad(q, ((0, 0), (0, 0), (0, 0), (0, lp - L), (0, 0)))
    kv_pad = ((0, 0), (0, 0), (block, lp - L + block), (0, 0))
    kp = jnp.pad(k, kv_pad).reshape(b_, hk, nb + 2, block, dh)
    vp = jnp.pad(v, kv_pad).reshape(b_, hk, nb + 2, block, dh)
    kw = jnp.concatenate([kp[:, :, :-2], kp[:, :, 1:-1], kp[:, :, 2:]], axis=3)
    vw = jnp.concatenate([vp[:, :, :-2], vp[:, :, 1:-1], vp[:, :, 2:]], axis=3)
    qb = q.reshape(b_, hk, g, nb, block, dh)
    s = jnp.einsum('bhgnqd,bhnkd->bhgnqk', qb, kw).astype(jnp.float32) * (dh ** -0.5)
    s = s + bias[:, :, None]
    rel = band_rel(block)
    kpos = jnp.arange(nb)[:, None, None] * block + jnp.arange(3 * block)[None, None, :] - block
    valid = (jnp.abs(rel) <= half_window)[None] & (kpos >= 0) & (kpos < L)
    s = jnp.where(valid, s, NEG)
    m = jnp.max(s, axis=-1, keepdims=True)
    if sink is not None:
        sinkb = sink.astype(jnp.float32)[None, :, :, None, None, None]
        m = jnp.maximum(m, sinkb)
    e = jnp.exp(s - m)
    denom = jnp.sum(e, axis=-1, keepdims=True)
    if sink is not None:
        denom = denom + jnp.exp(sinkb - m)
    o = jnp.einsum('bhgnqk,bhnkd->bhgnqd', e, vw.astype(jnp.float32)) / denom
    lse = (jnp.log(denom) + m)[..., 0]
    o = o.reshape(b_, hk, g, lp, dh)[:, :, :, :L].astype(k.dtype)
    lse = lse.reshape(b_, hk, g, lp)[..., :L]
    return o, lse

def windowed_gqa_sink(qa, ka, va, bias_table, sink):
    b_, s_, _ = qa.shape
    q = qa.reshape(b_, s_, N_KV_A, GROUP_A, HEAD_DIM).transpose(0, 2, 3, 1, 4)
    k = ka.reshape(b_, s_, N_KV_A, HEAD_DIM).transpose(0, 2, 1, 3)
    v = va.reshape(b_, s_, N_KV_A, HEAD_DIM).transpose(0, 2, 1, 3)
    bias = bias_table[t5_bucket(band_rel(WINDOW_A))][..., :N_HEADS_A]
    bias = bias.transpose(2, 0, 1).reshape(N_KV_A, GROUP_A, WINDOW_A, 3 * WINDOW_A)
    o, _ = banded_attention(q, k, v, bias.astype(jnp.float32), WINDOW_A, WINDOW_A,
                            sink.reshape(N_KV_A, GROUP_A))
    return o.transpose(0, 3, 1, 2, 4).reshape(b_, s_, WIDTH_A)

def dilated_mixture(qb_, kb_, vb_, bias_table):
    b_, s_, _ = qb_.shape
    to_heads = lambda t: t.reshape(b_, s_, N_HEADS_B, HEAD_DIM).transpose(0, 2, 1, 3)
    q, k, v = to_heads(qb_), to_heads(kb_), to_heads(vb_)
    outs, lses = [], []
    for window, dil in DILATED_PATTERNS:
        half = window // (2 * dil)
        ls = s_ // dil
        sub = lambda t: t.reshape(b_, N_HEADS_B, ls, dil, HEAD_DIM).transpose(0, 1, 3, 2, 4) \
                         .reshape(b_, N_HEADS_B * dil, ls, HEAD_DIM)
        bias = bias_table[t5_bucket(band_rel(half) * dil)][..., N_HEADS_A:]
        bias = jnp.repeat(bias.transpose(2, 0, 1), dil, axis=0)[:, None]
        o, lse = banded_attention(sub(q)[:, :, None], sub(k), sub(v),
                                  bias.astype(jnp.float32), half, half, None)
        o = o.reshape(b_, N_HEADS_B, dil, ls, HEAD_DIM).transpose(0, 1, 3, 2, 4) \
             .reshape(b_, N_HEADS_B, s_, HEAD_DIM)
        lse = lse.reshape(b_, N_HEADS_B, dil, ls).transpose(0, 1, 3, 2).reshape(b_, N_HEADS_B, s_)
        outs.append(o)
        lses.append(lse)
    w = jax.nn.softmax(jnp.stack(lses, axis=0), axis=0)
    o = jnp.sum(w[..., None] * jnp.stack(outs, axis=0).astype(jnp.float32), axis=0).astype(q.dtype)
    return o.transpose(0, 2, 1, 3).reshape(b_, s_, WIDTH_B)

def first_inputs(seed: int = 0) -> dict:
    key = jax.random.key(seed)
    ks = jax.random.split(key, 20)
    nrm = lambda k, shape, scale: (jax.random.normal(k, shape, jnp.float32) * scale)
    gain = lambda k, n: 1.0 + nrm(k, (DEPTH, n), 0.02)
    return {
        "x": nrm(ks[0], (BATCH, SEQ, D_MODEL), 1.0),
        "p": nrm(ks[1], (DEPTH, BATCH, SEQ, PLE_DIM), 1.0),
        "rel_bias_table": nrm(ks[2], (NUM_BUCKETS, N_BIAS_HEADS), 0.5),
        "g_pre_mix": gain(ks[3], D_MODEL),
        "w_in": nrm(ks[4], (DEPTH, D_MODEL, D_IN_PROJ), D_MODEL ** -0.5),
        "sink_a": nrm(ks[5], (DEPTH, N_HEADS_A), 0.5),
        "g_out_a": gain(ks[6], WIDTH_A),
        "g_out_b": gain(ks[7], WIDTH_B),
        "w_o": nrm(ks[8], (DEPTH, D_MIX, D_MODEL), D_MIX ** -0.5),
        "g_post_mix": gain(ks[9], D_MODEL),
        "g_pre_mlp": gain(ks[10], D_MODEL),
        "w_up": nrm(ks[11], (DEPTH, D_MODEL, D_FF), D_MODEL ** -0.5),
        "w_down": nrm(ks[12], (DEPTH, D_FF, D_MODEL), D_FF ** -0.5),
        "g_post_mlp": gain(ks[13], D_MODEL),
        "w_ple_proj": nrm(ks[14], (DEPTH, PLE_DIM, D_MODEL), PLE_DIM ** -0.5),
        "w_ple_gate": nrm(ks[15], (DEPTH, D_MODEL, D_MODEL), D_MODEL ** -0.5),
        "b_ple_gate": nrm(ks[16], (DEPTH, D_MODEL), 0.02),
        "g_post_ple": gain(ks[17], D_MODEL),
    }

def first_block(x, p, rel_bias_table, g_pre_mix, w_in, sink_a, g_out_a, g_out_b, w_o,
              g_post_mix, g_pre_mlp, w_up, w_down, g_post_mlp, w_ple_proj, w_ple_gate,
              b_ple_gate, g_post_ple):
    h = x
    offs = np.cumsum([0, WIDTH_A, KV_WIDTH_A, KV_WIDTH_A, WIDTH_B, WIDTH_B, WIDTH_B])
    for i in range(DEPTH):
        u = rmsnorm(h, g_pre_mix[i])
        proj = jnp.einsum('bsd,de->bse', u, w_in[i])
        qa, ka, va, qb, kb, vb = [proj[..., offs[j]:offs[j + 1]] for j in range(6)]
        o_a = rmsnorm(windowed_gqa_sink(qa, ka, va, rel_bias_table, sink_a[i]), g_out_a[i])
        o_b = rmsnorm(dilated_mixture(qb, kb, vb, rel_bias_table), g_out_b[i])
        mix = jnp.einsum('bse,ed->bsd', jnp.concatenate([o_a, o_b], axis=-1), w_o[i])
        h = h + rmsnorm(mix, g_post_mix[i])
        v_ = rmsnorm(h, g_pre_mlp[i])
        a = jax.nn.relu(jnp.einsum('bsd,df->bsf', v_, w_up[i]))
        ff = jnp.einsum('bsf,fd->bsd', a * a, w_down[i])
        h = h + rmsnorm(ff, g_post_mlp[i])
        gate = jax.nn.sigmoid(jnp.einsum('bsd,de->bse', h, w_ple_gate[i]) + b_ple_gate[i])
        ple = jnp.einsum('bsk,kd->bsd', p[i], w_ple_proj[i])
        h = h + rmsnorm(gate * ple, g_post_ple[i])
    return h


DEPTH_2 = 2

N_META = 16
GATE_CLAMP = 1.0 - 1e-6
CONV_DIM = D_MODEL // 2
CONV_K = 31
MLA_HEADS = D_MODEL // 128
Q_RANK = D_MODEL // 4
KV_RANK = D_MODEL // 8
NOPE_DIM = 64
ROPE_DIM = 32
V_DIM = 64
QK_DIM = NOPE_DIM + ROPE_DIM
ROPE_BASE = 10000.0
Q_BLOCK = 128
HGRN_HEADS = D_MODEL // 256
HGRN_DK = 128
HGRN_DV = (D_MODEL // 2) // HGRN_HEADS
HGRN_CHUNK = 64
D_FF_2 = 4 * D_MODEL
N_BRANCH = 3

SPLIT_SIZES = (
    2 * CONV_DIM,
    Q_RANK,
    KV_RANK,
    ROPE_DIM,
    HGRN_HEADS * HGRN_DK,
    HGRN_HEADS * HGRN_DK,
    HGRN_HEADS * HGRN_DV,
    HGRN_HEADS * HGRN_DV,
    N_BRANCH * D_MODEL,
)
SPLIT_POINTS = tuple(int(s) for s in np.cumsum(SPLIT_SIZES)[:-1])
N_IN = int(sum(SPLIT_SIZES))


def rms_norm(x, g):
    xf = x.astype(jnp.float32)
    y = xf * lax.rsqrt(jnp.mean(xf * xf, axis=-1, keepdims=True) + EPS)
    return (y * g.astype(jnp.float32)).astype(x.dtype)

def layer_norm(x, g, b):
    xf = x.astype(jnp.float32)
    mu = jnp.mean(xf, axis=-1, keepdims=True)
    xc = xf - mu
    y = xc * lax.rsqrt(jnp.mean(xc * xc, axis=-1, keepdims=True) + EPS)
    return (y * g.astype(jnp.float32) + b.astype(jnp.float32)).astype(x.dtype)

def apply_rope(x, cos, sin):
    half = ROPE_DIM // 2
    xf = x.astype(jnp.float32)
    x1, x2 = xf[..., :half], xf[..., half:]
    out = jnp.concatenate([x1 * cos - x2 * sin, x1 * sin + x2 * cos], axis=-1)
    return out.astype(x.dtype)

def conv_module(u, conv_w, conv_b, ln_g, ln_b, w_proj):
    a, gt = jnp.split(u, 2, axis=-1)
    h = a * jax.nn.sigmoid(gt)
    h = lax.conv_general_dilated(
        h, conv_w[:, None, :].astype(h.dtype), window_strides=(1,), padding=[(CONV_K - 1, 0)],
        dimension_numbers=('NWC', 'WIO', 'NWC'), feature_group_count=CONV_DIM) + conv_b
    h = jax.nn.silu(layer_norm(h, ln_g, ln_b))
    return h @ w_proj

def causal_block_attention(q, k, v):
    B, L, H, Dq = q.shape
    n_blk = -(-L // Q_BLOCK)
    Lp = n_blk * Q_BLOCK
    qp = jnp.pad(q, ((0, 0), (0, Lp - L), (0, 0), (0, 0)))
    qb = qp.reshape(B, n_blk, Q_BLOCK, H, Dq).transpose(1, 0, 2, 3, 4)
    starts = jnp.arange(n_blk, dtype=jnp.int32) * Q_BLOCK
    k_pos = jnp.arange(L, dtype=jnp.int32)
    scale = Dq ** -0.5

    def one_block(args):
        q_blk, start = args
        s = jnp.einsum('bqhd,bkhd->bhqk', q_blk, k).astype(jnp.float32) * scale
        q_pos = start + jnp.arange(Q_BLOCK, dtype=jnp.int32)
        mask = k_pos[None, :] <= q_pos[:, None]
        s = jnp.where(mask, s, -1e30)
        p = jax.nn.softmax(s, axis=-1).astype(v.dtype)
        return jnp.einsum('bhqk,bkhd->bqhd', p, v)

    ob = lax.map(one_block, (qb, starts))
    return ob.transpose(1, 0, 2, 3, 4).reshape(B, Lp, H, V_DIM)[:, :L]

def mla(c_q, c_kv, k_rope, cos, sin, q_a_g, w_uq, kv_a_g, w_ukv, q_norm_g, k_norm_g, w_proj):
    B, L = c_q.shape[:2]
    q = (rms_norm(c_q, q_a_g) @ w_uq).reshape(B, L, MLA_HEADS, QK_DIM)
    kv = (rms_norm(c_kv, kv_a_g) @ w_ukv).reshape(B, L, MLA_HEADS, NOPE_DIM + V_DIM)
    k_nope, v = kv[..., :NOPE_DIM], kv[..., NOPE_DIM:]
    k_r = jnp.broadcast_to(k_rope[:, :, None, :], (B, L, MLA_HEADS, ROPE_DIM))
    k = jnp.concatenate([k_nope, k_r], axis=-1)
    q = rms_norm(q, q_norm_g)
    k = rms_norm(k, k_norm_g)
    q = jnp.concatenate([q[..., :NOPE_DIM], apply_rope(q[..., NOPE_DIM:], cos, sin)], axis=-1)
    k = jnp.concatenate([k[..., :NOPE_DIM], apply_rope(k[..., NOPE_DIM:], cos, sin)], axis=-1)
    o = causal_block_attention(q, k, v)
    return o.reshape(B, L, MLA_HEADS * V_DIM) @ w_proj

def hgrn2(q, f_raw, i, g, lb, norm_g, w_proj):
    B, L = q.shape[:2]
    f32 = jnp.float32
    lbf = lb.astype(f32)
    fr = f_raw.astype(f32)
    k = (1.0 - lbf) * jax.nn.sigmoid(-fr)
    log_f = jnp.log1p(-jnp.minimum(k, GATE_CLAMP))
    v = jax.nn.silu(i.astype(f32))
    qf = q.astype(f32)
    pad_front = (-N_META) % HGRN_CHUNK
    pad_back = (-(pad_front + L)) % HGRN_CHUNK
    pads = ((0, 0), (pad_front, pad_back), (0, 0))
    qf, k, v, log_f = [jnp.pad(a, pads) for a in (qf, k, v, log_f)]
    Lp = L + pad_front + pad_back
    nc = Lp // HGRN_CHUNK

    def to_chunks(a, d):
        return a.reshape(B, nc, HGRN_CHUNK, HGRN_HEADS, d).transpose(1, 0, 3, 2, 4)

    qc, kc, lfc = to_chunks(qf, HGRN_DK), to_chunks(k, HGRN_DK), to_chunks(log_f, HGRN_DK)
    vc = to_chunks(v, HGRN_DV)
    causal = jnp.tril(jnp.ones((HGRN_CHUNK, HGRN_CHUNK), dtype=bool))[:, :, None]

    def chunk_step(S, inp):
        q_c, k_c, v_c, lf_c = inp
        b = jnp.cumsum(lf_c, axis=2)
        o_inter = jnp.einsum('bhtk,bhkv->bhtv', q_c * jnp.exp(b), S)
        diff = b[:, :, :, None, :] - b[:, :, None, :, :]
        decay = jnp.where(causal, jnp.exp(jnp.where(causal, diff, 0.0)), 0.0)
        A = jnp.einsum('bhtk,bhtsk,bhsk->bhts', q_c, decay, k_c)
        o_intra = jnp.einsum('bhts,bhsv->bhtv', A, v_c)
        b_last = b[:, :, -1:, :]
        S_new = jnp.exp(b_last[:, :, 0, :])[..., None] * S + jnp.einsum(
            'bhsk,bhsv->bhkv', k_c * jnp.exp(b_last - b), v_c)
        return S_new, o_inter + o_intra

    S0 = jnp.zeros((B, HGRN_HEADS, HGRN_DK, HGRN_DV), f32)
    _, oc = lax.scan(chunk_step, S0, (qc, kc, vc, lfc))
    o = oc.transpose(1, 0, 3, 2, 4).reshape(B, Lp, HGRN_HEADS, HGRN_DV)[:, pad_front:pad_front + L]
    o = o * lax.rsqrt(jnp.mean(o * o, axis=-1, keepdims=True) + EPS)
    o = o.reshape(B, L, HGRN_HEADS * HGRN_DV) * norm_g.astype(f32)
    o = (o * jax.nn.silu(g.astype(f32))).astype(q.dtype)
    return o @ w_proj

def second_inputs(seed: int = 0) -> dict:
    key = jax.random.key(seed)
    ks = iter(jax.random.split(key, 32))

    def nrm(shape, scale):
        return jax.random.normal(next(ks), shape, jnp.float32) * scale

    def gain(shape):
        return 1.0 + 0.1 * nrm(shape, 1.0)

    D = D_MODEL
    return {
        'x': nrm((BATCH, SEQ, D), 1.0),
        'meta': nrm((N_META, D), 1.0),
        'norm1_g': gain((DEPTH_2, D)),
        'w_in': nrm((DEPTH_2, D, N_IN), D ** -0.5),
        'conv_w': nrm((DEPTH_2, CONV_K, CONV_DIM), CONV_K ** -0.5),
        'conv_b': nrm((DEPTH_2, CONV_DIM), 0.02),
        'conv_ln_g': gain((DEPTH_2, CONV_DIM)),
        'conv_ln_b': nrm((DEPTH_2, CONV_DIM), 0.02),
        'w_conv_out': nrm((DEPTH_2, CONV_DIM, D), CONV_DIM ** -0.5),
        'q_a_norm_g': gain((DEPTH_2, Q_RANK)),
        'w_uq': nrm((DEPTH_2, Q_RANK, MLA_HEADS * QK_DIM), Q_RANK ** -0.5),
        'kv_a_norm_g': gain((DEPTH_2, KV_RANK)),
        'w_ukv': nrm((DEPTH_2, KV_RANK, MLA_HEADS * (NOPE_DIM + V_DIM)), KV_RANK ** -0.5),
        'q_norm_g': gain((DEPTH_2, QK_DIM)),
        'k_norm_g': gain((DEPTH_2, QK_DIM)),
        'w_attn_out': nrm((DEPTH_2, MLA_HEADS * V_DIM, D), (MLA_HEADS * V_DIM) ** -0.5),
        'hgrn_lb_logits': nrm((DEPTH_2, HGRN_HEADS * HGRN_DK), 1.0),
        'hgrn_norm_g': gain((DEPTH_2, HGRN_HEADS * HGRN_DV)),
        'w_hgrn_out': nrm((DEPTH_2, HGRN_HEADS * HGRN_DV, D), (HGRN_HEADS * HGRN_DV) ** -0.5),
        'w_out': nrm((DEPTH_2, D, D), D ** -0.5),
        'norm2_g': gain((DEPTH_2, D)),
        'w_ff1': nrm((DEPTH_2, D, D_FF_2), D ** -0.5),
        'w_ff2': nrm((DEPTH_2, D_FF_2, D), D_FF_2 ** -0.5),
    }

def second_block(x, meta, norm1_g, w_in, conv_w, conv_b, conv_ln_g, conv_ln_b, w_conv_out,
              q_a_norm_g, w_uq, kv_a_norm_g, w_ukv, q_norm_g, k_norm_g, w_attn_out,
              hgrn_lb_logits, hgrn_norm_g, w_hgrn_out, w_out, norm2_g, w_ff1, w_ff2):
    B = x.shape[0]
    D = D_MODEL
    x = jnp.concatenate([jnp.broadcast_to(meta[None].astype(x.dtype), (B, N_META, D)), x], axis=1)
    L = x.shape[1]
    half = ROPE_DIM // 2
    pos = jnp.arange(L, dtype=jnp.float32)
    inv_freq = ROPE_BASE ** (-jnp.arange(half, dtype=jnp.float32) / half)
    ang = pos[:, None] * inv_freq[None, :]
    cos = jnp.cos(ang)[None, :, None, :]
    sin = jnp.sin(ang)[None, :, None, :]
    p_lb = jax.nn.softmax(hgrn_lb_logits.astype(jnp.float32), axis=0)
    lower_bounds = jnp.cumsum(p_lb, axis=0) - p_lb[0:1]

    for l in range(DEPTH_2):
        h = rms_norm(x, norm1_g[l])
        u = h @ w_in[l]
        (u_conv, c_q, c_kv, k_rope, hq, hf, hi, hg, u_gate) = jnp.split(u, SPLIT_POINTS, axis=-1)
        y_a = conv_module(u_conv, conv_w[l], conv_b[l], conv_ln_g[l], conv_ln_b[l], w_conv_out[l])
        y_b = mla(c_q, c_kv, k_rope, cos, sin, q_a_norm_g[l], w_uq[l], kv_a_norm_g[l], w_ukv[l],
                  q_norm_g[l], k_norm_g[l], w_attn_out[l])
        y_c = hgrn2(hq, hf, hi, hg, lower_bounds[l], hgrn_norm_g[l], w_hgrn_out[l])
        gates = jax.nn.sigmoid(u_gate).reshape(B, L, N_BRANCH, D)
        mix = gates[:, :, 0] * y_a + gates[:, :, 1] * y_b + gates[:, :, 2] * y_c
        x = x + mix @ w_out[l]
        h2 = rms_norm(x, norm2_g[l])
        x = x + jnp.square(jax.nn.relu(h2 @ w_ff1[l])) @ w_ff2[l]

    return x[:, N_META:]


def setup_inputs(seed=0):
    out = dict(first_inputs(seed))
    for name, value in second_inputs(seed + 1).items():
        if name != "x":
            out[name + "_2"] = value
    return out


def reference(
    x, p, rel_bias_table, g_pre_mix, w_in, sink_a, g_out_a, g_out_b, w_o, g_post_mix, g_pre_mlp,
    w_up, w_down, g_post_mlp, w_ple_proj, w_ple_gate, b_ple_gate, g_post_ple, meta_2, norm1_g_2,
    w_in_2, conv_w_2, conv_b_2, conv_ln_g_2, conv_ln_b_2, w_conv_out_2, q_a_norm_g_2, w_uq_2,
    kv_a_norm_g_2, w_ukv_2, q_norm_g_2, k_norm_g_2, w_attn_out_2, hgrn_lb_logits_2,
    hgrn_norm_g_2, w_hgrn_out_2, w_out_2, norm2_g_2, w_ff1_2, w_ff2_2,
):
    x = first_block(
        x, p, rel_bias_table, g_pre_mix, w_in, sink_a, g_out_a, g_out_b, w_o, g_post_mix,
        g_pre_mlp, w_up, w_down, g_post_mlp, w_ple_proj, w_ple_gate, b_ple_gate, g_post_ple,
    )
    return second_block(
        x, meta_2, norm1_g_2, w_in_2, conv_w_2, conv_b_2, conv_ln_g_2, conv_ln_b_2,
        w_conv_out_2, q_a_norm_g_2, w_uq_2, kv_a_norm_g_2, w_ukv_2, q_norm_g_2, k_norm_g_2,
        w_attn_out_2, hgrn_lb_logits_2, hgrn_norm_g_2, w_hgrn_out_2, w_out_2, norm2_g_2,
        w_ff1_2, w_ff2_2,
    )


_drawn_inputs = setup_inputs


def setup_inputs(seed=0):
    import zlib

    import numpy as np

    out = dict(_drawn_inputs(seed))
    spreads = {}
    factors = {'sink_a': 8.0,
     'g_out_a': 4.893,
     'g_out_b': 5.034,
     'g_post_mix': 3.495,
     'g_pre_mlp': 4.073,
     'g_post_mlp': 4.344,
     'b_ple_gate': 8.0,
     'g_post_ple': 4.83,
     'conv_b_2': 6.826,
     'conv_ln_b_2': 21.618,
     'q_a_norm_g_2': 8.0,
     'kv_a_norm_g_2': 3.826,
     'q_norm_g_2': 8.0,
     'k_norm_g_2': 8.0,
     'conv_ln_g_2': 3.756,
     'hgrn_lb_logits_2': 3.297,
     'hgrn_norm_g_2': 3.998}
    for name, (base, spread) in spreads.items():
        noise = np.random.default_rng([zlib.crc32(name.encode()), seed]).standard_normal(out[name].shape)
        drawn = base * np.exp(spread * noise) if base else spread * noise
        out[name] = jnp.asarray(drawn.astype(out[name].dtype))
    for name, factor in factors.items():
        out[name] = (out[name] * factor).astype(out[name].dtype)
    return out
```

```python
from contextlib import ExitStack, contextmanager

import numpy as np
import concourse.bass as bass
from concourse import mybir

F32 = mybir.dt.float32
U8 = mybir.dt.uint8
ACT = mybir.ActivationFunctionType
ALU = mybir.AluOpType
AX = mybir.AxisListType.X

P = 128
D = 1024
KD = D // P
S = 512
META = 16
T = S + META
EPS = 1e-6
NEG = -1e30
CH = 8 * P
RING = 4

DH = 64
WIN = 128
DILATED = ((128, 1), (512, 4), (2048, 16))
QB = S // P
REL = 1024
BW = 896
FF_GROUPS = 4

V1 = {}
_at = 0
for _name, _n in (("g_pre_mix", 8), ("g_out", 8), ("g_post_mix", 8), ("g_pre_mlp", 8), ("g_post_mlp", 8),
                  ("b_gate", 8), ("g_post_ple", 8)):
    V1[_name] = _at
    _at += _n
V1_COLS = _at

ATT_CHUNKS = 4
N1_CHUNKS = 2 + 4 * ATT_CHUNKS + KD + 16 * FF_GROUPS + KD + 2


LAYERS = 2
TAPS = 31
CONV_TILES = 4
HEADS_G = 4
GCH = 128
CHUNKS_G = S // GCH
CLAMP = 1.0 - 1e-6
LEVELS = 7
QK = 96
NOPE = 64
ROPE = 32
QT = 5
V2 = {}
_at = 0
for _name, _n in (("norm1", 8), ("conv_w", TAPS * CONV_TILES), ("conv_b", 4), ("ln_g", 4), ("ln_b", 4), ("q_a", 2),
                  ("kv_a", 1), ("q_norm", 1), ("k_norm", 1), ("lb0", 4), ("lb1", 4), ("second", 1), ("hgrn_g", 4),
                  ("norm2", 8)):
    V2[_name] = _at
    _at += _n
V2_COLS = _at
N2_CHUNKS = 8 + 24 + 4 + 16 + 16 + 8 + 16 * FF_GROUPS


LOOPS = {
    "conv": {"chunk_full0": 16, "chunk_full1": 16, "chunk_full2": 16, "chunk_full3": 16, "sig_ready": 2,
        "unit_done0": 2, "unit_done1": 2, "unit_free0": 2, "unit_free1": 2},
    "gates": {"chunk_full0": 16, "chunk_full1": 16, "chunk_full2": 16, "chunk_full3": 16, "unit_done0": 2,
        "unit_done1": 2, "unit_free0": 2, "unit_free1": 2},
    "recurrence": {"a_ready": 1, "chunk_full0": 16, "chunk_full1": 16, "chunk_full2": 16, "chunk_full3": 16,
        "f_sig": 1, "go_copied": 1, "go_done": 1, "gss_done": 1, "kft_done": 1, "kft_ready": 1, "level_ready": 7,
        "pair_done0": 4, "pair_done1": 4, "pair_free0": 4, "pair_free1": 4, "q_ready": 1, "rms_ready": 1,
        "sig_ready": 2, "state_ready": 1, "unit_done0": 2, "unit_done1": 2, "unit_free0": 2, "unit_free1": 2,
        "upd_done": 1, "v_ready": 1, "vtok_ready": 1, "vtr_done": 1},
    "mla": {"cT_ready0": 5, "cT_ready1": 5, "causal_done0": 6, "causal_done1": 6, "causal_free0": 6,
        "causal_free1": 6, "co_done": 2, "co_free": 2, "ctr_done0": 5, "ctr_done1": 5, "mlaw_in": 16, "mlaw_used": 1,
        "qexp_ready": 2, "qk_free": 2, "qk_raw": 4, "qk_ready": 2, "qmax_ready": 2, "rms_ready": 4, "unit_done0": 6,
        "unit_done1": 6, "unit_free0": 6, "unit_free1": 6, "vt_done": 1, "vt_ready": 1},
    "mix": {"chunk_full0": 16, "chunk_full1": 16, "chunk_full2": 16, "chunk_full3": 16, "unit_done0": 3,
        "unit_done1": 3, "unit_free0": 3, "unit_free1": 3},
    "ff2": {"chunk_full0": 64, "chunk_full1": 64, "chunk_full2": 64, "chunk_full3": 64, "hid_ready": 8,
        "unit_done0": 8, "unit_done1": 8, "unit_free0": 8, "unit_free1": 8},
    "layer": {"a_ready": 4, "cT_ready0": 22, "cT_ready1": 22, "c_ready": 1, "causal_done0": 24, "causal_done1": 24,
        "causal_free0": 24, "causal_free1": 24, "centred": 1, "chunk_full0": 560, "chunk_full1": 560,
        "chunk_full2": 560, "chunk_full3": 560, "co_done": 8, "co_free": 8, "conv_ready": 4, "ctr_done0": 22,
        "ctr_done1": 22, "f_sig": 4, "go_copied": 4, "go_done": 4, "gss_done": 4, "h_ready": 8, "hc_padded": 1,
        "hid_ready": 32, "kft_done": 4, "kft_ready": 4, "layer_begun": 1, "lb_exp_ready": 1, "lb_max_ready": 1,
        "level_ready": 28, "ln_ready": 1, "lnsig_ready": 1, "m_done": 1, "mean_ready": 1, "mlaw_in": 64,
        "mlaw_used": 5, "pair_done0": 16, "pair_done1": 16, "pair_free0": 16, "pair_free1": 16, "q_ready": 4,
        "qexp_ready": 8, "qk_free": 8, "qk_raw": 16, "qk_ready": 8, "qmax_ready": 8, "rms_ready": 25,
        "sig_ready": 12, "sq_ready": 23, "state_ready": 4, "u_ready": 16, "unit_done0": 101, "unit_done1": 101,
        "unit_free0": 101, "unit_free1": 101, "upd_done": 4, "v_ready": 4, "vt_done": 4, "vt_ready": 4,
        "vtok_ready": 4, "vtr_done": 4, "zb_ready": 1, "zc_ready": 1, "ztail_done": 1},
}


class Counts:

    def __init__(self, eng):
        self.eng, self.seen, self.loops = eng, {}, []

    def next(self, sem, by=1):
        self.seen[sem.name] = self.seen.get(sem.name, 0) + by
        return self.now(sem)

    def now(self, sem):
        value = self.seen.get(sem.name, 0)
        for reg, per in self.loops:
            if per.get(sem.name, 0):
                value = reg * per[sem.name] + value
        return value

    @contextmanager
    def loop(self, count, per):
        before = dict(self.seen)
        with self.eng.Fori(0, count) as reg:
            self.loops.append((reg, per))
            yield reg
            self.loops.pop()
        for name, value in self.seen.items():
            once, begun = value - before.get(name, 0), before.get(name, 0)
            assert once in (0, per.get(name, 0)), f"{name}: {once} an iteration, not {per.get(name, 0)}"
            self.seen[name] = begun + count * per.get(name, 0)


class Tokens:

    def __init__(self, start, count, parts):
        self.start, self.count, self.parts, self.width = start, count, parts, count // parts

    def of(self, x):
        return x[:, self.start:self.start + self.count].rearrange("p (h n) -> p h n", h=self.parts)

    def part(self, x, h):
        return x[:, self.start + h * self.width:self.start + (h + 1) * self.width]


def program(nc, xT, pT, metaT, w, w_mla, vec1, vec2, table, onehot, addmask, sink, cosines, sines, turn, causal, pairs, out):
    ctx = ExitStack()
    with ctx:
        def sb(name, shape, dt=F32):
            return ctx.enter_context(nc.sbuf_tensor(name, shape, dt))

        def sem(name):
            return ctx.enter_context(nc.semaphore(name))

        ps = ctx.enter_context(nc.psum_tensor("ps", [P, 8, 512], F32))
        H = sb("H", [P, KD, T])
        U = sb("U", [P, KD, T])
        M = sb("M", [P, KD, T])
        HID = sb("HID", [P, KD, T])
        ring = sb("ring", [P, RING, CH])
        rms = sb("rms", [P, 2, T])
        rstd = sb("rstd", [P, T])
        relu = sb("relu", [P, 2, T])
        ones = sb("ones", [P, P])
        ident = sb("ident", [P, P])
        v1 = sb("v1", [P, V1_COLS])
        v2all = sb("v2all", [P, LAYERS, V2_COLS])
        v2 = sb("v2", [P, V2_COLS])
        small = sb("small", [P, 192])
        smalls = [0]

        def few(*shape):
            size = int(np.prod(shape))
            view = small[:, smalls[0]:smalls[0] + size]
            smalls[0] += size
            assert smalls[0] <= 192
            return view if len(shape) == 1 else view.rearrange("p (a b) -> p a b", b=shape[1])

        ARENA = 27400
        arena = sb("arena", [P, ARENA])
        taken = [0]

        def carve(*shape, rows=P):
            size = int(np.prod(shape))
            view = arena[0:rows, taken[0]:taken[0] + size]
            taken[0] += size
            assert taken[0] <= ARENA, taken[0]
            return view if len(shape) == 1 else view.rearrange("p (a b) -> p a b", b=shape[1])

        pt = carve(2, S)
        ka = carve(S)
        vaT = carve(S)
        va = carve(QB, P)
        qa = carve(S)
        qb = carve(S)
        kb = carve(S)
        vbT = carve(S)
        vb = carve(QB, P)
        bw = carve(4, BW)
        ss = carve(2 * QB, S).rearrange("p (i b) s -> p i b s", i=2)
        eT = carve(2, 512)
        otok = carve(QB, D)
        tab = carve(16, rows=32)
        oneh = carve(REL, rows=32)
        addm = carve(REL, rows=16)
        brow = carve(REL, rows=16)
        nmax = few(2, 4)
        nms = few(2, 4)
        srel = few(2, 4)
        esink = few(2, 4)
        den = few(2, 4)
        den2 = few(2, 4)
        rinv = few(2, 4)
        sinks = few(8)
        nsinks = few(8)
        ss8 = few(8)
        rms8 = few(8)
        r8 = few(8)

        taken[0] = 0
        gates = carve(24, T)
        za = carve(4, T)
        zb = carve(4, T)
        zc = carve(4, T)
        hc = carve(CONV_TILES, TAPS - 1 + T)
        mlaw = arena[:, taken[0] - 1024:taken[0]]
        amat = carve(CHUNKS_G, GCH)
        atail = carve(META, rows=META)
        cq = carve(2, T)
        ckv = carve(T)
        kraw = carve(T)
        cosT = carve(T, rows=QK)
        sinT = carve(T, rows=QK)
        triT = carve(640)
        shared = taken[0]
        vtok = carve(CHUNKS_G + 1, GCH)
        kft = carve(CHUNKS_G, GCH)
        state = carve(CHUNKS_G + 1, GCH)
        taken[0] = shared
        vt = carve(QT, P)
        eT2 = carve(2, 512)
        pairf = U[:, :, :].rearrange("p k t -> p (k t)")[:, 0:(LEVELS + 1) * GCH]
        rotm = sb("rotm", [QK, QK])
        pairm = sb("pairm", [P, (LEVELS + 1) * GCH], U8)
        Ms = [M[:, k, :] for k in range(KD)]
        Hs = [HID[:, k, :] for k in range(KD)]
        Us = [U[:, k, :] for k in range(KD)]
        kk, pre, suf, qg_, vT, gs, oT, qfull = Ms
        kfull = Hs[0]
        lq = [Hs[1], Hs[2]]
        lk = [Hs[3], Hs[4]]
        gsq = Hs[7]
        qgain, kgain, rot1 = [u[0:QK] for u in Us[0:3]]
        qh_of, kh_of = [[u[0:QK] for u in Us[i:i + 2]] for i in (3, 5)]
        tails = Ms[5:7]

        def exps_of(hd, i):
            return Hs[4 * hd + i] if i < QT - 1 else tails[hd][0:META]

        TRB = (7, 3)
        qsq, ksq = relu[0:QK, 0, :], relu[0:QK, 1, :]
        otok2 = M[:, :, :].rearrange("p k t -> p (k t)")[:, 0:QT * 512].rearrange("p (i c) -> p i c", i=QT)
        lb_max, lb_sum, oml = (few(4) for _ in range(3))
        lb_e = few(2, 4)
        rms_v, mu = Hs[7], relu[:, 1, :]
        qmax, qden, qinv = (few(2, QT) for _ in range(3))
        headcol = few(2)
        bias_dram = nc.dram_tensor("bias_rows", (16, REL), F32, kind="Internal").ap()
        bias_slide = bass.AP(tensor=bias_dram.tensor, offset=0, ap=[[REL, 16], [1, P], [1, BW]])

        full = [sem(f"chunk_full{j}") for j in range(RING)]
        chunks_started = sem("chunks_started")
        vec_in = sem("vec_in")
        x_in = sem("x_in")
        bias_in = sem("bias_in")
        brow_ready = sem("brow_ready")
        brow_out = sem("brow_out")
        bw_in = sem("bw_in")
        bw_used = sem("bw_used")
        consts = sem("consts")
        unit_done = [sem(f"unit_done{b}") for b in range(2)]
        unit_free = [sem(f"unit_free{b}") for b in range(2)]
        sq_ready = sem("sq_ready")
        rms_ready = sem("rms_ready")
        u_ready = sem("u_ready")
        h_ready = sem("h_ready")
        m_ready = sem("m_ready")
        m_zero = sem("m_zero")
        hid_ready = sem("hid_ready")
        gate_ready = sem("gate_ready")
        qkv_ready = sem("qkv_ready")
        s_done = [sem(f"scores_done{b}") for b in range(3)]
        s_free = [sem(f"scores_free{b}") for b in range(3)]
        tr_done = [sem(f"tr_done{b}") for b in range(2)]
        eT_ready = [sem(f"eT_ready{b}") for b in range(2)]
        max_ready = sem("max_ready")
        exp_ready = sem("exp_ready")
        o_done = sem("o_done")
        o_free = sem("o_free")
        r8_ready = sem("r8_ready")
        osq_ready = sem("osq_ready")
        on_ready = sem("on_ready")
        oT_ready = [sem(f"oT_ready{b}") for b in range(2)]
        out_done = sem("out_done")
        consts2_in = sem("consts2_in")
        layer_begun = sem("layer_begun")
        hc_padded = sem("hc_padded")
        lb_max_ready = sem("lb_max_ready")
        lb_exp_ready = sem("lb_exp_ready")
        sig_ready = sem("sig_ready")
        conv_ready = sem("conv_ready")
        mean_ready = sem("mean_ready")
        centred = sem("centred")
        ln_ready = sem("ln_ready")
        lnsig_ready = sem("lnsig_ready")
        c_ready = sem("c_ready")
        f_sig = sem("f_sig")
        q_ready = sem("q_ready")
        v_ready = sem("v_ready")
        vtok_ready = sem("vtok_ready")
        level_ready = sem("level_ready")
        pair_done = [sem(f"pair_done{b}") for b in range(2)]
        pair_free = [sem(f"pair_free{b}") for b in range(2)]
        a_ready = sem("a_ready")
        kft_done = sem("kft_done")
        kft_ready = sem("kft_ready")
        upd_done = sem("upd_done")
        state_ready = sem("state_ready")
        go_done = sem("go_done")
        go_copied = sem("go_copied")
        gss_done = sem("gss_done")
        vtr_done = sem("vtr_done")
        zc_ready = sem("zc_ready")
        mlaw_in = sem("mlaw_in")
        mlaw_used = sem("mlaw_used")
        qk_raw = sem("qk_raw")
        qk_ready = sem("qk_ready")
        qk_free = sem("qk_free")
        vt_done = sem("vt_done")
        vt_ready = sem("vt_ready")
        c_done = [sem(f"causal_done{b}") for b in range(2)]
        c_free = [sem(f"causal_free{b}") for b in range(2)]
        qmax_ready = sem("qmax_ready")
        qexp_ready = sem("qexp_ready")
        ctr_done = [sem(f"ctr_done{b}") for b in range(2)]
        cT_ready = [sem(f"cT_ready{b}") for b in range(2)]
        co_done = sem("co_done")
        co_free = sem("co_free")
        ztail_done = sem("ztail_done")
        zb_ready = sem("zb_ready")
        m_done = sem("m_done")
        passed = sem("passed")

        T0 = Tokens(0, S, 1)
        T1 = Tokens(META, S, 1)

        def psum_of(b, tok, m=P):
            return ps[0:m, 2 * b:2 * b + tok.parts, 0:tok.width]

        ATT_PER = {"unit_done0": 2, "unit_done1": 2, "unit_free0": 2, "unit_free1": 2, "qkv_ready": 4,
                   "chunk_full0": 16, "chunk_full1": 16, "chunk_full2": 16, "chunk_full3": 16,
                   "scores_done0": 6, "scores_done1": 5, "scores_done2": 5,
                   "scores_free0": 6, "scores_free1": 5, "scores_free2": 5,
                   "tr_done0": 9, "tr_done1": 9, "eT_ready0": 9, "eT_ready1": 9, "max_ready": 4, "exp_ready": 4,
                   "o_done": 4, "o_free": 4, "bw_in": 64}
        FF_PER = {"unit_done0": 8, "unit_done1": 8, "unit_free0": 8, "unit_free1": 8, "hid_ready": 8,
                  "chunk_full0": 64, "chunk_full1": 64, "chunk_full2": 64, "chunk_full3": 64}

        T2 = Tokens(0, T, 2)
        CONV_PER, GATE_PER, GREC_PER, MLA_PER, MIX_PER, FF2_PER, LAYER_PER = (LOOPS[x] for x in (
            "conv", "gates", "recurrence", "mla", "mix", "ff2", "layer"))

        def level_blocks(x, size, half):
            cols = T if 2 * size <= META else S
            return x[:, 0:cols].rearrange("p (n two b) -> p n two b", two=2, b=size)[:, :, half, :]

        def level_total(x, size, half):
            v = level_blocks(x, size, half)
            return v[:, :, size - 1:size].to_broadcast([P, v.shape[1], size])

        HEADS = ((True, 0), (True, 1), (False, 0), (False, 1))

        def key_blocks(banded, b):
            return range(max(0, b - 1), min(QB, b + 2)) if banded else range(QB)

        def copy_causal_tile(eng, n, i):
            tb = 0 if eng.engine == nc.scalar.engine else 1
            rows = P if i < QT - 1 else META
            eng.wait_ge(ctr_done[tb], n.next(ctr_done[tb]))
            whole = min(i + 1, QT - 1)
            last = None
            for keys, c0, c1 in ((P, 0, whole * rows),) + (((META, whole * rows, (whole + 1) * rows),) if i == QT - 1 else ()):
                dst, src = eT2[0:keys, tb, c0:c1], ps[0:keys, TRB[tb], c0:c1]
                last = eng.activation(dst, src, ACT.Copy) if tb == 0 else eng.tensor_copy(dst, src)
            last.then_inc(cT_ready[tb], 1)

        block = ctx.enter_context(nc.Block())

        @block.sync
        def _(sp):
            for j in range(RING):
                sp.dma_start(ring[:, j, :], w[j]).then_inc(full[j], 16)
            with sp.Fori(1, (N1_CHUNKS + LAYERS * N2_CHUNKS) // RING) as i:
                for j in range(RING):
                    sp.wait_ge(chunks_started, 4 * i + j - 2)
                    sp.dma_start(ring[:, j, :], w[bass.ds(4 * i + j, 1)].rearrange("o p n -> p (o n)")).then_inc(full[j], 16)

        @block.gpsimd
        def _(pool):
            pool.memset(ones[:, :], 1.0)
            pool.memset(ident[:, :], 0.0)
            pool.drain()
            pool.affine_select(out=ident[:, :], in_=ident[:, :], compare_op=ALU.not_equal, fill=1.0, base=0,
                               pattern=[[-1, P]], channel_multiplier=1)
            pool.drain().then_inc(consts, 1)
            n = Counts(pool)
            pool.wait_ge(brow_ready, 1)
            pool.dma_start(bias_dram, brow[:, :]).then_inc(brow_out, 16)
            pool.wait_ge(brow_out, 16)
            with n.loop(4, {"bw_used": 1}) as t:
                pool.wait_ge(bw_used, n.next(bw_used))
                for j, row in enumerate((t, t + 4, 2 * t + 8, 2 * t + 9)):
                    pool.dma_start(bw[:, j, :], bias_slide[bass.ds(row, 1)].rearrange("o p c -> p (o c)")).then_inc(bw_in, 16)
            pool.wait_ge(h_ready, KD)
            pool.memset(M[:, :, META:], 0.0).then_inc(m_zero, 1)
            pool.wait_ge(h_ready, 3 * KD)
            pool.memset(amat, 0.0)
            pool.memset(atail, 0.0)
            pool.drain().then_inc(consts, 1)
            for dst, src in ((cosT, cosines), (sinT, sines), (triT, causal), (rotm[:, :], turn), (pairf, pairs),
                             (v2all[:, :, :], vec2)):
                pool.dma_start(dst, src).then_inc(consts2_in, 16)
            n = Counts(pool)
            with n.loop(LAYERS, LAYER_PER) as layer:
                pool.wait_ge(layer_begun, n.next(layer_begun))
                pool.sem_inc(passed, 1)
                pool.memset(hc[:, :, 0:TAPS - 1], 0.0).then_inc(hc_padded, 1)
                with n.loop(4, MLA_PER) as pair:
                    pool.wait_ge(mlaw_used, n.next(mlaw_used))
                    pool.dma_start(mlaw, w_mla[bass.ds(layer * 4 + pair, 1)].rearrange("o p c -> p (o c)")).then_inc(mlaw_in, 16)
                pool.wait_ge(mlaw_used, n.next(mlaw_used))

        @block.tensor
        def _(pe):
            n = Counts(pe)
            at = {"chunk": 0, "unit": 0}

            def chunk():
                slot = at["chunk"] % RING
                at["chunk"] += 1
                pe.wait_ge(full[slot], n.next(full[slot], 16))
                return [ring[:, slot, j * P:(j + 1) * P] for j in range(8)]

            def unit(weights, acts, tok, m=P, ready=None, counts_chunk=False):
                b = at["unit"] % 2
                at["unit"] += 1
                pe.wait_ge(unit_free[b], n.next(unit_free[b]))
                for k, (wt, a) in enumerate(zip(weights, acts)):
                    if ready is not None:
                        pe.wait_ge(ready, n.next(ready))
                    for h in range(tok.parts):
                        mm = pe.matmul(ps[0:m, 2 * b + h, 0:tok.width], wt, tok.part(a, h),
                                       start=(k == 0), stop=(k == len(acts) - 1))
                        if counts_chunk and k == 0 and h == 0:
                            mm.then_inc(chunks_started, 1)
                mm.then_inc(unit_done[b], 1)

            def project(acts, tok, count, ready=None):
                for m in range(count):
                    unit(chunk(), acts, tok, ready=ready if m == 0 else None, counts_chunk=True)

            def sum_squares(tok, count=KD):
                unit([ones[:, :]] * count, [HID[:, k, :] for k in range(count)], tok, ready=sq_ready)

            Uk = [U[:, k, :] for k in range(KD)]
            Hk = [H[:, k, :] for k in range(KD)]
            HIDk = [HID[:, k, :] for k in range(KD)]
            pe.wait_ge(consts, 1)
            pe.wait_ge(bias_in, 48)
            for h in range(2):
                b = at["unit"] % 2
                at["unit"] += 1
                pe.wait_ge(unit_free[b], n.next(unit_free[b]))
                pe.matmul(ps[0:16, 2 * b, 0:512], tab[:, :], oneh[:, h * 512:(h + 1) * 512],
                          start=True, stop=True).then_inc(unit_done[b], 1)

            sum_squares(T1)
            project(Uk, T1, 1, ready=u_ready)
            project(Uk, T1, 1)
            tr = [0]

            def transposed(b, blocks):
                for j, src in enumerate(blocks):
                    mm = pe.transpose(ps[0:src.shape[-1], 1 + 2 * b, j * P:j * P + src.shape[0]], src, ident[0:src.shape[0], 0:src.shape[0]])
                mm.then_inc(tr_done[b], 1)

            def transpose_values(src):
                for b in range(2):
                    transposed(b, [src[:, (2 * b + j) * P:(2 * b + j + 1) * P] for j in range(2)])
                for b in range(2):
                    pe.wait_ge(eT_ready[b], n.next(eT_ready[b]))

            pe.wait_ge(qkv_ready, n.next(qkv_ready, 2))
            transpose_values(vaT)
            assert at["unit"] % 2 == 1

            def scores(hd):
                banded, half = HEADS[hd]
                q, k = (qa, ka) if banded else (qb, kb)
                rows = slice(64 * half, 64 * half + 64)
                for b in range(QB):
                    u = (hd * QB + b) % 3
                    keys = key_blocks(banded, b)
                    pe.wait_ge(s_free[u], n.next(s_free[u]))
                    pe.matmul(ps[:, 4 + u, 0:len(keys) * P], q[rows, b * P:(b + 1) * P],
                              k[rows, keys[0] * P:(keys[-1] + 1) * P], start=True, stop=True).then_inc(s_done[u], 1)

            def transpose_exps(hd, b):
                keys = key_blocks(HEADS[hd][0], b)
                transposed(b % 2, [ss[:, hd % 2, b, j * P:(j + 1) * P] for j in range(len(keys))])

            def weigh(hd, b):
                banded, half = HEADS[hd]
                v = va if banded else vb
                keys = key_blocks(banded, b)
                pe.wait_ge(eT_ready[b % 2], n.next(eT_ready[b % 2]))
                for j, kblock in enumerate(keys):
                    mm = pe.matmul(ps[:, 7, b * DH:(b + 1) * DH], eT[:, b % 2, j * P:(j + 1) * P],
                                   v[:, kblock, 64 * half:64 * half + 64], start=(j == 0), stop=(j == len(keys) - 1))
                return mm

            def attend(hd):
                pe.wait_ge(exp_ready, n.next(exp_ready))
                transpose_exps(hd, 0)
                pe.wait_ge(o_free, n.next(o_free))
                for b in range(QB):
                    if b + 1 < QB:
                        transpose_exps(hd, b + 1)
                    mm = weigh(hd, b)
                mm.then_inc(o_done, 1)

            with n.loop(4, ATT_PER) as t:
                project(Uk, T1, 4)
                pe.wait_ge(qkv_ready, n.next(qkv_ready, 4))
                transpose_values(vbT)
                scores(0)
                scores(1)
                attend(0)
                scores(2)
                attend(1)
                scores(3)
                attend(2)
                attend(3)

            pe.wait_ge(on_ready, n.next(on_ready))
            for f in range(KD):
                if f >= 2:
                    pe.wait_ge(oT_ready[f % 2], n.next(oT_ready[f % 2]))
                transposed(f % 2, [otok[:, b, f * P:(f + 1) * P] for b in range(QB)])
            for b in range(2):
                pe.wait_ge(oT_ready[b], n.next(oT_ready[b]))
            project(Uk, T1, KD)
            sum_squares(T1)

            sum_squares(T1)
            first = True
            pe.wait_ge(u_ready, n.next(u_ready, KD))
            with n.loop(FF_GROUPS, FF_PER):
                project(Uk, T1, KD)
                project(HIDk, T1, KD, ready=hid_ready)
            sum_squares(T1)

            pe.wait_ge(h_ready, n.next(h_ready, 2 * KD))
            project(Hk, T1, KD)
            for m in range(KD):
                if m % 4 == 0:
                    tiles = chunk()
                unit(tiles[2 * (m % 4):2 * (m % 4) + 2], [pt[:, k, :] for k in range(2)], T0, counts_chunk=m % 4 == 0)
            sum_squares(T1)

            ZA, ZB, ZC = ([z[:, k, :] for k in range(4)] for z in (za, zb, zc))

            def pair_products(level):
                b = level % 2
                lhs, rhs = (kk, qg_) if level == 0 else (lk[level % 2], lq[level % 2])
                pe.wait_ge(pair_free[b], n.next(pair_free[b]))
                if level <= 4:
                    pe.matmul(ps[0:META, 6, level * META:(level + 1) * META], lhs[:, S:T], rhs[:, S:T], start=True, stop=True)
                for c in range(CHUNKS_G):
                    mm = pe.matmul(ps[:, 4 + b, c * GCH:(c + 1) * GCH], lhs[:, c * GCH:(c + 1) * GCH],
                                   rhs[:, c * GCH:(c + 1) * GCH], start=True, stop=True)
                mm.then_inc(pair_done[b], 1)

            pe.wait_ge(consts, 2)
            pe.wait_ge(consts2_in, 16 * 6)
            with n.loop(LAYERS, LAYER_PER) as layer:
                sum_squares(T2)
                pe.wait_ge(u_ready, n.next(u_ready, KD))
                pe.sem_inc(passed, 1)
                with n.loop(2, CONV_PER):
                    project(Uk, T2, 4)
                with n.loop(6, GATE_PER):
                    project(Uk, T2, 4)
                unit([ones[:, :]] * 4, ZA, T2, ready=conv_ready)
                project(Uk, T2, 4)
                sum_squares(T2, 4)
                unit([ones[:, :]] * 2, [Hs[4], Hs[5]], T2, ready=sq_ready)
                unit([ones[:, :]], [Hs[6]], T2, ready=sq_ready)

                with n.loop(HEADS_G, GREC_PER):
                    project(Uk, T2, 4)
                    pe.wait_ge(v_ready, n.next(v_ready))
                    for c in range(CHUNKS_G):
                        pe.transpose(ps[:, 7, c * GCH:(c + 1) * GCH], vT[:, c * GCH:(c + 1) * GCH], ident[:, :])
                    pe.transpose(ps[0:META, 6, 2 * P:3 * P], vT[:, S:T], ident[:, :]).then_inc(vtr_done, 1)
                    pe.wait_ge(vtok_ready, n.next(vtok_ready))
                    pair_products(0)
                    for level in range(1, LEVELS + 1):
                        pe.wait_ge(level_ready, n.next(level_ready))
                        pair_products(level)
                    pe.wait_ge(a_ready, n.next(a_ready))
                    for c in range(CHUNKS_G):
                        mm = pe.transpose(ps[:, 7, c * GCH:(c + 1) * GCH], kfull[:, c * GCH:(c + 1) * GCH], ident[:, :])
                    mm.then_inc(kft_done, 1)
                    pe.wait_ge(kft_ready, n.next(kft_ready))
                    for c in range(CHUNKS_G):
                        mm = pe.matmul(ps[:, 6, c * GCH:(c + 1) * GCH], kft[:, c, :], vtok[:, c, :], start=True, stop=True)
                    mm.then_inc(upd_done, 1)
                    pe.wait_ge(state_ready, n.next(state_ready))
                    for c in range(CHUNKS_G + 1):
                        rows, cols = (GCH, slice(c * GCH, (c + 1) * GCH)) if c < CHUNKS_G else (META, slice(S, T))
                        dst = ps[:, 4, cols] if c < CHUNKS_G else ps[:, 5, 0:META]
                        inner = amat[:, c, :] if c < CHUNKS_G else atail
                        mm = pe.matmul(dst, vtok[0:rows, c, :], inner, start=True, stop=(c == 0))
                        if c > 0:
                            mm = pe.matmul(dst, state[:, c, :], qfull[:, cols], start=False, stop=True)
                    mm.then_inc(go_done, 1)
                    pe.wait_ge(go_copied, n.next(go_copied))
                    for h in range(2):
                        mm = pe.matmul(ps[:, 6 + h, 0:T2.width], ones[:, :], T2.part(gsq, h), start=True, stop=True)
                    mm.then_inc(gss_done, 1)

                def causal_scores(hd):
                    for i in range(QT - 1):
                        b = i % 2
                        pe.wait_ge(c_free[b], n.next(c_free[b]))
                        pe.matmul(ps[:, 4 + b, 0:(i + 1) * P], qh_of[hd][:, i * P:(i + 1) * P],
                                  kh_of[hd][:, 0:(i + 1) * P], start=True, stop=True).then_inc(c_done[b], 1)
                    for b in range(2):
                        pe.wait_ge(c_free[b], n.next(c_free[b]))
                        pe.matmul(ps[0:META, 4 + b, 0:T2.width], qh_of[hd][:, S:T], T2.part(kh_of[hd], b),
                                  start=True, stop=True).then_inc(c_done[b], 1)

                def causal_transpose(hd, i):
                    tb = (hd * QT + i) % 2
                    rows = P if i < QT - 1 else META
                    e = exps_of(hd, i)
                    for j in range(i + 1):
                        keys = P if j < QT - 1 else META
                        mm = pe.transpose(ps[0:keys, TRB[tb], j * rows:(j + 1) * rows], e[:, j * P:j * P + keys], ident[0:rows, 0:rows])
                    mm.then_inc(ctr_done[tb], 1)

                def causal_weigh(hd, i):
                    tb = (hd * QT + i) % 2
                    rows = P if i < QT - 1 else META
                    pe.wait_ge(cT_ready[tb], n.next(cT_ready[tb]))
                    for j in range(i + 1):
                        keys = P if j < QT - 1 else META
                        mm = pe.matmul(ps[0:rows, 6, i * DH:(i + 1) * DH], eT2[0:keys, tb, j * rows:(j + 1) * rows],
                                       vt[0:keys, j, hd * DH:(hd + 1) * DH], start=(j == 0), stop=(j == i))
                    return mm

                pe.wait_ge(c_ready, n.next(c_ready))
                pe.wait_ge(zc_ready, n.next(zc_ready))
                pe.sem_inc(passed, 1)
                with n.loop(4, MLA_PER):
                    pe.wait_ge(mlaw_in, n.next(mlaw_in, 16))
                    tile = [mlaw[:, j * P:(j + 1) * P] for j in range(8)]
                    pe.wait_ge(co_free, n.now(co_free) + 1)
                    for j in range(QT):
                        rows = P if j < QT - 1 else META
                        dst = ps[0:rows, 7, j * P:(j + 1) * P] if j < QT - 1 else ps[0:rows, 6, 384:512]
                        mm = pe.matmul(dst, ckv[:, j * P:j * P + rows], tile[6], start=True, stop=True)
                    mm.then_inc(vt_done, 1)
                    for hd in range(2):
                        unit([tile[3 * hd][:, 0:QK], tile[3 * hd + 1][:, 0:QK]], [cq[:, 0, :], cq[:, 1, :]], T2, m=QK)
                        unit([tile[3 * hd + 2][:, 0:NOPE]], [ckv], T2, m=NOPE)
                        unit([ones[0:QK, 0:QK]], [qsq], T2, m=QK, ready=qk_raw)
                        unit([rotm[:, :]], [qgain], T2, m=QK)
                        unit([ones[0:QK, 0:QK]], [ksq], T2, m=QK, ready=qk_raw)
                        unit([rotm[:, :]], [kgain], T2, m=QK)
                    pe.drain().then_inc(mlaw_used, 1)
                    pe.wait_ge(vt_ready, n.next(vt_ready))
                    pe.wait_ge(qk_ready, n.next(qk_ready, 2))
                    causal_scores(0)
                    causal_scores(1)
                    pe.wait_ge(unit_free[1], n.now(unit_free[1]) + 1)
                    for hd in range(2):
                        pe.wait_ge(qexp_ready, n.next(qexp_ready))
                        causal_transpose(hd, 0)
                        pe.wait_ge(co_free, n.next(co_free))
                        for i in range(QT):
                            if i + 1 < QT:
                                causal_transpose(hd, i + 1)
                            mm = causal_weigh(hd, i)
                        mm.then_inc(co_done, 1)

                pe.wait_ge(co_free, n.now(co_free) + 1)
                for f in range(4):
                    tb = f % 2
                    if f >= 2:
                        pe.wait_ge(cT_ready[tb], n.next(cT_ready[tb]))
                    for j in range(QT - 1):
                        mm = pe.transpose(ps[:, TRB[tb], j * P:(j + 1) * P], otok2[:, j, f * P:(f + 1) * P], ident[:, :])
                    mm.then_inc(ctr_done[tb], 1)
                    mm = pe.transpose(ps[:, 6, f * META:(f + 1) * META], otok2[0:META, QT - 1, f * P:(f + 1) * P], ident[0:META, 0:META])
                mm.then_inc(ztail_done, 1)
                for tb in range(2):
                    pe.wait_ge(cT_ready[tb], n.next(cT_ready[tb]))
                pe.wait_ge(zb_ready, n.next(zb_ready))
                pe.sem_inc(passed, 1)
                with n.loop(4, MIX_PER):
                    for _ in range(2):
                        tiles = chunk()
                        unit(tiles[0:4], ZA, T2, counts_chunk=True)
                        unit(tiles[4:8], ZB, T2)
                        tiles = chunk()
                        unit(tiles[0:4], ZC, T2, counts_chunk=True)
                pe.wait_ge(m_done, n.next(m_done, 1))
                project([M[:, k, :] for k in range(KD)], T2, KD)
                sum_squares(T2)
                pe.wait_ge(u_ready, n.next(u_ready, KD))
                pe.sem_inc(passed, 1)
                with n.loop(FF_GROUPS, FF2_PER):
                    project(Uk, T2, KD)
                    project(HIDk, T2, KD, ready=hid_ready)
            pe.drain().then_inc(chunks_started, 1)

        @block.scalar
        def _(act):
            n = Counts(act)
            at = {"unit": 0}

            def take():
                b = at["unit"] % 2
                at["unit"] += 1
                return b, n.next(unit_done[b])

            act.dma_start(v1[:, :], vec1).then_inc(vec_in, 16)
            act.dma_start(sinks[:, :], sink.to_broadcast([P, 8])).then_inc(vec_in, 16)
            act.dma_start(tab[:, :], table).then_inc(bias_in, 16)
            act.dma_start(oneh[:, :], onehot).then_inc(bias_in, 16)
            act.dma_start(addm[:, :], addmask).then_inc(bias_in, 16)
            act.dma_start(H[:, :, META:], xT).then_inc(x_in, 16)
            act.dma_start(H[:, :, 0:META], metaT).then_inc(x_in, 16)
            act.dma_start(pt[:, :, :], pT).then_inc(x_in, 16)

            def root_mean(tok, count, dst=rms[:, 0, :], m=P):
                b, done = take()
                act.wait_ge(unit_done[b], done)
                act.activation(tok.of(dst[0:m]), psum_of(b, tok, m), ACT.Sqrt, bias=EPS, scale=1.0 / count).then_inc(unit_free[b], 1)
                act.drain().then_inc(rms_ready, 1)

            def squares(src, tok, ready=None, free=None):
                for k in range(KD):
                    if ready is not None:
                        act.wait_ge(ready, n.next(ready))
                    act.activation(tok.of(HID[:, k, :]), tok.of(src[:, k, :]), ACT.Square).then_inc(sq_ready, 1)

            act.wait_ge(x_in, 48)
            take()
            take()
            squares(H, T1)
            root_mean(T1, D)

            def evacuate(dst, tok, func=ACT.Copy, bias=0.0, flip=False, ready=None):
                b, done = take()
                act.wait_ge(unit_done[b], done)
                src = psum_of(b, tok)
                if flip:
                    src = ps[:, 2 * b, :].rearrange("p (b q) -> p b q", q=P)[:, :, ::-1]
                    dst = dst.rearrange("p (b q) -> p b q", q=P)
                else:
                    dst = tok.of(dst)
                act.activation(dst, src, func, bias=bias).then_inc(unit_free[b], 1)
                if ready is not None:
                    act.drain().then_inc(ready, 1)

            evacuate(ka, T0, ready=qkv_ready)
            evacuate(vaT, T0, ready=qkv_ready)

            def copy_values(dst):
                act.wait_ge(tr_done[0], n.next(tr_done[0]))
                act.activation(dst[:, 0:2, :], ps[:, 1, 0:2 * P].rearrange("p (j d) -> p j d", d=P), ACT.Copy).then_inc(eT_ready[0], 1)

            copy_values(va)

            def exps(hd):
                banded, half = HEADS[hd]
                act.wait_ge(max_ready, n.next(max_ready))
                for b in range(QB):
                    e = ss[:, hd % 2, b, 0:len(key_blocks(banded, b)) * P]
                    act.activation(e, e, ACT.Exp, bias=(nms if banded else nmax)[:, hd % 2, b:b + 1],
                                   accum_out=den[:, hd % 2, b:b + 1])
                if banded:
                    act.activation(esink[:, hd % 2, :], srel[:, hd % 2, :], ACT.Exp)
                act.drain().then_inc(exp_ready, 1)

            def copy_exps(hd):
                for b in (0, 2):
                    act.wait_ge(tr_done[0], n.next(tr_done[0]))
                    wd = len(key_blocks(HEADS[hd][0], b)) * P
                    act.activation(eT[:, 0, 0:wd], ps[:, 1, 0:wd], ACT.Copy).then_inc(eT_ready[0], 1)

            with n.loop(4, ATT_PER) as t:
                evacuate(qa, T0, flip=True, ready=qkv_ready)
                evacuate(qb, T0, flip=True, ready=qkv_ready)
                evacuate(kb, T0, ready=qkv_ready)
                evacuate(vbT, T0, ready=qkv_ready)
                copy_values(vb)
                exps(0)
                exps(1)
                copy_exps(0)
                exps(2)
                copy_exps(1)
                exps(3)
                copy_exps(2)
                copy_exps(3)

            act.wait_ge(o_free, 1 + 16)
            for b in range(QB):
                for half in range(2):
                    act.activation(ss[:, half, b, :], otok[:, b, half * 512:(half + 1) * 512], ACT.Square,
                                   accum_out=ss8[:, 2 * b + half:2 * b + half + 1])
            act.drain()
            act.activation(rms8[:, :], ss8[:, :], ACT.Sqrt, bias=EPS, scale=1.0 / 512)
            act.drain().then_inc(osq_ready, 1)
            for f in range(0, KD, 2):
                act.wait_ge(tr_done[0], n.next(tr_done[0]))
                act.activation(U[:, f, META:].rearrange("p (b q) -> p b q", q=P),
                               ps[:, 1, :].rearrange("p (b q) -> p b q", q=P)[:, :, ::-1], ACT.Copy,
                               scale=v1[:, V1["g_out"] + f:V1["g_out"] + f + 1]).then_inc(oT_ready[0], 1)

            def out_and_squares(tok):
                for m in range(KD):
                    b, done = take()
                    act.wait_ge(unit_done[b], done)
                    act.activation(tok.of(M[:, m, :]), psum_of(b, tok), ACT.Copy)
                    act.activation(tok.of(HID[:, m, :]), psum_of(b, tok), ACT.Square).then_inc(unit_free[b], 1)
                    act.drain().then_inc(sq_ready, 1)

            out_and_squares(T1)
            root_mean(T1, D)
            squares(H, T1, ready=h_ready)
            root_mean(T1, D)
            with n.loop(FF_GROUPS, FF_PER):
                for m in range(KD):
                    b, done = take()
                    act.wait_ge(unit_done[b], done)
                    act.activation(T1.of(relu[:, m % 2, :]), psum_of(b, T1), ACT.Relu).then_inc(unit_free[b], 1)
                    act.drain()
                    act.activation(T1.of(HID[:, m, :]), T1.of(relu[:, m % 2, :]), ACT.Square).then_inc(hid_ready, 1)
                    n.next(hid_ready)
                for m in range(KD):
                    take()
            squares(M, T1, ready=m_ready)
            root_mean(T1, D)
            for m in range(KD):
                b, done = take()
                act.wait_ge(unit_done[b], done)
                act.activation(T1.of(U[:, m, :]), psum_of(b, T1), ACT.Sigmoid,
                               bias=v1[:, V1["b_gate"] + m:V1["b_gate"] + m + 1]).then_inc(unit_free[b], 1)
                act.drain().then_inc(gate_ready, 1)
            for m in range(KD):
                take()
            squares(M, T1, ready=m_ready)
            root_mean(T1, D)
            n.next(h_ready, 2 * KD)

            with n.loop(LAYERS, LAYER_PER) as layer:
                act.wait_ge(layer_begun, n.next(layer_begun))
                act.wait_ge(lb_max_ready, n.next(lb_max_ready))
                act.activation(lb_e, lb_e, ACT.Exp).then_inc(lb_exp_ready, 1)
                squares(H, T2)
                root_mean(T2, D)
                with n.loop(2, CONV_PER):
                    for j in range(2):
                        evacuate(relu[:, j, :], T2, func=ACT.Sigmoid, ready=sig_ready)
                        take()
                with n.loop(6, GATE_PER) as g:
                    for j in range(4):
                        b, done = take()
                        act.wait_ge(unit_done[b], done)
                        act.activation(gates[:, bass.ds(4 * g + j, 1), :].rearrange("p o (h n) -> p (o h) n", h=2),
                                       psum_of(b, T2), ACT.Sigmoid).then_inc(unit_free[b], 1)
                b, done = take()
                act.wait_ge(unit_done[b], done)
                act.activation(T2.of(mu), psum_of(b, T2), ACT.Copy, scale=1.0 / 512).then_inc(unit_free[b], 1)
                act.drain().then_inc(mean_ready, 1)
                for dst, rows in ((cq[:, 0, :], slice(0, P)), (cq[:, 1, :], slice(0, P)), (ckv, slice(0, P)),
                                  (kraw, slice(NOPE, QK))):
                    b, done = take()
                    act.wait_ge(unit_done[b], done)
                    act.activation(T2.of(dst[rows]), ps[rows, 2 * b:2 * b + 2, 0:T2.width], ACT.Copy).then_inc(unit_free[b], 1)
                act.drain()
                act.wait_ge(centred, n.next(centred))
                for src, dst in ((za[:, 0, :], 0), (za[:, 1, :], 1), (za[:, 2, :], 2), (za[:, 3, :], 3),
                                 (cq[:, 0, :], 4), (cq[:, 1, :], 5), (ckv, 6)):
                    act.activation(Hs[dst], src, ACT.Square).then_inc(sq_ready, 1)
                root_mean(T2, 512)
                root_mean(T2, 256, dst=rms[:, 1, :])
                root_mean(T2, P, dst=rms_v)
                act.wait_ge(ln_ready, n.next(ln_ready))
                for k in range(4):
                    act.activation(Hs[k], za[:, k, :], ACT.Sigmoid, bias=v2[:, V2["ln_b"] + k:V2["ln_b"] + k + 1])
                act.drain().then_inc(lnsig_ready, 1)

                with n.loop(HEADS_G, GREC_PER):
                    b, done = take()
                    act.wait_ge(unit_done[b], done)
                    act.activation(T2.of(relu[:, 0, :]), psum_of(b, T2), ACT.Sigmoid, scale=-1.0).then_inc(unit_free[b], 1)
                    act.drain().then_inc(f_sig, 1)
                    evacuate(qg_, T2, ready=q_ready)
                    for dst in (Hs[6], Hs[5]):
                        b, done = take()
                        act.wait_ge(unit_done[b], done)
                        act.activation(T2.of(dst), psum_of(b, T2), ACT.Sigmoid)
                        act.drain().then_inc(sig_ready, 1)
                    act.wait_ge(vtr_done, n.next(vtr_done))
                    act.activation(vtok[:, 0:CHUNKS_G, :], ps[:, 7, :].rearrange("p (c d) -> p c d", d=P), ACT.Copy)
                    act.activation(vtok[0:META, CHUNKS_G, :], ps[0:META, 6, 2 * P:3 * P], ACT.Copy)
                    act.drain().then_inc(vtok_ready, 1)
                    act.wait_ge(kft_done, n.next(kft_done))
                    act.activation(kft, ps[:, 7, :].rearrange("p (c d) -> p c d", d=P), ACT.Copy).then_inc(kft_ready, 1)
                    act.wait_ge(go_done, n.next(go_done))
                    for dst, func in ((oT, ACT.Copy), (gsq, ACT.Square)):
                        act.activation(dst[:, 0:S], ps[:, 4, :], func)
                        act.activation(dst[:, S:T], ps[:, 5, 0:META], func)
                    act.drain().then_inc(go_copied, 1)
                    act.wait_ge(gss_done, n.next(gss_done))
                    act.activation(T2.of(rms[:, 0, :]), ps[:, 6:8, 0:T2.width], ACT.Sqrt, bias=EPS, scale=1.0 / P)
                    act.drain().then_inc(rms_ready, 1)

                def causal_exps(hd):
                    act.wait_ge(qmax_ready, n.next(qmax_ready))
                    for i in range(QT):
                        rows = P if i < QT - 1 else META
                        e = exps_of(hd, i)[:, 0:min((i + 1) * P, T)]
                        act.activation(e, e, ACT.Exp, bias=qmax[0:rows, hd, i:i + 1], accum_out=qden[0:rows, hd, i:i + 1])
                    act.drain().then_inc(qexp_ready, 1)

                def copy_causal(hd):
                    for i in range(QT):
                        if (hd * QT + i) % 2 == 0:
                            copy_causal_tile(act, n, i)

                with n.loop(4, MLA_PER):
                    act.wait_ge(vt_done, n.next(vt_done))
                    act.activation(vt[:, 0:QT - 1, :], ps[:, 7, :].rearrange("p (c d) -> p c d", d=P), ACT.Copy)
                    act.activation(vt[0:META, QT - 1, :], ps[0:META, 6, 384:512], ACT.Copy)
                    act.drain().then_inc(vt_ready, 1)
                    for hd in range(2):
                        act.wait_ge(qk_free, n.next(qk_free))
                        b, done = take()
                        act.wait_ge(unit_done[b], done)
                        act.activation(T2.of(qsq), psum_of(b, T2, QK), ACT.Square)
                        act.activation(T2.of(qgain), psum_of(b, T2, QK), ACT.Copy, scale=v2[0:QK, V2["q_norm"]:V2["q_norm"] + 1]).then_inc(unit_free[b], 1)
                        act.drain().then_inc(qk_raw, 1)
                        b, done = take()
                        act.wait_ge(unit_done[b], done)
                        act.activation(T2.of(kraw[0:NOPE]), psum_of(b, T2, NOPE), ACT.Copy).then_inc(unit_free[b], 1)
                        act.drain()
                        act.activation(ksq, kraw[0:QK], ACT.Square)
                        act.activation(kgain, kraw[0:QK], ACT.Copy, scale=v2[0:QK, V2["k_norm"]:V2["k_norm"] + 1])
                        act.drain().then_inc(qk_raw, 1)
                        for side in range(2):
                            root_mean(T2, QK, dst=rms[:, side, :], m=QK)
                            take()
                    causal_exps(0)
                    causal_exps(1)
                    copy_causal(0)
                    copy_causal(1)
                for f in (0, 2):
                    act.wait_ge(ctr_done[0], n.next(ctr_done[0]))
                    act.activation(zb[:, f, 0:S], ps[:, TRB[0], :], ACT.Copy).then_inc(cT_ready[0], 1)
                act.wait_ge(ztail_done, n.next(ztail_done))
                act.activation(zb[:, :, S:T], ps[:, 6, 0:4 * META].rearrange("p (f t) -> p f t", f=4), ACT.Copy).then_inc(zb_ready, 1)
                with n.loop(4, MIX_PER):
                    for _ in range(6):
                        take()
                for _ in range(KD):
                    take()
                squares(H, T2, ready=h_ready)
                root_mean(T2, D)
                with n.loop(FF_GROUPS, FF2_PER):
                    for m in range(KD):
                        b, done = take()
                        act.wait_ge(unit_done[b], done)
                        act.activation(T2.of(relu[:, m % 2, :]), psum_of(b, T2), ACT.Relu).then_inc(unit_free[b], 1)
                        act.drain()
                        act.activation(HID[:, m, :], relu[:, m % 2, :], ACT.Square).then_inc(hid_ready, 1)
                        n.next(hid_ready)
                    for m in range(KD):
                        take()
            act.wait_ge(layer_begun, n.next(layer_begun))
            act.dma_start(out, H[:, :, META:]).then_inc(out_done, 16)
            act.wait_ge(out_done, 16)

        @block.vector
        def _(dve):
            n = Counts(dve)
            at = {"unit": 0}
            for b in range(2):
                dve.sem_inc(unit_free[b], 1)
            for b in range(3):
                dve.sem_inc(s_free[b], 1)
            dve.sem_inc(o_free, 1)
            dve.sem_inc(bw_used, 1)
            for b in range(2):
                dve.sem_inc(pair_free[b], 1)
                dve.sem_inc(c_free[b], 1)
            dve.sem_inc(co_free, 1)
            dve.sem_inc(qk_free, 1)

            def take():
                b = at["unit"] % 2
                at["unit"] += 1
                return b, n.next(unit_done[b])

            def col(name, k):
                return v1[:, V1[name] + k:V1[name] + k + 1]

            def norm(src, dst, gain, tok):
                dve.wait_ge(rms_ready, n.next(rms_ready))
                dve.reciprocal(tok.of(rstd), tok.of(rms[:, 0, :]))
                dve.drain()
                for k in range(KD):
                    dve.scalar_tensor_tensor(tok.of(dst[:, k, :]), tok.of(src[:, k, :]), col(gain, k), tok.of(rstd),
                                             ALU.mult, ALU.mult).then_inc(u_ready, 1)

            def norm_and_add(gain, tok):
                dve.wait_ge(rms_ready, n.next(rms_ready))
                dve.reciprocal(tok.of(rstd), tok.of(rms[:, 0, :]))
                dve.drain()
                for k in range(KD):
                    dve.scalar_tensor_tensor(tok.of(M[:, k, :]), tok.of(M[:, k, :]), col(gain, k), tok.of(rstd),
                                             ALU.mult, ALU.mult)
                dve.drain()
                for k in range(KD):
                    dve.tensor_tensor(tok.of(H[:, k, :]), tok.of(H[:, k, :]), tok.of(M[:, k, :]), ALU.add).then_inc(h_ready, 1)

            dve.wait_ge(vec_in, 32)
            dve.tensor_scalar(nsinks[:, :], sinks[:, :], -1.0, None, ALU.mult)
            dve.wait_ge(bias_in, 48)
            for h in range(2):
                b, done = take()
                dve.wait_ge(unit_done[b], done)
                dve.tensor_tensor(brow[:, h * 512:(h + 1) * 512], ps[0:16, 2 * b, :], addm[:, h * 512:(h + 1) * 512],
                                  ALU.add).then_inc(unit_free[b], 1)
            dve.drain().then_inc(brow_ready, 1)
            dve.wait_ge(x_in, 48)
            take()
            norm(H, U, "g_pre_mix", T1)
            take()
            take()

            def copy_values(dst):
                dve.wait_ge(tr_done[1], n.next(tr_done[1]))
                dve.tensor_copy(dst[:, 2:4, :], ps[:, 3, 0:2 * P].rearrange("p (j d) -> p j d", d=P)).then_inc(eT_ready[1], 1)

            copy_values(va)

            def maxima(hd, t):
                banded, half = HEADS[hd]
                i = hd % 2
                for b in range(QB):
                    u = (hd * QB + b) % 3
                    keys = key_blocks(banded, b)
                    wd = len(keys) * P
                    c = 384 - P * b + keys[0] * P
                    dve.wait_ge(s_done[u], n.next(s_done[u]))
                    dve.scalar_tensor_tensor(ss[:, i, b, 0:wd], ps[:, 4 + u, 0:wd], DH ** -0.5, bw[:, hd, c:c + wd],
                                             ALU.mult, ALU.add).then_inc(s_free[u], 1)
                dve.drain()
                for b in range(QB):
                    wd = len(key_blocks(banded, b)) * P
                    dve.tensor_reduce(nmax[:, i, b:b + 1], ss[:, i, b, 0:wd], AX, ALU.max, negate=True)
                if banded:
                    dve.drain()
                    dve.tensor_tensor(nms[:, i, :], nmax[:, i, :], nsinks[:, bass.ds(t + 4 * half, 1)].to_broadcast([P, 4]), ALU.min)
                    dve.drain()
                    dve.tensor_tensor(srel[:, i, :], nms[:, i, :], sinks[:, bass.ds(t + 4 * half, 1)].to_broadcast([P, 4]), ALU.add)
                dve.drain().then_inc(max_ready, 1)

            def outputs(hd, t):
                banded, half = HEADS[hd]
                i = hd % 2
                for b in (1, 3):
                    wd = len(key_blocks(banded, b)) * P
                    dve.wait_ge(tr_done[1], n.next(tr_done[1]))
                    dve.tensor_copy(eT[:, 1, 0:wd], ps[:, 3, 0:wd]).then_inc(eT_ready[1], 1)
                dve.wait_ge(exp_ready, n.next(exp_ready))
                total = den
                if banded:
                    dve.tensor_tensor(den2[:, i, :], den[:, i, :], esink[:, i, :], ALU.add)
                    total = den2
                    dve.drain()
                dve.reciprocal(rinv[:, i, :], total[:, i, :])
                dve.drain()
                dve.wait_ge(o_done, n.next(o_done))
                at_col = t * DH + 256 * half if banded else t * P + 512 + DH * half
                dve.tensor_tensor(otok[:, :, bass.ds(at_col, DH)], ps[:, 7, 0:QB * DH].rearrange("p (b d) -> p b d", d=DH),
                                  rinv[:, i, :].unsqueeze(2).to_broadcast([P, QB, DH]), ALU.mult).then_inc(o_free, 1)

            with n.loop(4, ATT_PER) as t:
                for _ in range(4):
                    take()
                copy_values(vb)
                dve.wait_ge(bw_in, n.next(bw_in, 64))
                maxima(0, t)
                maxima(1, t)
                outputs(0, t)
                maxima(2, t)
                outputs(1, t)
                maxima(3, t)
                dve.drain().then_inc(bw_used, 1)
                outputs(2, t)
                outputs(3, t)

            dve.wait_ge(osq_ready, 1)
            dve.reciprocal(r8[:, :], rms8[:, :])
            dve.drain()
            for b in range(QB):
                for half in range(2):
                    o = otok[:, b, half * 512:(half + 1) * 512]
                    dve.tensor_scalar(o, o, r8[:, 2 * b + half:2 * b + half + 1], None, ALU.mult)
            dve.drain().then_inc(on_ready, 1)
            for f in range(1, KD, 2):
                dve.wait_ge(tr_done[1], n.next(tr_done[1]))
                dve.tensor_scalar(U[:, f, META:].rearrange("p (b q) -> p b q", q=P),
                                  ps[:, 3, :].rearrange("p (b q) -> p b q", q=P)[:, :, ::-1],
                                  col("g_out", f), None, ALU.mult).then_inc(oT_ready[1], 1)
            for m in range(KD):
                take()
            take()
            norm_and_add("g_post_mix", T1)
            take()
            norm(H, U, "g_pre_mlp", T1)
            dve.wait_ge(m_zero, 1)
            with n.loop(FF_GROUPS, FF_PER):
                for m in range(KD):
                    take()
                    n.next(hid_ready)
                for m in range(KD):
                    b, done = take()
                    dve.wait_ge(unit_done[b], done)
                    dve.tensor_tensor(T1.of(M[:, m, :]), T1.of(M[:, m, :]), psum_of(b, T1), ALU.add).then_inc(unit_free[b], 1)
                dve.drain()
            for m in range(KD):
                dve.sem_inc(m_ready, 1)
            take()
            norm_and_add("g_post_mlp", T1)
            for m in range(KD):
                take()
            for m in range(KD):
                b, done = take()
                dve.wait_ge(gate_ready, n.next(gate_ready))
                dve.wait_ge(unit_done[b], done)
                dve.tensor_tensor(T1.of(M[:, m, :]), psum_of(b, T1), T1.of(U[:, m, :]), ALU.mult).then_inc(unit_free[b], 1)
                dve.drain().then_inc(m_ready, 1)
            take()
            norm_and_add("g_post_ple", T1)

            def col2(name, k=0, rows=P):
                return v2[0:rows, V2[name] + k:V2[name] + k + 1]

            def norm2(gain):
                dve.wait_ge(rms_ready, n.next(rms_ready))
                dve.reciprocal(rstd[:, :], rms[:, 0, :])
                dve.drain()
                for k in range(KD):
                    dve.scalar_tensor_tensor(U[:, k, :], H[:, k, :], col2(gain, k), rstd[:, :], ALU.mult, ALU.mult).then_inc(u_ready, 1)

            def gated(dst, sig):
                b, done = take()
                dve.wait_ge(unit_done[b], done)
                dve.wait_ge(sig_ready, n.next(sig_ready))
                dve.tensor_tensor(dst, psum_of(b, T2), T2.of(sig), ALU.mult).then_inc(unit_free[b], 1)

            pairm3 = pairm[:, :].rearrange("p (l t) -> p l t", t=GCH)

            def level_operands(level):
                size, i = 2 ** (level - 1), level % 2
                dve.tensor_tensor(level_blocks(lq[i], size, 1), level_blocks(qg_, size, 1), level_blocks(pre, size, 1), ALU.mult)
                dve.tensor_tensor(level_blocks(lk[i], size, 0), level_blocks(kk, size, 0), level_blocks(suf, size, 0), ALU.mult)
                dve.drain().then_inc(level_ready, 1)

            def level_up(level):
                size = 2 ** (level - 1)
                dve.tensor_tensor(level_blocks(suf, size, 0), level_blocks(suf, size, 0), level_total(pre, size, 1), ALU.mult)
                dve.drain()
                dve.tensor_tensor(level_blocks(pre, size, 1), level_blocks(pre, size, 1), level_total(pre, size, 0), ALU.mult)
                dve.drain()

            def select_pairs(level):
                b = level % 2
                dve.drain()
                mask = pairm3[:, level, :].unsqueeze(1).to_broadcast([P, CHUNKS_G, GCH])
                dve.wait_ge(pair_done[b], n.next(pair_done[b]))
                dve.sem_inc(passed, 1)
                dve.copy_predicated(amat, mask, ps[:, 4 + b, :].rearrange("p (c t) -> p c t", t=GCH)).then_inc(pair_free[b], 1)

            def select_tails():
                for level in range(5):
                    dve.drain()
                    dve.copy_predicated(atail, pairm3[0:META, level, 0:META], ps[0:META, 6, level * META:(level + 1) * META])

            dve.wait_ge(consts2_in, 96)
            dve.tensor_copy(pairm[:, :], pairf)
            dve.drain()
            with n.loop(LAYERS, LAYER_PER) as layer:
                dve.tensor_copy(v2[:, :], v2all[:, bass.ds(layer, 1), :].rearrange("p o c -> p (o c)"))
                dve.drain().then_inc(layer_begun, 1)
                lb01 = v2[:, V2["lb0"]:V2["lb0"] + 8].rearrange("p (l h) -> p l h", l=2)
                dve.tensor_tensor(lb_max, lb01[:, 0, :], lb01[:, 1, :], ALU.max)
                dve.drain()
                dve.tensor_tensor(lb_e, lb01, lb_max.unsqueeze(1).to_broadcast([P, 2, 4]), ALU.subtract)
                dve.drain().then_inc(lb_max_ready, 1)
                dve.wait_ge(lb_exp_ready, n.next(lb_exp_ready))
                dve.tensor_tensor(lb_sum, lb_e[:, 0, :], lb_e[:, 1, :], ALU.add)
                dve.drain()
                dve.reciprocal(lb_sum, lb_sum)
                dve.drain()
                dve.tensor_tensor(lb_e, lb_e, lb_sum.unsqueeze(1).to_broadcast([P, 2, 4]), ALU.mult)
                dve.drain()
                dve.scalar_tensor_tensor(oml, lb_e[:, 1, :], col2("second"), lb_e[:, 0, :], ALU.mult, ALU.add)
                dve.drain()
                dve.tensor_tensor(oml, oml, lb_e[:, 0, :], ALU.subtract)
                dve.drain()
                dve.tensor_scalar(oml, oml, -1.0, 1.0, ALU.mult, ALU.add)

                dve.drain()
                take()
                norm2("norm1")
                with n.loop(2, CONV_PER) as c:
                    for j in range(2):
                        take()
                        gated(hc[:, bass.ds(2 * c + j, 1), TAPS - 1:].rearrange("p o (h n) -> p (o h) n", h=2), relu[:, j, :])
                dve.drain()
                dve.wait_ge(hc_padded, n.next(hc_padded))
                for k in range(TAPS):
                    for t in range(CONV_TILES):
                        x, wk = hc[:, t, k:k + T], col2("conv_w", t * TAPS + k)
                        if k == 0:
                            ins = dve.tensor_scalar(za[:, t, :], x, wk, col2("conv_b", t), ALU.mult, ALU.add)
                        else:
                            ins = dve.scalar_tensor_tensor(za[:, t, :], x, wk, za[:, t, :], ALU.mult, ALU.add)
                        if k == TAPS - 1:
                            ins.then_inc(conv_ready, 1)
                    dve.drain()
                dve.drain().then_inc(mlaw_used, 1)
                with n.loop(6, GATE_PER):
                    for _ in range(4):
                        take()
                take()
                dve.wait_ge(mean_ready, n.next(mean_ready))
                for t in range(CONV_TILES):
                    dve.tensor_tensor(za[:, t, :], za[:, t, :], mu, ALU.subtract)
                dve.drain().then_inc(centred, 1)
                for _ in range(4):
                    take()
                take()
                dve.wait_ge(rms_ready, n.next(rms_ready))
                dve.reciprocal(rstd[:, :], rms[:, 0, :])
                dve.drain()
                for t in range(CONV_TILES):
                    dve.scalar_tensor_tensor(za[:, t, :], za[:, t, :], col2("ln_g", t), rstd[:, :], ALU.mult, ALU.mult)
                dve.drain().then_inc(ln_ready, 1)
                for src, count, names in ((rms[:, 1, :], 2, "q_a"), (rms_v, 1, "kv_a")):
                    take()
                    dve.wait_ge(rms_ready, n.next(rms_ready))
                    dve.reciprocal(rstd[:, :], src)
                    dve.drain()
                    for k in range(count):
                        x = cq[:, k, :] if count == 2 else ckv
                        dve.scalar_tensor_tensor(x, x, col2(names, k), rstd[:, :], ALU.mult, ALU.mult)
                    dve.drain()
                dve.drain().then_inc(c_ready, 1)
                dve.wait_ge(lnsig_ready, n.next(lnsig_ready))
                for t in range(CONV_TILES):
                    dve.scalar_tensor_tensor(za[:, t, :], za[:, t, :], col2("ln_b", t), Hs[t], ALU.add, ALU.mult)

                with n.loop(HEADS_G, GREC_PER) as h:
                    dve.drain()
                    dve.tensor_copy(headcol[:, 0:1], oml[:, bass.ds(h, 1)])
                    dve.tensor_copy(headcol[:, 1:2], v2[:, bass.ds(h + V2["hgrn_g"], 1)])
                    dve.memset(suf, 1.0)
                    dve.drain()
                    take()
                    dve.wait_ge(f_sig, n.next(f_sig))
                    dve.tensor_scalar(kk, relu[:, 0, :], headcol[:, 0:1], None, ALU.mult)
                    dve.drain()
                    dve.tensor_scalar(pre, kk, CLAMP, -1.0, ALU.min, ALU.mult)
                    dve.drain()
                    dve.tensor_scalar(pre, pre, 1.0, None, ALU.add)
                    dve.drain()
                    take()
                    dve.wait_ge(q_ready, n.next(q_ready))
                    level_operands(1)
                    level_up(1)
                    level_operands(2)
                    level_up(2)
                    gated(T2.of(vT), Hs[6])
                    dve.drain().then_inc(v_ready, 1)
                    select_pairs(0)
                    select_pairs(1)
                    level_operands(3)
                    level_up(3)
                    gated(T2.of(gs), Hs[5])
                    for level in range(4, LEVELS + 1):
                        select_pairs(level - 2)
                        level_operands(level)
                        level_up(level)
                        if level == 6:
                            select_tails()
                    dve.tensor_tensor(qfull, qg_, pre, ALU.mult)
                    dve.tensor_tensor(kfull[:, 0:S], kk[:, 0:S], suf[:, 0:S], ALU.mult)
                    select_pairs(LEVELS - 1)
                    select_pairs(LEVELS)
                    dve.drain().then_inc(a_ready, 1)
                    dve.wait_ge(upd_done, n.next(upd_done))
                    dve.tensor_copy(state[:, 1, :], ps[:, 6, 0:GCH])
                    for c in range(1, CHUNKS_G):
                        dve.drain()
                        dve.scalar_tensor_tensor(state[:, c + 1, :], state[:, c, :], pre[:, (c + 1) * GCH - 1:(c + 1) * GCH],
                                                 ps[:, 6, c * GCH:(c + 1) * GCH], ALU.mult, ALU.add)
                    dve.drain().then_inc(state_ready, 1)
                    dve.wait_ge(rms_ready, n.next(rms_ready))
                    dve.reciprocal(rstd[:, :], rms[:, 0, :])
                    dve.drain()
                    dve.scalar_tensor_tensor(oT, oT, headcol[:, 1:2], rstd[:, :], ALU.mult, ALU.mult)
                    dve.drain()
                    dve.tensor_tensor(zc[:, bass.ds(h, 1), :].rearrange("p o t -> p (o t)"), oT, gs, ALU.mult)

                dve.drain().then_inc(zc_ready, 1)

                def rotated(src, dst, side, hd):
                    take()
                    dve.tensor_tensor(dst, src, cosT, ALU.mult)
                    dve.wait_ge(rms_ready, n.next(rms_ready))
                    dve.reciprocal(rstd[0:QK, :], rms[0:QK, side, :])
                    b, done = take()
                    dve.wait_ge(unit_done[b], done)
                    dve.tensor_tensor(T2.of(rot1), psum_of(b, T2, QK), T2.of(sinT), ALU.mult).then_inc(unit_free[b], 1)
                    dve.drain()
                    dve.tensor_tensor(dst, dst, rot1, ALU.add)
                    dve.drain()
                    dve.tensor_tensor(dst, dst, rstd[0:QK, :], ALU.mult)
                    dve.drain()

                def causal_maxima(hd):
                    for i in range(QT):
                        e = exps_of(hd, i)
                        if i < QT - 1:
                            b, wd = i % 2, (i + 1) * P
                            dve.wait_ge(c_done[b], n.next(c_done[b]))
                            dve.scalar_tensor_tensor(e[:, 0:wd], ps[:, 4 + b, 0:wd], QK ** -0.5, triT[:, S - i * P:S + P],
                                                     ALU.mult, ALU.add).then_inc(c_free[b], 1)
                        else:
                            for b in range(2):
                                dve.wait_ge(c_done[b], n.next(c_done[b]))
                                dve.scalar_tensor_tensor(T2.part(e, b), ps[0:META, 4 + b, 0:T2.width], QK ** -0.5,
                                                         triT[0:META, b * T2.width:(b + 1) * T2.width],
                                                         ALU.mult, ALU.add).then_inc(c_free[b], 1)
                    dve.drain()
                    for i in range(QT):
                        e = exps_of(hd, i)[:, 0:min((i + 1) * P, T)]
                        rows = P if i < QT - 1 else META
                        dve.tensor_reduce(qmax[0:rows, hd, i:i + 1], e, AX, ALU.max, negate=True)
                    dve.drain().then_inc(qmax_ready, 1)

                def causal_outputs(hd, pair):
                    for i in range(QT):
                        if (hd * QT + i) % 2 == 1:
                            copy_causal_tile(dve, n, i)
                    dve.wait_ge(qexp_ready, n.next(qexp_ready))
                    dve.reciprocal(qinv[:, hd, 0:QT - 1], qden[:, hd, 0:QT - 1])
                    dve.reciprocal(qinv[0:META, hd, QT - 1:QT], qden[0:META, hd, QT - 1:QT])
                    dve.drain()
                    dve.wait_ge(co_done, n.next(co_done))
                    cols = bass.ds(pair * P + hd * DH, DH)
                    dve.tensor_tensor(otok2[:, 0:QT - 1, cols], ps[:, 6, 0:(QT - 1) * DH].rearrange("p (b d) -> p b d", d=DH),
                                      qinv[:, hd, 0:QT - 1].unsqueeze(2).to_broadcast([P, QT - 1, DH]), ALU.mult)
                    dve.tensor_scalar(otok2[0:META, QT - 1, cols], ps[0:META, 6, (QT - 1) * DH:QT * DH],
                                      qinv[0:META, hd, QT - 1:QT], None, ALU.mult)
                    dve.drain().then_inc(co_free, 1)

                with n.loop(4, MLA_PER) as pair:
                    for hd in range(2):
                        take()
                        take()
                        dve.wait_ge(qk_raw, n.next(qk_raw, 2))
                        rotated(qgain, qh_of[hd], 0, hd)
                        rotated(kgain, kh_of[hd], 1, hd)
                        dve.drain().then_inc(qk_ready, 1)
                        dve.drain().then_inc(qk_free, 1)
                    causal_maxima(0)
                    causal_maxima(1)
                    causal_outputs(0, pair)
                    causal_outputs(1, pair)
                for f in (1, 3):
                    dve.wait_ge(ctr_done[1], n.next(ctr_done[1]))
                    dve.tensor_copy(zb[:, f, 0:S], ps[:, TRB[1], :]).then_inc(cT_ready[1], 1)

                def gate_of(branch, m):
                    return gates[:, bass.ds(m + branch * KD, 1), :].rearrange("p o (h n) -> p (o h) n", h=2)

                with n.loop(4, MIX_PER) as i:
                    for j in range(2):
                        m = 2 * i + j
                        mix = M[:, bass.ds(m, 1), :].rearrange("p o (h n) -> p (o h) n", h=2)
                        for branch in range(3):
                            b, done = take()
                            dve.wait_ge(unit_done[b], done)
                            dst = mix if branch == 0 else T2.of(relu[:, branch - 1, :])
                            dve.tensor_tensor(dst, psum_of(b, T2), gate_of(branch, m), ALU.mult).then_inc(unit_free[b], 1)
                        dve.drain()
                        dve.tensor_tensor(mix, mix, T2.of(relu[:, 0, :]), ALU.add)
                        dve.drain()
                        dve.tensor_tensor(mix, mix, T2.of(relu[:, 1, :]), ALU.add)
                        dve.drain()
                dve.drain().then_inc(m_done, 1)
                for m in range(KD):
                    b, done = take()
                    dve.wait_ge(unit_done[b], done)
                    dve.tensor_tensor(T2.of(H[:, m, :]), T2.of(H[:, m, :]), psum_of(b, T2), ALU.add).then_inc(unit_free[b], 1)
                    dve.drain().then_inc(h_ready, 1)
                take()
                norm2("norm2")
                with n.loop(FF_GROUPS, FF2_PER):
                    for m in range(KD):
                        take()
                        n.next(hid_ready)
                    for m in range(KD):
                        b, done = take()
                        dve.wait_ge(unit_done[b], done)
                        dve.tensor_tensor(T2.of(H[:, m, :]), T2.of(H[:, m, :]), psum_of(b, T2), ALU.add).then_inc(unit_free[b], 1)
                    dve.drain()
            dve.drain().then_inc(layer_begun, 1)


def tiles_of(wt):
    k, m = wt.shape
    return wt.reshape(k // P, P, m // P, P).transpose(2, 1, 0, 3).reshape(m // P, P, k)


def columns(v):
    return np.ascontiguousarray(v.reshape(-1, P).T)


def layout_first(a):
    w_in = a["w_in"][0]
    head = lambda base, h: w_in[:, base + h * DH:base + (h + 1) * DH]
    q_a = tiles_of(np.concatenate([head(0, h) for t in range(4) for h in (t, t + 4)], axis=1))
    ka, va = tiles_of(w_in[:, 512:640]), tiles_of(w_in[:, 640:768])
    q_b, k_b, v_b = (tiles_of(w_in[:, 768 + 512 * i:1280 + 512 * i]) for i in range(3))
    chunks = [ka[0], va[0]]
    for t in range(4):
        chunks += [q_a[t], q_b[t], k_b[t], v_b[t]]
    chunks += list(tiles_of(a["w_o"][0]))
    up, down = tiles_of(a["w_up"][0]), a["w_down"][0]
    for g in range(FF_GROUPS):
        chunks += list(up[8 * g:8 * g + 8]) + list(tiles_of(down[D * g:D * (g + 1)]))
    chunks += list(tiles_of(a["w_ple_gate"][0]))
    ple = tiles_of(a["w_ple_proj"][0])
    chunks += [np.concatenate(list(ple[4 * i:4 * i + 4]), axis=1) for i in range(2)]
    assert len(chunks) == N1_CHUNKS
    return chunks


def layout_second(a):
    ring_chunks, head_chunks = [], []
    for l in range(LAYERS):
        wt = tiles_of(np.concatenate([a["w_in_2"][l][:, :1408], np.zeros((D, NOPE), np.float32), a["w_in_2"][l][:, 1408:1440],
                                      np.zeros((D, P - QK), np.float32), a["w_in_2"][l][:, 1440:]], axis=1))
        value, gate, latent, rec, gates = wt[0:4], wt[4:8], wt[8:12], wt[12:28], wt[28:52]
        for t in range(4):
            ring_chunks += [gate[t], value[t]]
        ring_chunks += list(gates) + list(latent)
        q, f, i, g = (rec[4 * k:4 * k + 4] for k in range(4))
        for h in range(HEADS_G):
            ring_chunks += [f[h], q[h], i[h], g[h]]
        uq, ukv = a["w_uq_2"][l], a["w_ukv_2"][l]
        for pair in range(4):
            c = np.zeros((P, 8, P), np.float32)
            for j in range(2):
                h = 2 * pair + j
                c[:, 3 * j:3 * j + 2, :QK] = uq[:, h * QK:(h + 1) * QK].reshape(2, P, QK).transpose(1, 0, 2)
                c[:, 3 * j + 2, :NOPE] = ukv[:, h * P:h * P + NOPE]
                c[:, 6, j * DH:(j + 1) * DH] = ukv[:, h * P + NOPE:(h + 1) * P]
            head_chunks.append(c.reshape(P, CH))
        conv, att, rec = (tiles_of(a[k][l]) for k in ("w_conv_out_2", "w_attn_out_2", "w_hgrn_out_2"))
        for m in range(KD):
            ring_chunks += [np.concatenate([conv[m], att[m]], axis=1),
                            np.concatenate([rec[m], np.zeros((P, 512), np.float32)], axis=1)]
        ring_chunks += list(tiles_of(a["w_out_2"][l]))
        up, down = tiles_of(a["w_ff1_2"][l]), a["w_ff2_2"][l]
        for g in range(FF_GROUPS):
            ring_chunks += list(up[8 * g:8 * g + 8]) + list(tiles_of(down[D * g:D * (g + 1)]))
    assert len(ring_chunks) == LAYERS * N2_CHUNKS
    return ring_chunks, head_chunks


def vectors_second(a):
    out = []
    for l in range(LAYERS):
        pad = lambda v: np.concatenate([v, np.zeros(P - QK, np.float32)])
        out.append(np.concatenate([
            columns(a["norm1_g_2"][l]),
            a["conv_w_2"][l].T.reshape(CONV_TILES, P, TAPS).transpose(1, 0, 2).reshape(P, -1),
            columns(a["conv_b_2"][l]), columns(a["conv_ln_g_2"][l]), columns(a["conv_ln_b_2"][l]),
            columns(a["q_a_norm_g_2"][l]), columns(a["kv_a_norm_g_2"][l]), columns(pad(a["q_norm_g_2"][l])),
            columns(pad(a["k_norm_g_2"][l])), columns(a["hgrn_lb_logits_2"][0]), columns(a["hgrn_lb_logits_2"][1]),
            np.full((P, 1), float(l), np.float32), columns(a["hgrn_norm_g_2"][l]), columns(a["norm2_g_2"][l])], axis=1))
    return np.stack(out, axis=1)


def rotary_constants():
    half = ROPE // 2
    freq = np.float32(10000.0) ** (-np.arange(half, dtype=np.float32) / np.float32(half))
    ang = (np.arange(T, dtype=np.float32)[None, :] * freq[:, None]).astype(np.float32)
    cosines, sines = np.ones((QK, T), np.float32), np.zeros((QK, T), np.float32)
    cosines[NOPE:] = np.concatenate([np.cos(ang)] * 2)
    sines[NOPE:] = np.concatenate([np.sin(ang)] * 2)
    turn = np.zeros((QK, QK), np.float32)
    for j in range(half):
        turn[NOPE + half + j, NOPE + j] = -1.0
        turn[NOPE + j, NOPE + half + j] = 1.0
    return cosines, sines, turn


def mask_constants():
    causal = np.zeros((P, 640), np.float32)
    causal[:, S:] = np.where(np.arange(P)[None, :] <= np.arange(P)[:, None], 0.0, NEG)
    s, t = np.arange(GCH)[:, None], np.arange(GCH)[None, :]
    masks = [s == t]
    for level in range(1, LEVELS + 1):
        size = 2 ** (level - 1)
        masks.append((s // (2 * size) == t // (2 * size)) & (s % (2 * size) < size) & (t % (2 * size) >= size))
    return causal, np.concatenate(masks, axis=1).astype(np.float32)


def distance_constants():
    rel = np.arange(REL) - 511
    n = np.abs(rel)
    large = 8 + (np.log(np.maximum(n, 1) / 8.0) / np.log(128.0) * 8).astype(np.int64)
    bucket = np.where(rel > 0, 16, 0) + np.where(n < 8, n, np.minimum(large, 15))
    onehot = (np.arange(32)[:, None] == bucket[None, :]).astype(np.float32)
    seen = np.zeros(REL)
    for window, dil in DILATED:
        seen += (rel % dil == 0) & (n <= window // 2)
    dilated = np.where(seen > 0, np.log(np.maximum(seen, 1)), NEG)
    banded = np.where(n <= WIN, 0.0, NEG)
    return onehot, np.stack([banded] * 8 + [dilated] * 8).astype(np.float32)


def kernel(**inputs):
    import concourse.bacc as _bacc
    from concourse.bass_utils import run_bass_kernel_spmd as _run

    a = {k: np.asarray(v) for k, v in inputs.items()}
    onehot, addmask = distance_constants()
    cosines, sines, turn = rotary_constants()
    causal, pairs = mask_constants()
    ring_chunks, head_chunks = layout_second(a)
    arrays = {
        "xT": a["x"][0].T.reshape(KD, P, S).transpose(1, 0, 2),
        "pT": a["p"][0, 0].T.reshape(2, P, S).transpose(1, 0, 2),
        "metaT": a["meta_2"].T.reshape(KD, P, META).transpose(1, 0, 2),
        "w": np.stack(layout_first(a) + ring_chunks),
        "w_mla": np.stack(head_chunks),
        "vec1": np.concatenate([columns(v) for v in (
            a["g_pre_mix"][0], np.concatenate([a["g_out_a"][0], a["g_out_b"][0]]), a["g_post_mix"][0],
            a["g_pre_mlp"][0], a["g_post_mlp"][0], a["b_ple_gate"][0], a["g_post_ple"][0])], axis=1),
        "vec2": vectors_second(a),
        "table": a["rel_bias_table"],
        "onehot": onehot,
        "addmask": addmask,
        "sink": a["sink_a"],
        "cosines": cosines,
        "sines": sines,
        "turn": turn,
        "causal": causal,
        "pairs": pairs,
    }
    nc = _bacc.Bacc("TRN2", target_bir_lowering=False, num_devices=1)
    args = []
    for name, v in arrays.items():
        arrays[name] = np.ascontiguousarray(v)
        args.append(nc.dram_tensor(name, v.shape, F32, kind="ExternalInput").ap())
    out = nc.dram_tensor("out", (P, KD, S), F32, kind="ExternalOutput").ap()
    program(nc, *args, out)
    r = _run(nc, [arrays], core_ids=[0])
    got = r.results[0]["out"]
    return got.transpose(1, 0, 2).reshape(1, D, S).transpose(0, 2, 1)
```

```python
from contextlib import ExitStack, contextmanager

import numpy as np
import concourse.bass as bass
from concourse import mybir

F32 = mybir.dt.float32
F32R = mybir.dt.float32r
U8 = mybir.dt.uint8
ACT = mybir.ActivationFunctionType
ALU = mybir.AluOpType
AX = mybir.AxisListType.X

P = 128
D = 1024
KD = D // P
S = 512
META = 16
T = S + META
EPS = 1e-6
NEG = -1e30
CH = 8 * P
STAGE = 2
RING = 2
AHEAD = 2

DH = 64
WIN = 128
DILATED = ((128, 1), (512, 4), (2048, 16))
QB = S // P
REL = 1024
BW = 896
FF_GROUPS = 4

V1 = {}
_at = 0
for _name, _n in (("g_pre_mix", 8), ("g_out", 8), ("g_post_mix", 8), ("g_pre_mlp", 8), ("g_post_mlp", 8),
                  ("b_gate", 8), ("g_post_ple", 8)):
    V1[_name] = _at
    _at += _n
V1_COLS = _at

ATT_CHUNKS = 4
N1_CHUNKS = 2 + 4 * ATT_CHUNKS + KD + 16 * FF_GROUPS + KD + 2


LAYERS = 2
TAPS = 31
CONV_TILES = 4
HEADS_G = 4
GCH = 128
CHUNKS_G = S // GCH
CLAMP = 1.0 - 1e-6
LEVELS = 7
QK = 96
NOPE = 64
ROPE = 32
QT = 5
V2 = {}
_at = 0
for _name, _n in (("norm1", 8), ("conv_w", TAPS * CONV_TILES), ("conv_b", 4), ("ln_g", 4), ("ln_b", 4), ("q_a", 2),
                  ("kv_a", 1), ("q_norm", 1), ("k_norm", 1), ("lb0", 4), ("lb1", 4), ("second", 1), ("hgrn_g", 4),
                  ("norm2", 8)):
    V2[_name] = _at
    _at += _n
V2_COLS = _at
N2_CHUNKS = 8 + 24 + 4 + 16 + 16 + 8 + 16 * FF_GROUPS


LOOPS = {
    "attention": {"bw_in": 64, "eT_ready0": 9, "eT_ready1": 9, "exp_ready": 4, "max_ready": 4, "o_done": 4,
        "o_free": 4, "qkv_ready": 4, "scores_done0": 6, "scores_done1": 5, "scores_done2": 5, "scores_free0": 6,
        "scores_free1": 5, "scores_free2": 5, "stage_full0": 32, "stage_full1": 32, "tr_done0": 9, "tr_done1": 9,
        "unit_done0": 2, "unit_done1": 2, "unit_free0": 2, "unit_free1": 2},
    "ff": {"hid_ready": 8, "stage_full0": 128, "stage_full1": 128, "unit_done0": 8, "unit_done1": 8, "unit_free0": 8,
        "unit_free1": 8, "w_split": 16},
    "conv": {"sig_ready": 2, "stage_full0": 32, "stage_full1": 32, "unit_done0": 2, "unit_done1": 2, "unit_free0": 2,
        "unit_free1": 2, "w_split": 4},
    "gates": {"stage_full0": 32, "stage_full1": 32, "unit_done0": 2, "unit_done1": 2, "unit_free0": 2,
        "unit_free1": 2, "w_split": 4},
    "recurrence": {"a_ready": 1, "f_sig": 1, "go_copied": 1, "go_done": 1, "gss_done": 1, "kft_done": 1,
        "kft_ready": 1, "level_ready": 7, "pair_done0": 4, "pair_done1": 4, "pair_free0": 4, "pair_free1": 4,
        "q_ready": 1, "rms_ready": 1, "sig_ready": 2, "stage_full0": 32, "stage_full1": 32, "state_ready": 1,
        "unit_done0": 2, "unit_done1": 2, "unit_free0": 2, "unit_free1": 2, "upd_done": 1, "v_ready": 1,
        "vtok_ready": 1, "vtr_done": 1},
    "mla": {"cT_ready0": 5, "cT_ready1": 5, "causal_done0": 6, "causal_done1": 6, "causal_free0": 6,
        "causal_free1": 6, "co_done": 2, "co_free": 2, "ctr_done0": 5, "ctr_done1": 5, "mlaw_in": 16, "mlaw_used": 1,
        "qexp_ready": 2, "qk_free": 2, "qk_raw": 4, "qk_ready": 2, "qmax_ready": 2, "rms_ready": 4, "unit_done0": 6,
        "unit_done1": 6, "unit_free0": 6, "unit_free1": 6, "vt_done": 1, "vt_ready": 1},
    "mix": {"stage_full0": 32, "stage_full1": 32, "unit_done0": 3, "unit_done1": 3, "unit_free0": 3, "unit_free1": 3},
    "ff2": {"hid_ready": 8, "stage_full0": 128, "stage_full1": 128, "unit_done0": 8, "unit_done1": 8,
        "unit_free0": 8, "unit_free1": 8, "w_split": 16},
    "layer": {"a_ready": 4, "cT_ready0": 22, "cT_ready1": 22, "c_ready": 1, "causal_done0": 24, "causal_done1": 24,
        "causal_free0": 24, "causal_free1": 24, "centred": 1, "co_done": 8, "co_free": 8, "conv_ready": 4,
        "ctr_done0": 22, "ctr_done1": 22, "f_sig": 4, "go_copied": 4, "go_done": 4, "gss_done": 4, "h_ready": 8,
        "hc_padded": 1, "hid_ready": 32, "kft_done": 4, "kft_ready": 4, "layer_begun": 1, "lb_exp_ready": 1,
        "lb_max_ready": 1, "lead_ready": 16, "level_ready": 28, "ln_ready": 1, "lnsig_ready": 1, "m_done": 1,
        "mean_ready": 1, "mlaw_in": 64, "mlaw_used": 5, "pair_done0": 16, "pair_done1": 16, "pair_free0": 16,
        "pair_free1": 16, "q_ready": 4, "qexp_ready": 8, "qk_free": 8, "qk_raw": 16, "qk_ready": 8, "qmax_ready": 8,
        "rms_ready": 25, "sig_ready": 12, "sq_ready": 23, "stage_full0": 1120, "stage_full1": 1120, "state_ready": 4,
        "u_ready": 24, "unit_done0": 101, "unit_done1": 101, "unit_free0": 101, "unit_free1": 101, "upd_done": 4,
        "v_ready": 4, "vt_done": 4, "vt_ready": 4, "vtok_ready": 4, "vtr_done": 4, "w_lead_ready": 108,
        "w_split": 108, "whole_ready": 16, "zb_ready": 1, "zc_ready": 1, "ztail_done": 1},
}


class Counts:

    def __init__(self, eng):
        self.eng, self.seen, self.loops = eng, {}, []

    def next(self, sem, by=1):
        self.seen[sem.name] = self.seen.get(sem.name, 0) + by
        return self.now(sem)

    def now(self, sem):
        value = self.seen.get(sem.name, 0)
        for reg, per in self.loops:
            if per.get(sem.name, 0):
                value = reg * per[sem.name] + value
        return value

    @contextmanager
    def loop(self, count, per):
        before = dict(self.seen)
        with self.eng.Fori(0, count) as reg:
            self.loops.append((reg, per))
            yield reg
            self.loops.pop()
        for name, value in self.seen.items():
            once, begun = value - before.get(name, 0), before.get(name, 0)
            assert once in (0, per.get(name, 0)), f"{name}: {once} an iteration, not {per.get(name, 0)}"
            self.seen[name] = begun + count * per.get(name, 0)


class Tokens:

    def __init__(self, start, count, parts):
        self.start, self.count, self.parts, self.width = start, count, parts, count // parts

    def of(self, x):
        return x[:, self.start:self.start + self.count].rearrange("p (h n) -> p h n", h=self.parts)

    def part(self, x, h):
        return x[:, self.start + h * self.width:self.start + (h + 1) * self.width]


def program(nc, xT, pT, metaT, w, w_mla, vec1, vec2, table, onehot, addmask, sink, cosines, sines, turn, causal, pairs, out):
    ctx = ExitStack()
    with ctx:
        def sb(name, shape, dt=F32):
            return ctx.enter_context(nc.sbuf_tensor(name, shape, dt))

        def sem(name):
            return ctx.enter_context(nc.semaphore(name))

        ps = ctx.enter_context(nc.psum_tensor("ps", [P, 8, 512], F32))
        slab_cols = 52800
        origin = (nc.sbuf_base + 31) // 32 * 32
        ctx.enter_context(nc.sbuf_tensor("slab", [P, slab_cols], F32))
        top = [0]

        def at(name, shape, col=None, dt=F32, rows=P):
            size = int(np.prod(shape))
            if col is None:
                col = top[0]
                top[0] += (size + 7) // 8 * 8
            assert 4 * (col + size) + 64 <= 4 * slab_cols, name
            return nc.alloc_sbuf_tensor_at(name, [rows, *shape], dt, offset=origin + 4 * col).ap()

        H = at("H", [KD, T])
        col_u, col_m, col_hid = (top[0] + i * KD * T for i in range(3))
        U = at("U", [KD, T])
        M = at("M", [KD, T])
        HID = at("HID", [KD, T])
        Uh, Ul2 = at("Uh", [KD, T], col_u, F32R), at("Ul2", [KD, T], col_m, F32R)
        Mh, Ml = at("Mh", [KD, T], col_m, F32R), at("Ml", [KD, T], col_u, F32R)
        HIDh = at("HIDh", [KD, T], col_hid, F32R)
        stage = at("stage", [STAGE, CH])
        wh = at("wh", [RING, CH], dt=F32R)
        wl = at("wl", [RING, CH], dt=F32R)
        rms = at("rms", [2, T])
        rstd = at("rstd", [T])
        relu = at("relu", [2, T])
        ones = at("ones", [P])
        ident = at("ident", [P])
        v1 = at("v1", [V1_COLS])
        v2all = at("v2all", [LAYERS, V2_COLS])
        v2 = at("v2", [V2_COLS])
        rotm = at("rotm", [QK], rows=QK)
        small = at("small", [192])
        smalls = [0]

        def few(*shape):
            size = int(np.prod(shape))
            view = small[:, smalls[0]:smalls[0] + size]
            smalls[0] += size
            assert smalls[0] <= 192
            return view if len(shape) == 1 else view.rearrange("p (a b) -> p a b", b=shape[1])

        ARENA = 25288
        col_arena = top[0]
        arena = at("arena", [ARENA])
        HIDl = at("HIDl", [KD, T], col_arena, F32R)
        Ul1 = at("Ul1", [KD, T], col_arena + KD * T, F32R)
        pth = at("pth", [2, S], col_arena + 2 * KD * T, F32R)
        ptl = at("ptl", [2, S], col_arena + 2 * KD * T + 2 * S, F32R)
        taken = [0]

        def carve(*shape, rows=P):
            size = int(np.prod(shape))
            view = arena[0:rows, taken[0]:taken[0] + size]
            taken[0] += size
            assert taken[0] <= ARENA, taken[0]
            return view if len(shape) == 1 else view.rearrange("p (a b) -> p a b", b=shape[1])

        ka = carve(S)
        vaT = carve(S)
        va = carve(QB, P)
        qa = carve(S)
        qb = carve(S)
        kb = carve(S)
        vbT = carve(S)
        vb = carve(QB, P)
        bw = carve(4, BW)
        ss = carve(2 * QB, S).rearrange("p (i b) s -> p i b s", i=2)
        eT = carve(2, 512)
        otok = carve(QB, D)
        tab = carve(16, rows=32)
        oneh = carve(REL, rows=32)
        addm = carve(REL, rows=16)
        brow = carve(REL, rows=16)
        pt = carve(2, S)
        nmax = few(2, 4)
        nms = few(2, 4)
        srel = few(2, 4)
        esink = few(2, 4)
        den = few(2, 4)
        den2 = few(2, 4)
        rinv = few(2, 4)
        sinks = few(8)
        nsinks = few(8)
        ss8 = few(8)
        rms8 = few(8)
        r8 = few(8)

        taken[0] = 0
        gates = carve(24, T)
        za = carve(4, T)
        zc = carve(4, T)
        hc = carve(CONV_TILES, TAPS - 1 + T)
        zb = arena[:, taken[0] - CONV_TILES * (TAPS - 1 + T):][:, 0:4 * T].rearrange("p (a b) -> p a b", b=T)
        mlaw = M[:, 6:8, :].rearrange("p k t -> p (k t)")[:, 0:CH]
        amat = carve(CHUNKS_G, GCH)
        atail = carve(META, rows=META)
        cq = carve(2, T)
        ckv = carve(T)
        kraw = carve(T)
        cosT = carve(T, rows=QK)
        sinT = carve(T, rows=QK)
        triT = carve(640)
        shared = taken[0]
        vtok = carve(CHUNKS_G + 1, GCH)
        kft = carve(CHUNKS_G, GCH)
        state = carve(CHUNKS_G + 1, GCH)
        taken[0] = shared
        vt = carve(QT, P)
        eT2 = carve(2, 512)
        pairf = U[:, :, :].rearrange("p k t -> p (k t)")[:, 0:(LEVELS + 1) * GCH]
        pairm = sb("pairm", [P, (LEVELS + 1) * GCH], U8)
        Ms = [M[:, k, :] for k in range(KD)]
        Hs = [HID[:, k, :] for k in range(KD)]
        Us = [U[:, k, :] for k in range(KD)]
        kk, pre, suf, qg_, vT, gs, oT, qfull = Ms
        kfull = Hs[0]
        lq = [Hs[1], Hs[2]]
        lk = [Hs[3], Hs[4]]
        gsq = Hs[7]
        qgain, kgain, rot1 = [u[0:QK] for u in Us[0:3]]
        qh_of, kh_of = [[u[0:QK] for u in Us[i:i + 2]] for i in (3, 5)]
        tails = [Ms[5], Us[7]]

        def exps_of(hd, i):
            return Hs[4 * hd + i] if i < QT - 1 else tails[hd][0:META]

        TRB = (7, 3)
        qsq, ksq = relu[0:QK, 0, :], relu[0:QK, 1, :]
        otok2 = M[:, :, :].rearrange("p k t -> p (k t)")[:, 0:QT * 512].rearrange("p (i c) -> p i c", i=QT)
        lb_max, lb_sum, oml = (few(4) for _ in range(3))
        lb_e = few(2, 4)
        rms_v, mu = Hs[7], relu[:, 1, :]
        qmax, qden, qinv = (few(2, QT) for _ in range(3))
        headcol = few(2)
        bias_dram = nc.dram_tensor("bias_rows", (16, REL), F32, kind="Internal").ap()
        bias_slide = bass.AP(tensor=bias_dram.tensor, offset=0, ap=[[REL, 16], [1, P], [1, BW]])

        stage_full = [sem(f"stage_full{j}") for j in range(STAGE)]
        stage_free = [sem(f"stage_free{j}") for j in range(STAGE)]
        w_lead_ready = sem("w_lead_ready")
        w_split = sem("w_split")
        whole_ready = sem("whole_ready")
        lead_ready = sem("lead_ready")
        vec_in = sem("vec_in")
        x_in = sem("x_in")
        bias_in = sem("bias_in")
        brow_ready = sem("brow_ready")
        brow_out = sem("brow_out")
        bw_in = sem("bw_in")
        bw_used = sem("bw_used")
        consts = sem("consts")
        unit_done = [sem(f"unit_done{b}") for b in range(2)]
        unit_free = [sem(f"unit_free{b}") for b in range(2)]
        sq_ready = sem("sq_ready")
        rms_ready = sem("rms_ready")
        u_ready = sem("u_ready")
        h_ready = sem("h_ready")
        m_ready = sem("m_ready")
        pt_lead = sem("pt_lead")
        pt_ready = sem("pt_ready")
        m_zero = sem("m_zero")
        hid_ready = sem("hid_ready")
        gate_ready = sem("gate_ready")
        qkv_ready = sem("qkv_ready")
        s_done = [sem(f"scores_done{b}") for b in range(3)]
        s_free = [sem(f"scores_free{b}") for b in range(3)]
        tr_done = [sem(f"tr_done{b}") for b in range(2)]
        eT_ready = [sem(f"eT_ready{b}") for b in range(2)]
        max_ready = sem("max_ready")
        exp_ready = sem("exp_ready")
        o_done = sem("o_done")
        o_free = sem("o_free")
        r8_ready = sem("r8_ready")
        osq_ready = sem("osq_ready")
        on_ready = sem("on_ready")
        oT_ready = [sem(f"oT_ready{b}") for b in range(2)]
        out_done = sem("out_done")
        consts2_in = sem("consts2_in")
        layer_begun = sem("layer_begun")
        hc_padded = sem("hc_padded")
        lb_max_ready = sem("lb_max_ready")
        lb_exp_ready = sem("lb_exp_ready")
        sig_ready = sem("sig_ready")
        conv_ready = sem("conv_ready")
        mean_ready = sem("mean_ready")
        centred = sem("centred")
        ln_ready = sem("ln_ready")
        lnsig_ready = sem("lnsig_ready")
        c_ready = sem("c_ready")
        f_sig = sem("f_sig")
        q_ready = sem("q_ready")
        v_ready = sem("v_ready")
        vtok_ready = sem("vtok_ready")
        level_ready = sem("level_ready")
        pair_done = [sem(f"pair_done{b}") for b in range(2)]
        pair_free = [sem(f"pair_free{b}") for b in range(2)]
        a_ready = sem("a_ready")
        kft_done = sem("kft_done")
        kft_ready = sem("kft_ready")
        upd_done = sem("upd_done")
        state_ready = sem("state_ready")
        go_done = sem("go_done")
        go_copied = sem("go_copied")
        gss_done = sem("gss_done")
        vtr_done = sem("vtr_done")
        zc_ready = sem("zc_ready")
        mlaw_in = sem("mlaw_in")
        mlaw_used = sem("mlaw_used")
        qk_raw = sem("qk_raw")
        qk_ready = sem("qk_ready")
        qk_free = sem("qk_free")
        vt_done = sem("vt_done")
        vt_ready = sem("vt_ready")
        c_done = [sem(f"causal_done{b}") for b in range(2)]
        c_free = [sem(f"causal_free{b}") for b in range(2)]
        qmax_ready = sem("qmax_ready")
        qexp_ready = sem("qexp_ready")
        ctr_done = [sem(f"ctr_done{b}") for b in range(2)]
        cT_ready = [sem(f"cT_ready{b}") for b in range(2)]
        co_done = sem("co_done")
        co_free = sem("co_free")
        ztail_done = sem("ztail_done")
        zb_ready = sem("zb_ready")
        m_done = sem("m_done")
        passed = sem("passed")

        T0 = Tokens(0, S, 1)
        T1 = Tokens(META, S, 1)

        def psum_of(b, tok, m=P):
            return ps[0:m, 2 * b:2 * b + tok.parts, 0:tok.width]

        T2 = Tokens(0, T, 2)
        ATT_PER, FF_PER, CONV_PER, GATE_PER, GREC_PER, MLA_PER, MIX_PER, FF2_PER, LAYER_PER = (LOOPS[x] for x in (
            "attention", "ff", "conv", "gates", "recurrence", "mla", "mix", "ff2", "layer"))

        def level_blocks(x, size, half):
            cols = T if 2 * size <= META else S
            return x[:, 0:cols].rearrange("p (n two b) -> p n two b", two=2, b=size)[:, :, half, :]

        def level_total(x, size, half):
            v = level_blocks(x, size, half)
            return v[:, :, size - 1:size].to_broadcast([P, v.shape[1], size])

        HEADS = ((True, 0), (True, 1), (False, 0), (False, 1))

        def key_blocks(banded, b):
            return range(max(0, b - 1), min(QB, b + 2)) if banded else range(QB)

        def copy_causal_tile(eng, n, i):
            tb = 0 if eng.engine == nc.scalar.engine else 1
            rows = P if i < QT - 1 else META
            eng.wait_ge(ctr_done[tb], n.next(ctr_done[tb]))
            whole = min(i + 1, QT - 1)
            last = None
            for keys, c0, c1 in ((P, 0, whole * rows),) + (((META, whole * rows, (whole + 1) * rows),) if i == QT - 1 else ()):
                dst, src = eT2[0:keys, tb, c0:c1], ps[0:keys, TRB[tb], c0:c1]
                last = eng.activation(dst, src, ACT.Copy) if tb == 0 else eng.tensor_copy(dst, src)
            last.then_inc(cT_ready[tb], 1)

        block = ctx.enter_context(nc.Block())

        @block.sync
        def _(sp):
            for j in range(STAGE):
                sp.dma_start(stage[:, j, :], w[j]).then_inc(stage_full[j], 16)
            with sp.Fori(1, (N1_CHUNKS + LAYERS * N2_CHUNKS + AHEAD) // STAGE) as i:
                for j in range(STAGE):
                    sp.wait_ge(stage_free[j], i)
                    sp.dma_start(stage[:, j, :], w[bass.ds(STAGE * i + j, 1)].rearrange("o p n -> p (o n)")).then_inc(stage_full[j], 16)

        @block.gpsimd
        def _(pool):
            pool.memset(ones[:, :], 1.0)
            pool.memset(ident[:, :], 0.0)
            pool.drain()
            pool.affine_select(out=ident[:, :], in_=ident[:, :], compare_op=ALU.not_equal, fill=1.0, base=0,
                               pattern=[[-1, P]], channel_multiplier=1)
            pool.drain().then_inc(consts, 1)
            n = Counts(pool)
            pool.wait_ge(brow_ready, 1)
            pool.dma_start(bias_dram, brow[:, :]).then_inc(brow_out, 16)
            pool.wait_ge(brow_out, 16)
            with n.loop(4, {"bw_used": 1}) as t:
                pool.wait_ge(bw_used, n.next(bw_used))
                for j, row in enumerate((t, t + 4, 2 * t + 8, 2 * t + 9)):
                    pool.dma_start(bw[:, j, :], bias_slide[bass.ds(row, 1)].rearrange("o p c -> p (o c)")).then_inc(bw_in, 16)

            def rest_of_weights(count):
                with n.loop(count // 2, {w_lead_ready.name: 2}):
                    for j in range(2):
                        pool.wait_ge(w_lead_ready, n.next(w_lead_ready))
                        pool.tensor_tensor(wl[:, j, :], stage[:, j, :], wh[:, j, :].bitcast(F32), ALU.subtract).then_inc(w_split, 1)
                        pool.drain().then_inc(stage_free[j], 1)

            rest_of_weights(KD + AHEAD)
            pool.wait_ge(h_ready, KD)
            pool.memset(M[:, :, META:], 0.0).then_inc(m_zero, 1)
            rest_of_weights(16 * FF_GROUPS + KD + 2)
            pool.wait_ge(h_ready, 3 * KD)
            pool.memset(amat, 0.0)
            pool.memset(atail, 0.0)
            pool.drain().then_inc(consts, 1)
            for dst, src in ((cosT, cosines), (sinT, sines), (triT, causal), (rotm[:, :], turn), (pairf, pairs),
                             (v2all[:, :, :], vec2)):
                pool.dma_start(dst, src).then_inc(consts2_in, 16)
            with n.loop(LAYERS, LAYER_PER) as layer:
                pool.wait_ge(layer_begun, n.next(layer_begun))
                pool.sem_inc(passed, 1)
                pool.memset(hc[:, :, 0:TAPS - 1], 0.0).then_inc(hc_padded, 1)
                rest_of_weights(8 + 24 + 4 - AHEAD)
                with n.loop(4, MLA_PER) as pair:
                    pool.wait_ge(mlaw_used, n.next(mlaw_used))
                    pool.dma_start(mlaw, w_mla[bass.ds(layer * 4 + pair, 1)].rearrange("o p c -> p (o c)")).then_inc(mlaw_in, 16)
                pool.wait_ge(mlaw_used, n.next(mlaw_used))
                pool.sem_inc(passed, 1)
                rest_of_weights(KD + 16 * FF_GROUPS + AHEAD)

        @block.tensor
        def _(pe):
            n = Counts(pe)
            at = {"chunk": 0, "unit": 0}

            def chunk():
                slot = at["chunk"] % STAGE
                at["chunk"] += 1
                pe.wait_ge(stage_full[slot], n.next(stage_full[slot], 16))
                return [stage[:, slot, j * P:(j + 1) * P] for j in range(8)]

            def split_chunk():
                slot = at["chunk"] % STAGE
                at["chunk"] += 1
                n.next(stage_full[slot], 16)
                pe.wait_ge(w_split, n.next(w_split))
                return [[half[:, slot, j * P:(j + 1) * P] for half in (wh, wl)] for j in range(8)]

            def unit(weights, acts, tok, m=P, ready=None, frees=None):
                b = at["unit"] % 2
                at["unit"] += 1
                pe.wait_ge(unit_free[b], n.next(unit_free[b]))
                for k, (wt, a) in enumerate(zip(weights, acts)):
                    if ready is not None:
                        pe.wait_ge(ready, n.next(ready))
                    for h in range(tok.parts):
                        mm = pe.matmul(ps[0:m, 2 * b + h, 0:tok.width], wt, tok.part(a, h),
                                       start=(k == 0), stop=(k == len(acts) - 1))
                        if frees is not None and k == 0 and h == 0:
                            mm.then_inc(frees, 1)
                mm.then_inc(unit_done[b], 1)

            def split_unit(weights, acts, tok, ready=None):
                b = at["unit"] % 2
                at["unit"] += 1
                pe.wait_ge(unit_free[b], n.next(unit_free[b]))
                for k, ((w_lead, w_rest), (a_lead, a_rest)) in enumerate(zip(weights, acts)):
                    if ready is not None:
                        pe.wait_ge(ready, n.next(ready))
                    for h in range(tok.parts):
                        dst = ps[:, 2 * b + h, 0:tok.width]
                        pe.matmul(dst, w_lead, tok.part(a_lead, h), start=(k == 0), stop=False)
                        pe.matmul(dst, w_lead, tok.part(a_rest, h), start=False, stop=False)
                        mm = pe.matmul(dst, w_rest, tok.part(a_lead, h), start=False, stop=(k == len(acts) - 1))
                mm.then_inc(unit_done[b], 1)

            def project(acts, tok, count, ready=None):
                for m in range(count):
                    frees = stage_free[(at["chunk"] - 1) % STAGE] if m > 0 else None
                    unit(chunk(), acts, tok, ready=ready if m == 0 else None, frees=frees)
                pe.drain().then_inc(stage_free[(at["chunk"] - 1) % STAGE], 1)

            def split_project(acts, tok, count, ready=None):
                for m in range(count):
                    split_unit(split_chunk(), acts, tok, ready=ready if m == 0 else None)

            def sum_squares(tok, count=KD):
                unit([ones[:, :]] * count, [HID[:, k, :] for k in range(count)], tok, ready=sq_ready)

            Uk = [U[:, k, :] for k in range(KD)]
            U1k = [(Uh[:, k, :], Ul1[:, k, :]) for k in range(KD)]
            U2k = [(Uh[:, k, :], Ul2[:, k, :]) for k in range(KD)]
            HIDk = [(HIDh[:, k, :], HIDl[:, k, :]) for k in range(KD)]
            pe.wait_ge(consts, 1)
            pe.wait_ge(bias_in, 48)
            for h in range(2):
                b = at["unit"] % 2
                at["unit"] += 1
                pe.wait_ge(unit_free[b], n.next(unit_free[b]))
                pe.matmul(ps[0:16, 2 * b, 0:512], tab[:, :], oneh[:, h * 512:(h + 1) * 512],
                          start=True, stop=True).then_inc(unit_done[b], 1)

            sum_squares(T1)
            project(Uk, T1, 1, ready=u_ready)
            project(Uk, T1, 1)
            tr = [0]

            def transposed(b, blocks):
                for j, src in enumerate(blocks):
                    mm = pe.transpose(ps[0:src.shape[-1], 1 + 2 * b, j * P:j * P + src.shape[0]], src, ident[0:src.shape[0], 0:src.shape[0]])
                mm.then_inc(tr_done[b], 1)

            def transpose_values(src):
                for b in range(2):
                    transposed(b, [src[:, (2 * b + j) * P:(2 * b + j + 1) * P] for j in range(2)])
                for b in range(2):
                    pe.wait_ge(eT_ready[b], n.next(eT_ready[b]))

            pe.wait_ge(qkv_ready, n.next(qkv_ready, 2))
            transpose_values(vaT)
            assert at["unit"] % 2 == 1

            def scores(hd):
                banded, half = HEADS[hd]
                q, k = (qa, ka) if banded else (qb, kb)
                rows = slice(64 * half, 64 * half + 64)
                for b in range(QB):
                    u = (hd * QB + b) % 3
                    keys = key_blocks(banded, b)
                    pe.wait_ge(s_free[u], n.next(s_free[u]))
                    pe.matmul(ps[:, 4 + u, 0:len(keys) * P], q[rows, b * P:(b + 1) * P],
                              k[rows, keys[0] * P:(keys[-1] + 1) * P], start=True, stop=True).then_inc(s_done[u], 1)

            def transpose_exps(hd, b):
                keys = key_blocks(HEADS[hd][0], b)
                transposed(b % 2, [ss[:, hd % 2, b, j * P:(j + 1) * P] for j in range(len(keys))])

            def weigh(hd, b):
                banded, half = HEADS[hd]
                v = va if banded else vb
                keys = key_blocks(banded, b)
                pe.wait_ge(eT_ready[b % 2], n.next(eT_ready[b % 2]))
                for j, kblock in enumerate(keys):
                    mm = pe.matmul(ps[:, 7, b * DH:(b + 1) * DH], eT[:, b % 2, j * P:(j + 1) * P],
                                   v[:, kblock, 64 * half:64 * half + 64], start=(j == 0), stop=(j == len(keys) - 1))
                return mm

            def attend(hd):
                pe.wait_ge(exp_ready, n.next(exp_ready))
                transpose_exps(hd, 0)
                pe.wait_ge(o_free, n.next(o_free))
                for b in range(QB):
                    if b + 1 < QB:
                        transpose_exps(hd, b + 1)
                    mm = weigh(hd, b)
                mm.then_inc(o_done, 1)

            with n.loop(4, ATT_PER) as t:
                project(Uk, T1, 4)
                pe.wait_ge(qkv_ready, n.next(qkv_ready, 4))
                transpose_values(vbT)
                scores(0)
                scores(1)
                attend(0)
                scores(2)
                attend(1)
                scores(3)
                attend(2)
                attend(3)

            pe.wait_ge(on_ready, n.next(on_ready))
            for f in range(KD):
                if f >= 2:
                    pe.wait_ge(oT_ready[f % 2], n.next(oT_ready[f % 2]))
                transposed(f % 2, [otok[:, b, f * P:(f + 1) * P] for b in range(QB)])
            split_project(U1k, T1, KD, ready=u_ready)
            sum_squares(T1)

            sum_squares(T1)
            first = True
            pe.wait_ge(u_ready, n.next(u_ready, KD))
            with n.loop(FF_GROUPS, FF_PER):
                split_project(U1k, T1, KD)
                split_project(HIDk, T1, KD, ready=hid_ready)
            sum_squares(T1)

            split_project(U1k, T1, KD, ready=u_ready)
            pe.wait_ge(pt_ready, 1)
            for m in range(KD):
                if m % 4 == 0:
                    tiles = split_chunk()
                split_unit(tiles[2 * (m % 4):2 * (m % 4) + 2], [(pth[:, k, :], ptl[:, k, :]) for k in range(2)], T0)
            sum_squares(T1)

            ZA, ZB, ZC = ([z[:, k, :] for k in range(4)] for z in (za, zb, zc))

            def pair_products(level):
                b = level % 2
                lhs, rhs = (kk, qg_) if level == 0 else (lk[level % 2], lq[level % 2])
                pe.wait_ge(pair_free[b], n.next(pair_free[b]))
                if level <= 4:
                    pe.matmul(ps[0:META, 6, level * META:(level + 1) * META], lhs[:, S:T], rhs[:, S:T], start=True, stop=True)
                for c in range(CHUNKS_G):
                    mm = pe.matmul(ps[:, 4 + b, c * GCH:(c + 1) * GCH], lhs[:, c * GCH:(c + 1) * GCH],
                                   rhs[:, c * GCH:(c + 1) * GCH], start=True, stop=True)
                mm.then_inc(pair_done[b], 1)

            pe.wait_ge(consts, 2)
            pe.wait_ge(consts2_in, 16 * 6)
            with n.loop(LAYERS, LAYER_PER) as layer:
                sum_squares(T2)
                pe.wait_ge(u_ready, n.next(u_ready, KD))
                pe.sem_inc(passed, 1)
                with n.loop(2, CONV_PER):
                    split_project(U2k, T2, 4)
                with n.loop(6, GATE_PER):
                    split_project(U2k, T2, 4)
                split_project(U2k, T2, 4)
                unit([ones[:, :]] * 4, ZA, T2, ready=conv_ready)
                sum_squares(T2, 4)
                unit([ones[:, :]] * 2, [Hs[4], Hs[5]], T2, ready=sq_ready)
                unit([ones[:, :]], [Hs[6]], T2, ready=sq_ready)
                pe.wait_ge(u_ready, n.next(u_ready, KD))
                pe.sem_inc(passed, 1)
                with n.loop(HEADS_G, GREC_PER):
                    project(Uk, T2, 4)
                    pe.wait_ge(v_ready, n.next(v_ready))
                    for c in range(CHUNKS_G):
                        pe.transpose(ps[:, 7, c * GCH:(c + 1) * GCH], vT[:, c * GCH:(c + 1) * GCH], ident[:, :])
                    pe.transpose(ps[0:META, 6, 2 * P:3 * P], vT[:, S:T], ident[:, :]).then_inc(vtr_done, 1)
                    pe.wait_ge(vtok_ready, n.next(vtok_ready))
                    pair_products(0)
                    for level in range(1, LEVELS + 1):
                        pe.wait_ge(level_ready, n.next(level_ready))
                        pair_products(level)
                    pe.wait_ge(a_ready, n.next(a_ready))
                    for c in range(CHUNKS_G):
                        mm = pe.transpose(ps[:, 7, c * GCH:(c + 1) * GCH], kfull[:, c * GCH:(c + 1) * GCH], ident[:, :])
                    mm.then_inc(kft_done, 1)
                    pe.wait_ge(kft_ready, n.next(kft_ready))
                    for c in range(CHUNKS_G):
                        mm = pe.matmul(ps[:, 6, c * GCH:(c + 1) * GCH], kft[:, c, :], vtok[:, c, :], start=True, stop=True)
                    mm.then_inc(upd_done, 1)
                    pe.wait_ge(state_ready, n.next(state_ready))
                    for c in range(CHUNKS_G + 1):
                        rows, cols = (GCH, slice(c * GCH, (c + 1) * GCH)) if c < CHUNKS_G else (META, slice(S, T))
                        dst = ps[:, 4, cols] if c < CHUNKS_G else ps[:, 5, 0:META]
                        inner = amat[:, c, :] if c < CHUNKS_G else atail
                        mm = pe.matmul(dst, vtok[0:rows, c, :], inner, start=True, stop=(c == 0))
                        if c > 0:
                            mm = pe.matmul(dst, state[:, c, :], qfull[:, cols], start=False, stop=True)
                    mm.then_inc(go_done, 1)
                    pe.wait_ge(go_copied, n.next(go_copied))
                    for h in range(2):
                        mm = pe.matmul(ps[:, 6 + h, 0:T2.width], ones[:, :], T2.part(gsq, h), start=True, stop=True)
                    mm.then_inc(gss_done, 1)

                def causal_scores(hd):
                    for i in range(QT - 1):
                        b = i % 2
                        pe.wait_ge(c_free[b], n.next(c_free[b]))
                        pe.matmul(ps[:, 4 + b, 0:(i + 1) * P], qh_of[hd][:, i * P:(i + 1) * P],
                                  kh_of[hd][:, 0:(i + 1) * P], start=True, stop=True).then_inc(c_done[b], 1)
                    for b in range(2):
                        pe.wait_ge(c_free[b], n.next(c_free[b]))
                        pe.matmul(ps[0:META, 4 + b, 0:T2.width], qh_of[hd][:, S:T], T2.part(kh_of[hd], b),
                                  start=True, stop=True).then_inc(c_done[b], 1)

                def causal_transpose(hd, i):
                    tb = (hd * QT + i) % 2
                    rows = P if i < QT - 1 else META
                    e = exps_of(hd, i)
                    for j in range(i + 1):
                        keys = P if j < QT - 1 else META
                        mm = pe.transpose(ps[0:keys, TRB[tb], j * rows:(j + 1) * rows], e[:, j * P:j * P + keys], ident[0:rows, 0:rows])
                    mm.then_inc(ctr_done[tb], 1)

                def causal_weigh(hd, i):
                    tb = (hd * QT + i) % 2
                    rows = P if i < QT - 1 else META
                    pe.wait_ge(cT_ready[tb], n.next(cT_ready[tb]))
                    for j in range(i + 1):
                        keys = P if j < QT - 1 else META
                        mm = pe.matmul(ps[0:rows, 6, i * DH:(i + 1) * DH], eT2[0:keys, tb, j * rows:(j + 1) * rows],
                                       vt[0:keys, j, hd * DH:(hd + 1) * DH], start=(j == 0), stop=(j == i))
                    return mm

                pe.wait_ge(c_ready, n.next(c_ready))
                pe.wait_ge(zc_ready, n.next(zc_ready))
                pe.sem_inc(passed, 1)
                with n.loop(4, MLA_PER):
                    pe.wait_ge(mlaw_in, n.next(mlaw_in, 16))
                    tile = [mlaw[:, j * P:(j + 1) * P] for j in range(8)]
                    pe.wait_ge(co_free, n.now(co_free) + 1)
                    for j in range(QT):
                        rows = P if j < QT - 1 else META
                        dst = ps[0:rows, 7, j * P:(j + 1) * P] if j < QT - 1 else ps[0:rows, 6, 384:512]
                        mm = pe.matmul(dst, ckv[:, j * P:j * P + rows], tile[6], start=True, stop=True)
                    mm.then_inc(vt_done, 1)
                    for hd in range(2):
                        unit([tile[3 * hd][:, 0:QK], tile[3 * hd + 1][:, 0:QK]], [cq[:, 0, :], cq[:, 1, :]], T2, m=QK)
                        unit([tile[3 * hd + 2][:, 0:NOPE]], [ckv], T2, m=NOPE)
                        unit([ones[0:QK, 0:QK]], [qsq], T2, m=QK, ready=qk_raw)
                        unit([rotm[:, :]], [qgain], T2, m=QK)
                        unit([ones[0:QK, 0:QK]], [ksq], T2, m=QK, ready=qk_raw)
                        unit([rotm[:, :]], [kgain], T2, m=QK)
                    pe.drain().then_inc(mlaw_used, 1)
                    pe.wait_ge(vt_ready, n.next(vt_ready))
                    pe.wait_ge(qk_ready, n.next(qk_ready, 2))
                    causal_scores(0)
                    causal_scores(1)
                    pe.wait_ge(unit_free[1], n.now(unit_free[1]) + 1)
                    for hd in range(2):
                        pe.wait_ge(qexp_ready, n.next(qexp_ready))
                        causal_transpose(hd, 0)
                        pe.wait_ge(co_free, n.next(co_free))
                        for i in range(QT):
                            if i + 1 < QT:
                                causal_transpose(hd, i + 1)
                            mm = causal_weigh(hd, i)
                        mm.then_inc(co_done, 1)

                pe.wait_ge(co_free, n.now(co_free) + 1)
                for f in range(4):
                    tb = f % 2
                    if f >= 2:
                        pe.wait_ge(cT_ready[tb], n.next(cT_ready[tb]))
                    for j in range(QT - 1):
                        mm = pe.transpose(ps[:, TRB[tb], j * P:(j + 1) * P], otok2[:, j, f * P:(f + 1) * P], ident[:, :])
                    mm.then_inc(ctr_done[tb], 1)
                    mm = pe.transpose(ps[:, 6, f * META:(f + 1) * META], otok2[0:META, QT - 1, f * P:(f + 1) * P], ident[0:META, 0:META])
                mm.then_inc(ztail_done, 1)
                for tb in range(2):
                    pe.wait_ge(cT_ready[tb], n.next(cT_ready[tb]))
                pe.wait_ge(zb_ready, n.next(zb_ready))
                pe.sem_inc(passed, 1)
                with n.loop(4, MIX_PER):
                    for j in range(2):
                        tiles = chunk()
                        unit(tiles[0:4], ZA, T2, frees=stage_free[1] if j > 0 else None)
                        unit(tiles[4:8], ZB, T2)
                        tiles = chunk()
                        unit(tiles[0:4], ZC, T2, frees=stage_free[0])
                    pe.drain().then_inc(stage_free[1], 1)
                pe.wait_ge(m_done, n.next(m_done, 1))
                split_project([(Mh[:, k, :], Ml[:, k, :]) for k in range(KD)], T2, KD)
                sum_squares(T2)
                pe.wait_ge(u_ready, n.next(u_ready, KD))
                pe.sem_inc(passed, 1)
                with n.loop(FF_GROUPS, FF2_PER):
                    split_project(U2k, T2, KD)
                    split_project(HIDk, T2, KD, ready=hid_ready)

        @block.scalar
        def _(act):
            n = Counts(act)
            at = {"unit": 0, "chunk": 0}

            def take():
                b = at["unit"] % 2
                at["unit"] += 1
                return b, n.next(unit_done[b])

            def pass_chunks(count):
                for _ in range(count):
                    n.next(stage_full[at["chunk"] % STAGE], 16)
                    at["chunk"] += 1

            def split_weights():
                slot = at["chunk"] % STAGE
                at["chunk"] += 1
                act.wait_ge(stage_full[slot], n.next(stage_full[slot], 16))
                act.activation(wh[:, slot, :], stage[:, slot, :], ACT.Copy).then_inc(w_lead_ready, 1)

            def used_up(split=True):
                b, done = take()
                act.wait_ge(unit_done[b], done)
                if split:
                    split_weights()
                return b

            def split_inputs(src, tok):
                for k in range(KD):
                    act.wait_ge(whole_ready, n.next(whole_ready))
                    act.activation(tok.of(Uh[:, k, :]), tok.of(src[:, k, :]), ACT.Copy).then_inc(lead_ready, 1)

            act.dma_start(v1[:, :], vec1).then_inc(vec_in, 16)
            act.dma_start(sinks[:, :], sink.to_broadcast([P, 8])).then_inc(vec_in, 16)
            act.dma_start(tab[:, :], table).then_inc(bias_in, 16)
            act.dma_start(oneh[:, :], onehot).then_inc(bias_in, 16)
            act.dma_start(addm[:, :], addmask).then_inc(bias_in, 16)
            act.dma_start(H[:, :, META:], xT).then_inc(x_in, 16)
            act.dma_start(H[:, :, 0:META], metaT).then_inc(x_in, 16)
            act.dma_start(pt[:, :, :], pT).then_inc(x_in, 16)

            def root_mean(tok, count, dst=rms[:, 0, :], m=P):
                b, done = take()
                act.wait_ge(unit_done[b], done)
                act.activation(tok.of(dst[0:m]), psum_of(b, tok, m), ACT.Sqrt, bias=EPS, scale=1.0 / count).then_inc(unit_free[b], 1)
                act.drain().then_inc(rms_ready, 1)

            def squares(src, tok, ready=None, free=None):
                for k in range(KD):
                    if ready is not None:
                        act.wait_ge(ready, n.next(ready))
                    act.activation(tok.of(HID[:, k, :]), tok.of(src[:, k, :]), ACT.Square).then_inc(sq_ready, 1)

            act.wait_ge(x_in, 48)
            take()
            take()
            squares(H, T1)
            root_mean(T1, D)

            def evacuate(dst, tok, func=ACT.Copy, bias=0.0, flip=False, ready=None, split=False):
                b = used_up(split)
                src = psum_of(b, tok)
                if flip:
                    src = ps[:, 2 * b, :].rearrange("p (b q) -> p b q", q=P)[:, :, ::-1]
                    dst = dst.rearrange("p (b q) -> p b q", q=P)
                else:
                    dst = tok.of(dst)
                act.activation(dst, src, func, bias=bias).then_inc(unit_free[b], 1)
                if ready is not None:
                    act.drain().then_inc(ready, 1)

            pass_chunks(2)
            evacuate(ka, T0, ready=qkv_ready)
            evacuate(vaT, T0, ready=qkv_ready)

            def copy_values(dst):
                act.wait_ge(tr_done[0], n.next(tr_done[0]))
                act.activation(dst[:, 0:2, :], ps[:, 1, 0:2 * P].rearrange("p (j d) -> p j d", d=P), ACT.Copy).then_inc(eT_ready[0], 1)

            copy_values(va)

            def exps(hd):
                banded, half = HEADS[hd]
                act.wait_ge(max_ready, n.next(max_ready))
                for b in range(QB):
                    e = ss[:, hd % 2, b, 0:len(key_blocks(banded, b)) * P]
                    act.activation(e, e, ACT.Exp, bias=(nms if banded else nmax)[:, hd % 2, b:b + 1],
                                   accum_out=den[:, hd % 2, b:b + 1])
                if banded:
                    act.activation(esink[:, hd % 2, :], srel[:, hd % 2, :], ACT.Exp)
                act.drain().then_inc(exp_ready, 1)

            def copy_exps(hd):
                for b in (0, 2):
                    act.wait_ge(tr_done[0], n.next(tr_done[0]))
                    wd = len(key_blocks(HEADS[hd][0], b)) * P
                    act.activation(eT[:, 0, 0:wd], ps[:, 1, 0:wd], ACT.Copy).then_inc(eT_ready[0], 1)

            with n.loop(4, ATT_PER) as t:
                pass_chunks(4)
                evacuate(qa, T0, flip=True, ready=qkv_ready)
                evacuate(qb, T0, flip=True, ready=qkv_ready)
                evacuate(kb, T0, ready=qkv_ready)
                evacuate(vbT, T0, ready=qkv_ready)
                copy_values(vb)
                exps(0)
                exps(1)
                copy_exps(0)
                exps(2)
                copy_exps(1)
                exps(3)
                copy_exps(2)
                copy_exps(3)

            act.wait_ge(o_free, 1 + 16)
            for b in range(QB):
                for half in range(2):
                    act.activation(ss[:, half, b, :], otok[:, b, half * 512:(half + 1) * 512], ACT.Square,
                                   accum_out=ss8[:, 2 * b + half:2 * b + half + 1])
            act.drain()
            act.activation(rms8[:, :], ss8[:, :], ACT.Sqrt, bias=EPS, scale=1.0 / 512)
            act.drain().then_inc(osq_ready, 1)
            for _ in range(AHEAD):
                split_weights()
            for f in range(KD):
                if f % 2 == 0:
                    act.wait_ge(tr_done[0], n.next(tr_done[0]))
                    act.activation(HID[:, f, META:].rearrange("p (b q) -> p b q", q=P),
                                   ps[:, 1, :].rearrange("p (b q) -> p b q", q=P)[:, :, ::-1], ACT.Copy,
                                   scale=v1[:, V1["g_out"] + f:V1["g_out"] + f + 1]).then_inc(oT_ready[0], 1)
                    act.drain()
                else:
                    act.wait_ge(whole_ready, n.next(whole_ready))
                act.activation(T1.of(Uh[:, f, :]), T1.of(HID[:, f, :]), ACT.Copy).then_inc(lead_ready, 1)

            def out_and_squares(tok):
                for m in range(KD):
                    b = used_up()
                    act.activation(tok.of(M[:, m, :]), psum_of(b, tok), ACT.Copy)
                    act.activation(tok.of(HID[:, m, :]), psum_of(b, tok), ACT.Square).then_inc(unit_free[b], 1)
                    act.drain().then_inc(sq_ready, 1)

            out_and_squares(T1)
            root_mean(T1, D)
            squares(H, T1, ready=h_ready)
            root_mean(T1, D)
            split_inputs(HID, T1)
            with n.loop(FF_GROUPS, FF_PER):
                for m in range(KD):
                    used_up()
                for m in range(KD):
                    used_up()
            for k in range(2):
                act.activation(pth[:, k, :], pt[:, k, :], ACT.Copy)
            act.drain().then_inc(pt_lead, 1)
            squares(M, T1, ready=m_ready)
            root_mean(T1, D)
            split_inputs(H, T1)
            for m in range(KD):
                b = used_up()
                act.activation(T1.of(HID[:, m, :]), psum_of(b, T1), ACT.Sigmoid,
                               bias=v1[:, V1["b_gate"] + m:V1["b_gate"] + m + 1]).then_inc(unit_free[b], 1)
                act.drain().then_inc(gate_ready, 1)
            for m in range(KD):
                used_up(m % 4 == 3)
            squares(M, T1, ready=m_ready)
            root_mean(T1, D)
            n.next(h_ready, 2 * KD)

            with n.loop(LAYERS, LAYER_PER) as layer:
                act.wait_ge(layer_begun, n.next(layer_begun))
                act.wait_ge(lb_max_ready, n.next(lb_max_ready))
                act.activation(lb_e, lb_e, ACT.Exp).then_inc(lb_exp_ready, 1)
                squares(H, T2)
                root_mean(T2, D)
                split_inputs(HID, T2)
                with n.loop(2, CONV_PER):
                    for j in range(2):
                        evacuate(relu[:, j, :], T2, func=ACT.Sigmoid, ready=sig_ready, split=True)
                        used_up()
                with n.loop(6, GATE_PER) as g:
                    for j in range(4):
                        b = used_up()
                        act.activation(gates[:, bass.ds(4 * g + j, 1), :].rearrange("p o (h n) -> p (o h) n", h=2),
                                       psum_of(b, T2), ACT.Sigmoid).then_inc(unit_free[b], 1)
                for i, (dst, rows) in enumerate(((cq[:, 0, :], slice(0, P)), (cq[:, 1, :], slice(0, P)),
                                                 (ckv, slice(0, P)), (kraw, slice(NOPE, QK)))):
                    b = used_up(i < 4 - AHEAD)
                    act.activation(T2.of(dst[rows]), ps[rows, 2 * b:2 * b + 2, 0:T2.width], ACT.Copy).then_inc(unit_free[b], 1)
                b = used_up(False)
                act.activation(T2.of(mu), psum_of(b, T2), ACT.Copy, scale=1.0 / 512).then_inc(unit_free[b], 1)
                act.drain().then_inc(mean_ready, 1)
                act.wait_ge(centred, n.next(centred))
                for src, dst in ((za[:, 0, :], 0), (za[:, 1, :], 1), (za[:, 2, :], 2), (za[:, 3, :], 3),
                                 (cq[:, 0, :], 4), (cq[:, 1, :], 5), (ckv, 6)):
                    act.activation(Hs[dst], src, ACT.Square).then_inc(sq_ready, 1)
                root_mean(T2, 512)
                root_mean(T2, 256, dst=rms[:, 1, :])
                root_mean(T2, P, dst=rms_v)
                act.wait_ge(ln_ready, n.next(ln_ready))
                for k in range(4):
                    act.activation(Hs[k], za[:, k, :], ACT.Sigmoid, bias=v2[:, V2["ln_b"] + k:V2["ln_b"] + k + 1])
                act.drain().then_inc(lnsig_ready, 1)

                with n.loop(HEADS_G, GREC_PER):
                    pass_chunks(4)
                    b, done = take()
                    act.wait_ge(unit_done[b], done)
                    act.activation(T2.of(relu[:, 0, :]), psum_of(b, T2), ACT.Sigmoid, scale=-1.0).then_inc(unit_free[b], 1)
                    act.drain().then_inc(f_sig, 1)
                    evacuate(qg_, T2, ready=q_ready)
                    for dst in (Hs[6], Hs[5]):
                        b, done = take()
                        act.wait_ge(unit_done[b], done)
                        act.activation(T2.of(dst), psum_of(b, T2), ACT.Sigmoid)
                        act.drain().then_inc(sig_ready, 1)
                    act.wait_ge(vtr_done, n.next(vtr_done))
                    act.activation(vtok[:, 0:CHUNKS_G, :], ps[:, 7, :].rearrange("p (c d) -> p c d", d=P), ACT.Copy)
                    act.activation(vtok[0:META, CHUNKS_G, :], ps[0:META, 6, 2 * P:3 * P], ACT.Copy)
                    act.drain().then_inc(vtok_ready, 1)
                    act.wait_ge(kft_done, n.next(kft_done))
                    act.activation(kft, ps[:, 7, :].rearrange("p (c d) -> p c d", d=P), ACT.Copy).then_inc(kft_ready, 1)
                    act.wait_ge(go_done, n.next(go_done))
                    for dst, func in ((oT, ACT.Copy), (gsq, ACT.Square)):
                        act.activation(dst[:, 0:S], ps[:, 4, :], func)
                        act.activation(dst[:, S:T], ps[:, 5, 0:META], func)
                    act.drain().then_inc(go_copied, 1)
                    act.wait_ge(gss_done, n.next(gss_done))
                    act.activation(T2.of(rms[:, 0, :]), ps[:, 6:8, 0:T2.width], ACT.Sqrt, bias=EPS, scale=1.0 / P)
                    act.drain().then_inc(rms_ready, 1)

                def causal_exps(hd):
                    act.wait_ge(qmax_ready, n.next(qmax_ready))
                    for i in range(QT):
                        rows = P if i < QT - 1 else META
                        e = exps_of(hd, i)[:, 0:min((i + 1) * P, T)]
                        act.activation(e, e, ACT.Exp, bias=qmax[0:rows, hd, i:i + 1], accum_out=qden[0:rows, hd, i:i + 1])
                    act.drain().then_inc(qexp_ready, 1)

                def copy_causal(hd):
                    for i in range(QT):
                        if (hd * QT + i) % 2 == 0:
                            copy_causal_tile(act, n, i)

                with n.loop(4, MLA_PER):
                    act.wait_ge(vt_done, n.next(vt_done))
                    act.activation(vt[:, 0:QT - 1, :], ps[:, 7, :].rearrange("p (c d) -> p c d", d=P), ACT.Copy)
                    act.activation(vt[0:META, QT - 1, :], ps[0:META, 6, 384:512], ACT.Copy)
                    act.drain().then_inc(vt_ready, 1)
                    for hd in range(2):
                        act.wait_ge(qk_free, n.next(qk_free))
                        b, done = take()
                        act.wait_ge(unit_done[b], done)
                        act.activation(T2.of(qsq), psum_of(b, T2, QK), ACT.Square)
                        act.activation(T2.of(qgain), psum_of(b, T2, QK), ACT.Copy, scale=v2[0:QK, V2["q_norm"]:V2["q_norm"] + 1]).then_inc(unit_free[b], 1)
                        act.drain().then_inc(qk_raw, 1)
                        b, done = take()
                        act.wait_ge(unit_done[b], done)
                        act.activation(T2.of(kraw[0:NOPE]), psum_of(b, T2, NOPE), ACT.Copy).then_inc(unit_free[b], 1)
                        act.drain()
                        act.activation(ksq, kraw[0:QK], ACT.Square)
                        act.activation(kgain, kraw[0:QK], ACT.Copy, scale=v2[0:QK, V2["k_norm"]:V2["k_norm"] + 1])
                        act.drain().then_inc(qk_raw, 1)
                        for side in range(2):
                            root_mean(T2, QK, dst=rms[:, side, :], m=QK)
                            take()
                    causal_exps(0)
                    causal_exps(1)
                    copy_causal(0)
                    copy_causal(1)
                for f in (0, 2):
                    act.wait_ge(ctr_done[0], n.next(ctr_done[0]))
                    act.activation(zb[:, f, 0:S], ps[:, TRB[0], :], ACT.Copy).then_inc(cT_ready[0], 1)
                act.wait_ge(ztail_done, n.next(ztail_done))
                act.activation(zb[:, :, S:T], ps[:, 6, 0:4 * META].rearrange("p (f t) -> p f t", f=4), ACT.Copy).then_inc(zb_ready, 1)
                with n.loop(4, MIX_PER):
                    pass_chunks(4)
                    for _ in range(6):
                        take()
                for _ in range(AHEAD):
                    split_weights()
                for _ in range(KD):
                    used_up()
                squares(H, T2, ready=h_ready)
                root_mean(T2, D)
                split_inputs(HID, T2)
                with n.loop(FF_GROUPS, FF2_PER):
                    for m in range(KD):
                        used_up()
                    for m in range(KD):
                        used_up()
            act.wait_ge(layer_begun, n.next(layer_begun))
            act.dma_start(out, H[:, :, META:]).then_inc(out_done, 16)
            act.wait_ge(out_done, 16)

        @block.vector
        def _(dve):
            n = Counts(dve)
            at = {"unit": 0}
            for b in range(2):
                dve.sem_inc(unit_free[b], 1)
            for b in range(3):
                dve.sem_inc(s_free[b], 1)
            dve.sem_inc(o_free, 1)
            dve.sem_inc(bw_used, 1)
            for b in range(2):
                dve.sem_inc(pair_free[b], 1)
                dve.sem_inc(c_free[b], 1)
            dve.sem_inc(co_free, 1)
            dve.sem_inc(qk_free, 1)

            def take():
                b = at["unit"] % 2
                at["unit"] += 1
                return b, n.next(unit_done[b])

            def col(name, k):
                return v1[:, V1[name] + k:V1[name] + k + 1]

            def rest_of_input(src, rest, tok, k):
                dve.wait_ge(lead_ready, n.next(lead_ready))
                dve.tensor_tensor(tok.of(rest[:, k, :]), tok.of(src[:, k, :]), tok.of(Uh[:, k, :].bitcast(F32)),
                                  ALU.subtract).then_inc(u_ready, 1)

            def norm(gains, tok, dst, rest=None):
                dve.wait_ge(rms_ready, n.next(rms_ready))
                dve.reciprocal(tok.of(rstd), tok.of(rms[:, 0, :]))
                dve.drain()
                for k in range(KD):
                    ins = dve.scalar_tensor_tensor(tok.of(dst[:, k, :]), tok.of(H[:, k, :]), gains(k), tok.of(rstd),
                                                   ALU.mult, ALU.mult)
                    ins.then_inc(u_ready if rest is None else whole_ready, 1)
                    if rest is not None and k > 0:
                        rest_of_input(dst, rest, tok, k - 1)
                if rest is not None:
                    rest_of_input(dst, rest, tok, KD - 1)

            def hidden(b, done, m, tok):
                x = tok.of(relu[:, m % 2, :])
                dve.wait_ge(unit_done[b], done)
                dve.tensor_scalar(x, psum_of(b, tok), 0.0, None, ALU.max).then_inc(unit_free[b], 1)
                dve.drain()
                dve.tensor_tensor(x, x, x, ALU.mult)
                dve.drain()
                dve.tensor_copy(tok.of(HIDh[:, m, :]), x)
                dve.drain()
                dve.tensor_tensor(tok.of(HIDl[:, m, :]), x, tok.of(HIDh[:, m, :].bitcast(F32)), ALU.subtract).then_inc(hid_ready, 1)
                n.next(hid_ready)

            def norm_and_add(gain, tok):
                dve.wait_ge(rms_ready, n.next(rms_ready))
                dve.reciprocal(tok.of(rstd), tok.of(rms[:, 0, :]))
                dve.drain()
                for k in range(KD):
                    dve.scalar_tensor_tensor(tok.of(M[:, k, :]), tok.of(M[:, k, :]), col(gain, k), tok.of(rstd),
                                             ALU.mult, ALU.mult)
                dve.drain()
                for k in range(KD):
                    dve.tensor_tensor(tok.of(H[:, k, :]), tok.of(H[:, k, :]), tok.of(M[:, k, :]), ALU.add).then_inc(h_ready, 1)

            dve.wait_ge(vec_in, 32)
            dve.tensor_scalar(nsinks[:, :], sinks[:, :], -1.0, None, ALU.mult)
            dve.wait_ge(bias_in, 48)
            for h in range(2):
                b, done = take()
                dve.wait_ge(unit_done[b], done)
                dve.tensor_tensor(brow[:, h * 512:(h + 1) * 512], ps[0:16, 2 * b, :], addm[:, h * 512:(h + 1) * 512],
                                  ALU.add).then_inc(unit_free[b], 1)
            dve.drain().then_inc(brow_ready, 1)
            dve.wait_ge(x_in, 48)
            take()
            norm(lambda k: col("g_pre_mix", k), T1, U)
            take()
            take()

            def copy_values(dst):
                dve.wait_ge(tr_done[1], n.next(tr_done[1]))
                dve.tensor_copy(dst[:, 2:4, :], ps[:, 3, 0:2 * P].rearrange("p (j d) -> p j d", d=P)).then_inc(eT_ready[1], 1)

            copy_values(va)

            def maxima(hd, t):
                banded, half = HEADS[hd]
                i = hd % 2
                for b in range(QB):
                    u = (hd * QB + b) % 3
                    keys = key_blocks(banded, b)
                    wd = len(keys) * P
                    c = 384 - P * b + keys[0] * P
                    dve.wait_ge(s_done[u], n.next(s_done[u]))
                    dve.scalar_tensor_tensor(ss[:, i, b, 0:wd], ps[:, 4 + u, 0:wd], DH ** -0.5, bw[:, hd, c:c + wd],
                                             ALU.mult, ALU.add).then_inc(s_free[u], 1)
                dve.drain()
                for b in range(QB):
                    wd = len(key_blocks(banded, b)) * P
                    dve.tensor_reduce(nmax[:, i, b:b + 1], ss[:, i, b, 0:wd], AX, ALU.max, negate=True)
                if banded:
                    dve.drain()
                    dve.tensor_tensor(nms[:, i, :], nmax[:, i, :], nsinks[:, bass.ds(t + 4 * half, 1)].to_broadcast([P, 4]), ALU.min)
                    dve.drain()
                    dve.tensor_tensor(srel[:, i, :], nms[:, i, :], sinks[:, bass.ds(t + 4 * half, 1)].to_broadcast([P, 4]), ALU.add)
                dve.drain().then_inc(max_ready, 1)

            def outputs(hd, t):
                banded, half = HEADS[hd]
                i = hd % 2
                for b in (1, 3):
                    wd = len(key_blocks(banded, b)) * P
                    dve.wait_ge(tr_done[1], n.next(tr_done[1]))
                    dve.tensor_copy(eT[:, 1, 0:wd], ps[:, 3, 0:wd]).then_inc(eT_ready[1], 1)
                dve.wait_ge(exp_ready, n.next(exp_ready))
                total = den
                if banded:
                    dve.tensor_tensor(den2[:, i, :], den[:, i, :], esink[:, i, :], ALU.add)
                    total = den2
                    dve.drain()
                dve.reciprocal(rinv[:, i, :], total[:, i, :])
                dve.drain()
                dve.wait_ge(o_done, n.next(o_done))
                at_col = t * DH + 256 * half if banded else t * P + 512 + DH * half
                dve.tensor_tensor(otok[:, :, bass.ds(at_col, DH)], ps[:, 7, 0:QB * DH].rearrange("p (b d) -> p b d", d=DH),
                                  rinv[:, i, :].unsqueeze(2).to_broadcast([P, QB, DH]), ALU.mult).then_inc(o_free, 1)

            with n.loop(4, ATT_PER) as t:
                for _ in range(4):
                    take()
                copy_values(vb)
                dve.wait_ge(bw_in, n.next(bw_in, 64))
                maxima(0, t)
                maxima(1, t)
                outputs(0, t)
                maxima(2, t)
                outputs(1, t)
                maxima(3, t)
                dve.drain().then_inc(bw_used, 1)
                outputs(2, t)
                outputs(3, t)

            dve.wait_ge(osq_ready, 1)
            dve.reciprocal(r8[:, :], rms8[:, :])
            dve.drain()
            for b in range(QB):
                for half in range(2):
                    o = otok[:, b, half * 512:(half + 1) * 512]
                    dve.tensor_scalar(o, o, r8[:, 2 * b + half:2 * b + half + 1], None, ALU.mult)
            dve.drain().then_inc(on_ready, 1)
            for f in range(1, KD, 2):
                dve.wait_ge(tr_done[1], n.next(tr_done[1]))
                dve.tensor_scalar(HID[:, f, META:].rearrange("p (b q) -> p b q", q=P),
                                  ps[:, 3, :].rearrange("p (b q) -> p b q", q=P)[:, :, ::-1],
                                  col("g_out", f), None, ALU.mult).then_inc(oT_ready[1], 1)
                dve.drain().then_inc(whole_ready, 1)
                rest_of_input(HID, Ul1, T1, f - 1)
                rest_of_input(HID, Ul1, T1, f)
            for m in range(KD):
                take()
            take()
            norm_and_add("g_post_mix", T1)
            take()
            norm(lambda k: col("g_pre_mlp", k), T1, HID, Ul1)
            dve.wait_ge(m_zero, 1)
            with n.loop(FF_GROUPS, FF_PER):
                for m in range(KD):
                    hidden(*take(), m, T1)
                for m in range(KD):
                    b, done = take()
                    dve.wait_ge(unit_done[b], done)
                    dve.tensor_tensor(T1.of(M[:, m, :]), T1.of(M[:, m, :]), psum_of(b, T1), ALU.add).then_inc(unit_free[b], 1)
                dve.drain()
            for m in range(KD):
                dve.sem_inc(m_ready, 1)
            take()
            norm_and_add("g_post_mlp", T1)
            dve.drain()
            for k in range(KD):
                dve.sem_inc(whole_ready, 1)
            for k in range(KD):
                rest_of_input(H, Ul1, T1, k)
            dve.wait_ge(pt_lead, 1)
            for k in range(2):
                dve.tensor_tensor(ptl[:, k, :], pt[:, k, :], pth[:, k, :].bitcast(F32), ALU.subtract)
            dve.drain().then_inc(pt_ready, 1)
            for m in range(KD):
                take()
            for m in range(KD):
                b, done = take()
                dve.wait_ge(gate_ready, n.next(gate_ready))
                dve.wait_ge(unit_done[b], done)
                dve.tensor_tensor(T1.of(M[:, m, :]), psum_of(b, T1), T1.of(HID[:, m, :]), ALU.mult).then_inc(unit_free[b], 1)
                dve.drain().then_inc(m_ready, 1)
            take()
            norm_and_add("g_post_ple", T1)

            def col2(name, k=0, rows=P):
                return v2[0:rows, V2[name] + k:V2[name] + k + 1]

            def gated(dst, sig):
                b, done = take()
                dve.wait_ge(unit_done[b], done)
                dve.wait_ge(sig_ready, n.next(sig_ready))
                dve.tensor_tensor(dst, psum_of(b, T2), T2.of(sig), ALU.mult).then_inc(unit_free[b], 1)

            pairm3 = pairm[:, :].rearrange("p (l t) -> p l t", t=GCH)

            def level_operands(level):
                size, i = 2 ** (level - 1), level % 2
                dve.tensor_tensor(level_blocks(lq[i], size, 1), level_blocks(qg_, size, 1), level_blocks(pre, size, 1), ALU.mult)
                dve.tensor_tensor(level_blocks(lk[i], size, 0), level_blocks(kk, size, 0), level_blocks(suf, size, 0), ALU.mult)
                dve.drain().then_inc(level_ready, 1)

            def level_up(level):
                size = 2 ** (level - 1)
                dve.tensor_tensor(level_blocks(suf, size, 0), level_blocks(suf, size, 0), level_total(pre, size, 1), ALU.mult)
                dve.drain()
                dve.tensor_tensor(level_blocks(pre, size, 1), level_blocks(pre, size, 1), level_total(pre, size, 0), ALU.mult)
                dve.drain()

            def select_pairs(level):
                b = level % 2
                dve.drain()
                mask = pairm3[:, level, :].unsqueeze(1).to_broadcast([P, CHUNKS_G, GCH])
                dve.wait_ge(pair_done[b], n.next(pair_done[b]))
                dve.sem_inc(passed, 1)
                dve.copy_predicated(amat, mask, ps[:, 4 + b, :].rearrange("p (c t) -> p c t", t=GCH)).then_inc(pair_free[b], 1)

            def select_tails():
                for level in range(5):
                    dve.drain()
                    dve.copy_predicated(atail, pairm3[0:META, level, 0:META], ps[0:META, 6, level * META:(level + 1) * META])

            dve.wait_ge(consts2_in, 96)
            dve.tensor_copy(pairm[:, :], pairf)
            dve.drain()
            with n.loop(LAYERS, LAYER_PER) as layer:
                dve.tensor_copy(v2[:, :], v2all[:, bass.ds(layer, 1), :].rearrange("p o c -> p (o c)"))
                dve.drain().then_inc(layer_begun, 1)
                lb01 = v2[:, V2["lb0"]:V2["lb0"] + 8].rearrange("p (l h) -> p l h", l=2)
                dve.tensor_tensor(lb_max, lb01[:, 0, :], lb01[:, 1, :], ALU.max)
                dve.drain()
                dve.tensor_tensor(lb_e, lb01, lb_max.unsqueeze(1).to_broadcast([P, 2, 4]), ALU.subtract)
                dve.drain().then_inc(lb_max_ready, 1)
                dve.wait_ge(lb_exp_ready, n.next(lb_exp_ready))
                dve.tensor_tensor(lb_sum, lb_e[:, 0, :], lb_e[:, 1, :], ALU.add)
                dve.drain()
                dve.reciprocal(lb_sum, lb_sum)
                dve.drain()
                dve.tensor_tensor(lb_e, lb_e, lb_sum.unsqueeze(1).to_broadcast([P, 2, 4]), ALU.mult)
                dve.drain()
                dve.scalar_tensor_tensor(oml, lb_e[:, 1, :], col2("second"), lb_e[:, 0, :], ALU.mult, ALU.add)
                dve.drain()
                dve.tensor_tensor(oml, oml, lb_e[:, 0, :], ALU.subtract)
                dve.drain()
                dve.tensor_scalar(oml, oml, -1.0, 1.0, ALU.mult, ALU.add)

                dve.drain()
                take()
                norm(lambda k: col2("norm1", k), T2, HID, Ul2)
                with n.loop(2, CONV_PER) as c:
                    for j in range(2):
                        take()
                        gated(hc[:, bass.ds(2 * c + j, 1), TAPS - 1:].rearrange("p o (h n) -> p (o h) n", h=2), relu[:, j, :])
                dve.drain()
                dve.wait_ge(hc_padded, n.next(hc_padded))
                for k in range(TAPS):
                    for t in range(CONV_TILES):
                        x, wk = hc[:, t, k:k + T], col2("conv_w", t * TAPS + k)
                        if k == 0:
                            ins = dve.tensor_scalar(za[:, t, :], x, wk, col2("conv_b", t), ALU.mult, ALU.add)
                        else:
                            ins = dve.scalar_tensor_tensor(za[:, t, :], x, wk, za[:, t, :], ALU.mult, ALU.add)
                        if k == TAPS - 1:
                            ins.then_inc(conv_ready, 1)
                    dve.drain()
                with n.loop(6, GATE_PER):
                    for _ in range(4):
                        take()
                for _ in range(4):
                    b, done = take()
                dve.wait_ge(unit_done[b], done)
                for k in range(KD):
                    dve.scalar_tensor_tensor(U[:, k, :], H[:, k, :], col2("norm1", k), rstd[:, :], ALU.mult, ALU.mult).then_inc(u_ready, 1)
                take()
                dve.wait_ge(mean_ready, n.next(mean_ready))
                for t in range(CONV_TILES):
                    dve.tensor_tensor(za[:, t, :], za[:, t, :], mu, ALU.subtract)
                dve.drain().then_inc(centred, 1)
                take()
                dve.wait_ge(rms_ready, n.next(rms_ready))
                dve.reciprocal(rstd[:, :], rms[:, 0, :])
                dve.drain()
                for t in range(CONV_TILES):
                    dve.scalar_tensor_tensor(za[:, t, :], za[:, t, :], col2("ln_g", t), rstd[:, :], ALU.mult, ALU.mult)
                dve.drain().then_inc(ln_ready, 1)
                for src, count, names in ((rms[:, 1, :], 2, "q_a"), (rms_v, 1, "kv_a")):
                    take()
                    dve.wait_ge(rms_ready, n.next(rms_ready))
                    dve.reciprocal(rstd[:, :], src)
                    dve.drain()
                    for k in range(count):
                        x = cq[:, k, :] if count == 2 else ckv
                        dve.scalar_tensor_tensor(x, x, col2(names, k), rstd[:, :], ALU.mult, ALU.mult)
                    dve.drain()
                dve.drain().then_inc(c_ready, 1)
                dve.wait_ge(lnsig_ready, n.next(lnsig_ready))
                for t in range(CONV_TILES):
                    dve.scalar_tensor_tensor(za[:, t, :], za[:, t, :], col2("ln_b", t), Hs[t], ALU.add, ALU.mult)

                with n.loop(HEADS_G, GREC_PER) as h:
                    dve.drain()
                    dve.tensor_copy(headcol[:, 0:1], oml[:, bass.ds(h, 1)])
                    dve.tensor_copy(headcol[:, 1:2], v2[:, bass.ds(h + V2["hgrn_g"], 1)])
                    dve.memset(suf, 1.0)
                    dve.drain()
                    take()
                    dve.wait_ge(f_sig, n.next(f_sig))
                    dve.tensor_scalar(kk, relu[:, 0, :], headcol[:, 0:1], None, ALU.mult)
                    dve.drain()
                    dve.tensor_scalar(pre, kk, CLAMP, -1.0, ALU.min, ALU.mult)
                    dve.drain()
                    dve.tensor_scalar(pre, pre, 1.0, None, ALU.add)
                    dve.drain()
                    take()
                    dve.wait_ge(q_ready, n.next(q_ready))
                    level_operands(1)
                    level_up(1)
                    level_operands(2)
                    level_up(2)
                    gated(T2.of(vT), Hs[6])
                    dve.drain().then_inc(v_ready, 1)
                    select_pairs(0)
                    select_pairs(1)
                    level_operands(3)
                    level_up(3)
                    gated(T2.of(gs), Hs[5])
                    for level in range(4, LEVELS + 1):
                        select_pairs(level - 2)
                        level_operands(level)
                        level_up(level)
                        if level == 6:
                            select_tails()
                    dve.tensor_tensor(qfull, qg_, pre, ALU.mult)
                    dve.tensor_tensor(kfull[:, 0:S], kk[:, 0:S], suf[:, 0:S], ALU.mult)
                    select_pairs(LEVELS - 1)
                    select_pairs(LEVELS)
                    dve.drain().then_inc(a_ready, 1)
                    dve.wait_ge(upd_done, n.next(upd_done))
                    dve.tensor_copy(state[:, 1, :], ps[:, 6, 0:GCH])
                    for c in range(1, CHUNKS_G):
                        dve.drain()
                        dve.scalar_tensor_tensor(state[:, c + 1, :], state[:, c, :], pre[:, (c + 1) * GCH - 1:(c + 1) * GCH],
                                                 ps[:, 6, c * GCH:(c + 1) * GCH], ALU.mult, ALU.add)
                    dve.drain().then_inc(state_ready, 1)
                    dve.wait_ge(rms_ready, n.next(rms_ready))
                    dve.reciprocal(rstd[:, :], rms[:, 0, :])
                    dve.drain()
                    dve.scalar_tensor_tensor(oT, oT, headcol[:, 1:2], rstd[:, :], ALU.mult, ALU.mult)
                    dve.drain()
                    dve.tensor_tensor(zc[:, bass.ds(h, 1), :].rearrange("p o t -> p (o t)"), oT, gs, ALU.mult)

                dve.drain().then_inc(zc_ready, 1)
                dve.drain().then_inc(mlaw_used, 1)

                def rotated(src, dst, side, hd):
                    take()
                    dve.tensor_tensor(dst, src, cosT, ALU.mult)
                    dve.wait_ge(rms_ready, n.next(rms_ready))
                    dve.reciprocal(rstd[0:QK, :], rms[0:QK, side, :])
                    b, done = take()
                    dve.wait_ge(unit_done[b], done)
                    dve.tensor_tensor(T2.of(rot1), psum_of(b, T2, QK), T2.of(sinT), ALU.mult).then_inc(unit_free[b], 1)
                    dve.drain()
                    dve.tensor_tensor(dst, dst, rot1, ALU.add)
                    dve.drain()
                    dve.tensor_tensor(dst, dst, rstd[0:QK, :], ALU.mult)
                    dve.drain()

                def causal_maxima(hd):
                    for i in range(QT):
                        e = exps_of(hd, i)
                        if i < QT - 1:
                            b, wd = i % 2, (i + 1) * P
                            dve.wait_ge(c_done[b], n.next(c_done[b]))
                            dve.scalar_tensor_tensor(e[:, 0:wd], ps[:, 4 + b, 0:wd], QK ** -0.5, triT[:, S - i * P:S + P],
                                                     ALU.mult, ALU.add).then_inc(c_free[b], 1)
                        else:
                            for b in range(2):
                                dve.wait_ge(c_done[b], n.next(c_done[b]))
                                dve.scalar_tensor_tensor(T2.part(e, b), ps[0:META, 4 + b, 0:T2.width], QK ** -0.5,
                                                         triT[0:META, b * T2.width:(b + 1) * T2.width],
                                                         ALU.mult, ALU.add).then_inc(c_free[b], 1)
                    dve.drain()
                    for i in range(QT):
                        e = exps_of(hd, i)[:, 0:min((i + 1) * P, T)]
                        rows = P if i < QT - 1 else META
                        dve.tensor_reduce(qmax[0:rows, hd, i:i + 1], e, AX, ALU.max, negate=True)
                    dve.drain().then_inc(qmax_ready, 1)

                def causal_outputs(hd, pair):
                    for i in range(QT):
                        if (hd * QT + i) % 2 == 1:
                            copy_causal_tile(dve, n, i)
                    dve.wait_ge(qexp_ready, n.next(qexp_ready))
                    dve.reciprocal(qinv[:, hd, 0:QT - 1], qden[:, hd, 0:QT - 1])
                    dve.reciprocal(qinv[0:META, hd, QT - 1:QT], qden[0:META, hd, QT - 1:QT])
                    dve.drain()
                    dve.wait_ge(co_done, n.next(co_done))
                    cols = bass.ds(pair * P + hd * DH, DH)
                    dve.tensor_tensor(otok2[:, 0:QT - 1, cols], ps[:, 6, 0:(QT - 1) * DH].rearrange("p (b d) -> p b d", d=DH),
                                      qinv[:, hd, 0:QT - 1].unsqueeze(2).to_broadcast([P, QT - 1, DH]), ALU.mult)
                    dve.tensor_scalar(otok2[0:META, QT - 1, cols], ps[0:META, 6, (QT - 1) * DH:QT * DH],
                                      qinv[0:META, hd, QT - 1:QT], None, ALU.mult)
                    dve.drain().then_inc(co_free, 1)

                with n.loop(4, MLA_PER) as pair:
                    for hd in range(2):
                        take()
                        take()
                        dve.wait_ge(qk_raw, n.next(qk_raw, 2))
                        rotated(qgain, qh_of[hd], 0, hd)
                        rotated(kgain, kh_of[hd], 1, hd)
                        dve.drain().then_inc(qk_ready, 1)
                        dve.drain().then_inc(qk_free, 1)
                    causal_maxima(0)
                    causal_maxima(1)
                    causal_outputs(0, pair)
                    causal_outputs(1, pair)
                for f in (1, 3):
                    dve.wait_ge(ctr_done[1], n.next(ctr_done[1]))
                    dve.tensor_copy(zb[:, f, 0:S], ps[:, TRB[1], :]).then_inc(cT_ready[1], 1)

                def gate_of(branch, m):
                    return gates[:, bass.ds(m + branch * KD, 1), :].rearrange("p o (h n) -> p (o h) n", h=2)

                def tile_of(x, m):
                    return x[:, bass.ds(m, 1), :].rearrange("p o (h n) -> p (o h) n", h=2)

                with n.loop(4, MIX_PER) as i:
                    for j in range(2):
                        m = 2 * i + j
                        mix, parts = T2.of(rms[:, 0, :]), [T2.of(x) for x in (rms[:, 0, :], relu[:, 0, :], relu[:, 1, :])]
                        for branch in range(3):
                            b, done = take()
                            dve.wait_ge(unit_done[b], done)
                            dve.tensor_tensor(parts[branch], psum_of(b, T2), gate_of(branch, m), ALU.mult).then_inc(unit_free[b], 1)
                        for part in parts[1:]:
                            dve.drain()
                            dve.tensor_tensor(mix, mix, part, ALU.add)
                        dve.drain()
                        dve.tensor_copy(tile_of(Mh, m), mix)
                        dve.drain()
                        dve.tensor_tensor(tile_of(Ml, m), mix, tile_of(Mh, m).bitcast(F32), ALU.subtract)
                        dve.drain()
                dve.drain().then_inc(m_done, 1)
                for m in range(KD):
                    b, done = take()
                    dve.wait_ge(unit_done[b], done)
                    dve.tensor_tensor(T2.of(H[:, m, :]), T2.of(H[:, m, :]), psum_of(b, T2), ALU.add).then_inc(unit_free[b], 1)
                    dve.drain().then_inc(h_ready, 1)
                take()
                norm(lambda k: col2("norm2", k), T2, HID, Ul2)
                with n.loop(FF_GROUPS, FF2_PER):
                    for m in range(KD):
                        hidden(*take(), m, T2)
                    for m in range(KD):
                        b, done = take()
                        dve.wait_ge(unit_done[b], done)
                        dve.tensor_tensor(T2.of(H[:, m, :]), T2.of(H[:, m, :]), psum_of(b, T2), ALU.add).then_inc(unit_free[b], 1)
                    dve.drain()
            dve.drain().then_inc(layer_begun, 1)


def tiles_of(wt):
    k, m = wt.shape
    return wt.reshape(k // P, P, m // P, P).transpose(2, 1, 0, 3).reshape(m // P, P, k)


def columns(v):
    return np.ascontiguousarray(v.reshape(-1, P).T)


def layout_first(a):
    w_in = a["w_in"][0]
    head = lambda base, h: w_in[:, base + h * DH:base + (h + 1) * DH]
    q_a = tiles_of(np.concatenate([head(0, h) for t in range(4) for h in (t, t + 4)], axis=1))
    ka, va = tiles_of(w_in[:, 512:640]), tiles_of(w_in[:, 640:768])
    q_b, k_b, v_b = (tiles_of(w_in[:, 768 + 512 * i:1280 + 512 * i]) for i in range(3))
    chunks = [ka[0], va[0]]
    for t in range(4):
        chunks += [q_a[t], q_b[t], k_b[t], v_b[t]]
    chunks += list(tiles_of(a["w_o"][0]))
    up, down = tiles_of(a["w_up"][0]), a["w_down"][0]
    for g in range(FF_GROUPS):
        chunks += list(up[8 * g:8 * g + 8]) + list(tiles_of(down[D * g:D * (g + 1)]))
    chunks += list(tiles_of(a["w_ple_gate"][0]))
    ple = tiles_of(a["w_ple_proj"][0])
    chunks += [np.concatenate(list(ple[4 * i:4 * i + 4]), axis=1) for i in range(2)]
    assert len(chunks) == N1_CHUNKS
    return chunks


def layout_second(a):
    ring_chunks, head_chunks = [], []
    for l in range(LAYERS):
        wt = tiles_of(np.concatenate([a["w_in_2"][l][:, :1408], np.zeros((D, NOPE), np.float32), a["w_in_2"][l][:, 1408:1440],
                                      np.zeros((D, P - QK), np.float32), a["w_in_2"][l][:, 1440:]], axis=1))
        value, gate, latent, rec, gates = wt[0:4], wt[4:8], wt[8:12], wt[12:28], wt[28:52]
        for t in range(4):
            ring_chunks += [gate[t], value[t]]
        ring_chunks += list(gates) + list(latent)
        q, f, i, g = (rec[4 * k:4 * k + 4] for k in range(4))
        for h in range(HEADS_G):
            ring_chunks += [f[h], q[h], i[h], g[h]]
        uq, ukv = a["w_uq_2"][l], a["w_ukv_2"][l]
        for pair in range(4):
            c = np.zeros((P, 8, P), np.float32)
            for j in range(2):
                h = 2 * pair + j
                c[:, 3 * j:3 * j + 2, :QK] = uq[:, h * QK:(h + 1) * QK].reshape(2, P, QK).transpose(1, 0, 2)
                c[:, 3 * j + 2, :NOPE] = ukv[:, h * P:h * P + NOPE]
                c[:, 6, j * DH:(j + 1) * DH] = ukv[:, h * P + NOPE:(h + 1) * P]
            head_chunks.append(c.reshape(P, CH))
        conv, att, rec = (tiles_of(a[k][l]) for k in ("w_conv_out_2", "w_attn_out_2", "w_hgrn_out_2"))
        for m in range(KD):
            ring_chunks += [np.concatenate([conv[m], att[m]], axis=1),
                            np.concatenate([rec[m], np.zeros((P, 512), np.float32)], axis=1)]
        ring_chunks += list(tiles_of(a["w_out_2"][l]))
        up, down = tiles_of(a["w_ff1_2"][l]), a["w_ff2_2"][l]
        for g in range(FF_GROUPS):
            ring_chunks += list(up[8 * g:8 * g + 8]) + list(tiles_of(down[D * g:D * (g + 1)]))
    assert len(ring_chunks) == LAYERS * N2_CHUNKS
    return ring_chunks, head_chunks


def vectors_second(a):
    out = []
    for l in range(LAYERS):
        pad = lambda v: np.concatenate([v, np.zeros(P - QK, np.float32)])
        out.append(np.concatenate([
            columns(a["norm1_g_2"][l]),
            a["conv_w_2"][l].T.reshape(CONV_TILES, P, TAPS).transpose(1, 0, 2).reshape(P, -1),
            columns(a["conv_b_2"][l]), columns(a["conv_ln_g_2"][l]), columns(a["conv_ln_b_2"][l]),
            columns(a["q_a_norm_g_2"][l]), columns(a["kv_a_norm_g_2"][l]), columns(pad(a["q_norm_g_2"][l])),
            columns(pad(a["k_norm_g_2"][l])), columns(a["hgrn_lb_logits_2"][0]), columns(a["hgrn_lb_logits_2"][1]),
            np.full((P, 1), float(l), np.float32), columns(a["hgrn_norm_g_2"][l]), columns(a["norm2_g_2"][l])], axis=1))
    return np.stack(out, axis=1)


def rotary_constants():
    half = ROPE // 2
    freq = np.float32(10000.0) ** (-np.arange(half, dtype=np.float32) / np.float32(half))
    ang = (np.arange(T, dtype=np.float32)[None, :] * freq[:, None]).astype(np.float32)
    cosines, sines = np.ones((QK, T), np.float32), np.zeros((QK, T), np.float32)
    cosines[NOPE:] = np.concatenate([np.cos(ang)] * 2)
    sines[NOPE:] = np.concatenate([np.sin(ang)] * 2)
    turn = np.zeros((QK, QK), np.float32)
    for j in range(half):
        turn[NOPE + half + j, NOPE + j] = -1.0
        turn[NOPE + j, NOPE + half + j] = 1.0
    return cosines, sines, turn


def mask_constants():
    causal = np.zeros((P, 640), np.float32)
    causal[:, S:] = np.where(np.arange(P)[None, :] <= np.arange(P)[:, None], 0.0, NEG)
    s, t = np.arange(GCH)[:, None], np.arange(GCH)[None, :]
    masks = [s == t]
    for level in range(1, LEVELS + 1):
        size = 2 ** (level - 1)
        masks.append((s // (2 * size) == t // (2 * size)) & (s % (2 * size) < size) & (t % (2 * size) >= size))
    return causal, np.concatenate(masks, axis=1).astype(np.float32)


def distance_constants():
    rel = np.arange(REL) - 511
    n = np.abs(rel)
    large = 8 + (np.log(np.maximum(n, 1) / 8.0) / np.log(128.0) * 8).astype(np.int64)
    bucket = np.where(rel > 0, 16, 0) + np.where(n < 8, n, np.minimum(large, 15))
    onehot = (np.arange(32)[:, None] == bucket[None, :]).astype(np.float32)
    seen = np.zeros(REL)
    for window, dil in DILATED:
        seen += (rel % dil == 0) & (n <= window // 2)
    dilated = np.where(seen > 0, np.log(np.maximum(seen, 1)), NEG)
    banded = np.where(n <= WIN, 0.0, NEG)
    return onehot, np.stack([banded] * 8 + [dilated] * 8).astype(np.float32)


def kernel(**inputs):
    import concourse.bacc as _bacc
    from concourse.bass_utils import run_bass_kernel_spmd as _run

    a = {k: np.asarray(v) for k, v in inputs.items()}
    onehot, addmask = distance_constants()
    cosines, sines, turn = rotary_constants()
    causal, pairs = mask_constants()
    ring_chunks, head_chunks = layout_second(a)
    arrays = {
        "xT": a["x"][0].T.reshape(KD, P, S).transpose(1, 0, 2),
        "pT": a["p"][0, 0].T.reshape(2, P, S).transpose(1, 0, 2),
        "metaT": a["meta_2"].T.reshape(KD, P, META).transpose(1, 0, 2),
        "w": np.stack(layout_first(a) + ring_chunks + [np.zeros((P, CH), np.float32)] * AHEAD),
        "w_mla": np.stack(head_chunks),
        "vec1": np.concatenate([columns(v) for v in (
            a["g_pre_mix"][0], np.concatenate([a["g_out_a"][0], a["g_out_b"][0]]), a["g_post_mix"][0],
            a["g_pre_mlp"][0], a["g_post_mlp"][0], a["b_ple_gate"][0], a["g_post_ple"][0])], axis=1),
        "vec2": vectors_second(a),
        "table": a["rel_bias_table"],
        "onehot": onehot,
        "addmask": addmask,
        "sink": a["sink_a"],
        "cosines": cosines,
        "sines": sines,
        "turn": turn,
        "causal": causal,
        "pairs": pairs,
    }
    nc = _bacc.Bacc("TRN2", target_bir_lowering=False, num_devices=1)
    args = []
    for name, v in arrays.items():
        arrays[name] = np.ascontiguousarray(v)
        args.append(nc.dram_tensor(name, v.shape, F32, kind="ExternalInput").ap())
    out = nc.dram_tensor("out", (P, KD, S), F32, kind="ExternalOutput").ap()
    program(nc, *args, out)
    r = _run(nc, [arrays], core_ids=[0])
    got = r.results[0]["out"]
    return got.transpose(1, 0, 2).reshape(1, D, S).transpose(0, 2, 1)
```

```python
from contextlib import ExitStack, contextmanager

import numpy as np
import concourse.bass as bass
from concourse import mybir

F32 = mybir.dt.float32
F32R = mybir.dt.float32r
U8 = mybir.dt.uint8
ACT = mybir.ActivationFunctionType
ALU = mybir.AluOpType
AX = mybir.AxisListType.X

P = 128
D = 1024
KD = D // P
S = 512
META = 16
T = S + META
EPS = 1e-6
NEG = -1e30
CH = 8 * P
STAGE = 2
RING = 2
AHEAD = 2

DH = 64
WIN = 128
DILATED = ((128, 1), (512, 4), (2048, 16))
QB = S // P
REL = 1024
BW = 896
FF_GROUPS = 4

V1 = {}
_at = 0
for _name, _n in (("g_pre_mix", 8), ("g_out", 8), ("g_post_mix", 8), ("g_pre_mlp", 8), ("g_post_mlp", 8),
                  ("b_gate", 8), ("g_post_ple", 8)):
    V1[_name] = _at
    _at += _n
V1_COLS = _at

ATT_CHUNKS = 4
N1_CHUNKS = 2 + 4 * ATT_CHUNKS + KD + 16 * FF_GROUPS + KD + 2


LAYERS = 2
TAPS = 31
CONV_TILES = 4
HEADS_G = 4
GCH = 128
CHUNKS_G = S // GCH
CLAMP = 1.0 - 1e-6
LEVELS = 7
QK = 96
NOPE = 64
ROPE = 32
T2_TILES = 6
QT = 5
V2 = {}
_at = 0
for _name, _n in (("norm1", 8), ("conv_w", TAPS * CONV_TILES), ("conv_b", 4), ("ln_g", 4), ("ln_b", 4), ("q_a", 2),
                  ("kv_a", 1), ("q_norm", 1), ("k_norm", 1), ("lb0", 4), ("lb1", 4), ("second", 1), ("hgrn_g", 4),
                  ("norm2", 8)):
    V2[_name] = _at
    _at += _n
V2_COLS = _at
N2_CHUNKS = 8 + 24 + 4 + 16 + 16 + 8 + 16 * FF_GROUPS


LOOPS = {
    "attention": {"bw_in": 64, "eT_ready0": 9, "eT_ready1": 9, "exp_ready": 4, "max_ready": 4, "o_done": 4,
        "o_free": 4, "qkv_ready": 4, "scores_done0": 6, "scores_done1": 5, "scores_done2": 5, "scores_free0": 6,
        "scores_free1": 5, "scores_free2": 5, "stage_full0": 32, "stage_full1": 32, "tr_done0": 9, "tr_done1": 9,
        "unit_done0": 2, "unit_done1": 2, "unit_free0": 2, "unit_free1": 2},
    "ff": {"hid_ready": 8, "stage_full0": 128, "stage_full1": 128, "unit_done0": 8, "unit_done1": 8, "unit_free0": 8,
        "unit_free1": 8, "w_split": 16},
    "conv": {"sig_ready": 2, "stage_full0": 32, "stage_full1": 32, "unit_done0": 2, "unit_done1": 2},
    "gates": {"stage_full0": 32, "stage_full1": 32, "unit_done0": 2, "unit_done1": 2, "unit_free0": 2,
        "unit_free1": 2, "w_split": 4},
    "recurrence": {"a_ready": 1, "f_sig": 1, "go_copied": 1, "go_done": 1, "gss_done": 1, "inv_ready": 1,
        "kft_done": 1, "kft_ready": 1, "level_ready": 7, "pair_done0": 4, "pair_done1": 4, "pair_free0": 4,
        "pair_free1": 4, "q_ready": 1, "qg_ready": 1, "rms_ready": 1, "sig_ready": 2, "spread_done": 1,
        "stage_full0": 32, "stage_full1": 32, "state_ready": 1, "unit_done0": 2, "unit_done1": 2, "unit_free0": 2,
        "unit_free1": 2, "upd_done": 1, "v_ready": 1, "vtok_ready": 1, "vtr_done": 1},
    "mla": {"cT_ready0": 5, "cT_ready1": 5, "causal_done0": 6, "causal_done1": 6, "causal_free0": 6,
        "causal_free1": 6, "co_done": 2, "co_free": 2, "ctr_done0": 5, "ctr_done1": 5, "inv_ready": 4, "mlaw_in": 16,
        "mlaw_used": 1, "qexp_ready": 2, "qk_free": 2, "qk_raw": 4, "qk_ready": 2, "qmax_ready": 2, "rms_ready": 4,
        "unit_done0": 8, "unit_done1": 8, "unit_free0": 8, "unit_free1": 8, "vt_done": 1, "vt_ready": 1},
    "mix": {"stage_full0": 32, "stage_full1": 32, "unit_done0": 3, "unit_done1": 3, "unit_free0": 3, "unit_free1": 3},
    "ff2": {"hid_ready": 8, "stage_full0": 128, "stage_full1": 128, "unit_done0": 8, "unit_done1": 8,
        "unit_free0": 8, "unit_free1": 8, "w_split": 16},
    "layer": {"a_ready": 4, "cT_ready0": 22, "cT_ready1": 22, "c_ready": 1, "causal_done0": 24, "causal_done1": 24,
        "causal_free0": 24, "causal_free1": 24, "centred": 1, "co_done": 8, "co_free": 8, "conv_ready": 4,
        "ctr_done0": 22, "ctr_done1": 22, "f_sig": 4, "go_copied": 4, "go_done": 4, "gss_done": 4, "h_ready": 8,
        "hc_padded": 1, "hid_ready": 32, "inv_ready": 25, "kft_done": 4, "kft_ready": 4, "layer_begun": 1,
        "lb_exp_ready": 1, "lb_max_ready": 1, "lead_ready": 16, "level_ready": 28, "ln_ready": 1, "lnsig_ready": 1,
        "m_done": 1, "mean_ready": 1, "mlaw_in": 64, "mlaw_used": 5, "pair_done0": 16, "pair_done1": 16,
        "pair_free0": 16, "pair_free1": 16, "q_ready": 4, "qexp_ready": 8, "qg_ready": 4, "qk_free": 8, "qk_raw": 16,
        "qk_ready": 8, "qmax_ready": 8, "rms_ready": 25, "sig_ready": 12, "spread_done": 4, "sq_ready": 23,
        "stage_full0": 1120, "stage_full1": 1120, "state_ready": 4, "sum_ready": 3, "u_ready": 24, "unit_done0": 112,
        "unit_done1": 111, "unit_free0": 112, "unit_free1": 111, "upd_done": 4, "v_ready": 4, "vt_done": 4,
        "vt_ready": 4, "vtok_ready": 4, "vtr_done": 4, "w_lead_ready": 108, "w_split": 108, "whole_ready": 16,
        "zb_ready": 1, "zc_ready": 1, "ztail_done": 1},
}


class Counts:

    def __init__(self, eng):
        self.eng, self.seen, self.loops = eng, {}, []

    def next(self, sem, by=1):
        self.seen[sem.name] = self.seen.get(sem.name, 0) + by
        return self.now(sem)

    def now(self, sem):
        value = self.seen.get(sem.name, 0)
        for reg, per in self.loops:
            if per.get(sem.name, 0):
                value = reg * per[sem.name] + value
        return value

    @contextmanager
    def loop(self, count, per):
        before = dict(self.seen)
        with self.eng.Fori(0, count) as reg:
            self.loops.append((reg, per))
            yield reg
            self.loops.pop()
        for name, value in self.seen.items():
            once, begun = value - before.get(name, 0), before.get(name, 0)
            assert once in (0, per.get(name, 0)), f"{name}: {once} an iteration, not {per.get(name, 0)}"
            self.seen[name] = begun + count * per.get(name, 0)


class Tokens:

    def __init__(self, start, count, parts):
        self.start, self.count, self.parts, self.width = start, count, parts, count // parts
        self.tiles = parts * -(-self.width // P)
        self.rows = count // self.tiles

    def of(self, x):
        return x[:, self.start:self.start + self.count].rearrange("p (h n) -> p h n", h=self.parts)

    def part(self, x, h):
        return x[:, self.start + h * self.width:self.start + (h + 1) * self.width]


def program(nc, xT, pT, metaT, w, w_mla, vec1, vec2, table, onehot, addmask, sink, cosines, sines, turn, causal, pairs, out):
    ctx = ExitStack()
    with ctx:
        def sb(name, shape, dt=F32):
            return ctx.enter_context(nc.sbuf_tensor(name, shape, dt))

        def sem(name):
            return ctx.enter_context(nc.semaphore(name))

        ps = ctx.enter_context(nc.psum_tensor("ps", [P, 8, 512], F32))
        slab_cols = 52800
        origin = (nc.sbuf_base + 31) // 32 * 32
        ctx.enter_context(nc.sbuf_tensor("slab", [P, slab_cols], F32))
        top = [0]

        def at(name, shape, col=None, dt=F32, rows=P):
            size = int(np.prod(shape))
            if col is None:
                col = top[0]
                top[0] += (size + 7) // 8 * 8
            assert 4 * (col + size) + 64 <= 4 * slab_cols, name
            return nc.alloc_sbuf_tensor_at(name, [rows, *shape], dt, offset=origin + 4 * col).ap()

        H = at("H", [KD, T])
        col_u, col_m, col_hid = (top[0] + i * KD * T for i in range(3))
        U = at("U", [KD, T])
        M = at("M", [KD, T])
        HID = at("HID", [KD, T])
        Uh, Ul2 = at("Uh", [KD, T], col_u, F32R), at("Ul2", [KD, T], col_m, F32R)
        Mh, Ml = at("Mh", [KD, T], col_m, F32R), at("Ml", [KD, T], col_u, F32R)
        HIDh = at("HIDh", [KD, T], col_hid, F32R)
        stage = at("stage", [STAGE, CH])
        wh = at("wh", [RING, CH], dt=F32R)
        wl = at("wl", [RING, CH], dt=F32R)
        mixed = at("mixed", [T])
        rstd = at("rstd", [T])
        relu = at("relu", [2, T])
        ones = at("ones", [P])
        ident = at("ident", [P])
        v1 = at("v1", [V1_COLS])
        v2all = at("v2all", [LAYERS, V2_COLS])
        v2 = at("v2", [V2_COLS])
        rotm = at("rotm", [QK], rows=QK)
        small = at("small", [192])
        smalls = [0]

        def few(*shape):
            size = int(np.prod(shape))
            view = small[:, smalls[0]:smalls[0] + size]
            smalls[0] += size
            assert smalls[0] <= 192
            return view if len(shape) == 1 else view.rearrange("p (a b) -> p a b", b=shape[1])

        ARENA = 25288
        col_arena = top[0]
        arena = at("arena", [ARENA])
        HIDl = at("HIDl", [KD, T], col_arena, F32R)
        Ul1 = at("Ul1", [KD, T], col_arena + KD * T, F32R)
        pth = at("pth", [2, S], col_arena + 2 * KD * T, F32R)
        ptl = at("ptl", [2, S], col_arena + 2 * KD * T + 2 * S, F32R)
        taken = [0]

        def carve(*shape, rows=P):
            size = int(np.prod(shape))
            view = arena[0:rows, taken[0]:taken[0] + size]
            taken[0] += size
            assert taken[0] <= ARENA, taken[0]
            return view if len(shape) == 1 else view.rearrange("p (a b) -> p a b", b=shape[1])

        ka = carve(S)
        vaT = carve(S)
        va = carve(QB, P)
        qa = carve(S)
        qb = carve(S)
        kb = carve(S)
        vbT = carve(S)
        vb = carve(QB, P)
        bw = carve(4, BW)
        ss = carve(2 * QB, S).rearrange("p (i b) s -> p i b s", i=2)
        eT = carve(2, 512)
        otok = carve(QB, D)
        tab = carve(16, rows=32)
        oneh = carve(REL, rows=32)
        addm = carve(REL, rows=16)
        brow = carve(REL, rows=16)
        pt = carve(2, S)
        nmax = few(2, 4)
        nms = few(2, 4)
        srel = few(2, 4)
        esink = few(2, 4)
        den = few(2, 4)
        den2 = few(2, 4)
        rinv = few(2, 4)
        sinks = few(8)
        nsinks = few(8)
        ss8 = few(8)
        rms8 = few(8)
        r8 = few(8)

        taken[0] = 0
        gates = carve(24, T)
        za = carve(4, T)
        zc = carve(4, T)
        hc = carve(CONV_TILES, TAPS - 1 + T)
        zb = arena[:, taken[0] - CONV_TILES * (TAPS - 1 + T):][:, 0:4 * T].rearrange("p (a b) -> p a b", b=T)
        mlaw = M[:, 6:8, :].rearrange("p k t -> p (k t)")[:, 0:CH]
        amat = carve(CHUNKS_G, GCH)
        atail = carve(META, rows=META)
        cq = carve(2, T)
        ckv = carve(T)
        kraw = carve(T)
        cosT = carve(T, rows=QK)
        sinT = carve(T, rows=QK)
        triT = carve(640)
        shared = taken[0]
        vtok = carve(CHUNKS_G + 1, GCH)
        kft = carve(CHUNKS_G, GCH)
        state = carve(CHUNKS_G + 1, GCH)
        taken[0] = shared
        vt = carve(QT, P)
        eT2 = carve(2, 512)
        pairf = U[:, :, :].rearrange("p k t -> p (k t)")[:, 0:(LEVELS + 1) * GCH]
        pairm = sb("pairm", [P, (LEVELS + 1) * GCH], U8)
        Ms = [M[:, k, :] for k in range(KD)]
        Hs = [HID[:, k, :] for k in range(KD)]
        Us = [U[:, k, :] for k in range(KD)]
        kk, pre, suf, qg_, vT, gs, oT, qfull = Ms
        kfull = Hs[0]
        lq = [Hs[1], Hs[2]]
        lk = [Hs[3], Hs[4]]
        gsq = Hs[7]
        qgain, kgain, rot1 = [u[0:QK] for u in Us[0:3]]
        qh_of, kh_of = [[u[0:QK] for u in Us[i:i + 2]] for i in (3, 5)]
        tails = [Ms[5], Us[7]]

        def exps_of(hd, i):
            return Hs[4 * hd + i] if i < QT - 1 else tails[hd][0:META]

        TRB = (7, 5)
        qsq, ksq = relu[0:QK, 0, :], relu[0:QK, 1, :]
        otok2 = M[:, :, :].rearrange("p k t -> p (k t)")[:, 0:QT * 512].rearrange("p (i c) -> p i c", i=QT)
        lb_max, lb_sum, oml = (few(4) for _ in range(3))
        lb_e = few(2, 4)
        mu = relu[:, 1, :]
        qmax, qden, qinv = (few(2, QT) for _ in range(3))
        roots = few(3, T2_TILES)
        inverses = few(2, T2_TILES)
        headcol = few(2)
        bias_dram = nc.dram_tensor("bias_rows", (16, REL), F32, kind="Internal").ap()
        bias_slide = bass.AP(tensor=bias_dram.tensor, offset=0, ap=[[REL, 16], [1, P], [1, BW]])

        stage_full = [sem(f"stage_full{j}") for j in range(STAGE)]
        stage_free = [sem(f"stage_free{j}") for j in range(STAGE)]
        w_lead_ready = sem("w_lead_ready")
        w_split = sem("w_split")
        whole_ready = sem("whole_ready")
        lead_ready = sem("lead_ready")
        vec_in = sem("vec_in")
        x_in = sem("x_in")
        bias_in = sem("bias_in")
        brow_ready = sem("brow_ready")
        brow_out = sem("brow_out")
        bw_in = sem("bw_in")
        bw_used = sem("bw_used")
        consts = sem("consts")
        unit_done = [sem(f"unit_done{b}") for b in range(2)]
        unit_free = [sem(f"unit_free{b}") for b in range(2)]
        sq_ready = sem("sq_ready")
        rms_ready = sem("rms_ready")
        inv_ready = sem("inv_ready")
        sum_ready = sem("sum_ready")
        spread_done = sem("spread_done")
        u_ready = sem("u_ready")
        h_ready = sem("h_ready")
        m_ready = sem("m_ready")
        pt_lead = sem("pt_lead")
        pt_ready = sem("pt_ready")
        m_zero = sem("m_zero")
        hid_ready = sem("hid_ready")
        gate_ready = sem("gate_ready")
        qkv_ready = sem("qkv_ready")
        s_done = [sem(f"scores_done{b}") for b in range(3)]
        s_free = [sem(f"scores_free{b}") for b in range(3)]
        tr_done = [sem(f"tr_done{b}") for b in range(2)]
        eT_ready = [sem(f"eT_ready{b}") for b in range(2)]
        max_ready = sem("max_ready")
        exp_ready = sem("exp_ready")
        o_done = sem("o_done")
        o_free = sem("o_free")
        r8_ready = sem("r8_ready")
        osq_ready = sem("osq_ready")
        on_ready = sem("on_ready")
        oT_ready = [sem(f"oT_ready{b}") for b in range(2)]
        out_done = sem("out_done")
        consts2_in = sem("consts2_in")
        layer_begun = sem("layer_begun")
        hc_padded = sem("hc_padded")
        lb_max_ready = sem("lb_max_ready")
        lb_exp_ready = sem("lb_exp_ready")
        sig_ready = sem("sig_ready")
        conv_ready = sem("conv_ready")
        mean_ready = sem("mean_ready")
        centred = sem("centred")
        ln_ready = sem("ln_ready")
        lnsig_ready = sem("lnsig_ready")
        c_ready = sem("c_ready")
        f_sig = sem("f_sig")
        q_ready = sem("q_ready")
        qg_ready = sem("qg_ready")
        v_ready = sem("v_ready")
        vtok_ready = sem("vtok_ready")
        level_ready = sem("level_ready")
        pair_done = [sem(f"pair_done{b}") for b in range(2)]
        pair_free = [sem(f"pair_free{b}") for b in range(2)]
        a_ready = sem("a_ready")
        kft_done = sem("kft_done")
        kft_ready = sem("kft_ready")
        upd_done = sem("upd_done")
        state_ready = sem("state_ready")
        go_done = sem("go_done")
        go_copied = sem("go_copied")
        gss_done = sem("gss_done")
        vtr_done = sem("vtr_done")
        zc_ready = sem("zc_ready")
        mlaw_in = sem("mlaw_in")
        mlaw_used = sem("mlaw_used")
        qk_raw = sem("qk_raw")
        qk_ready = sem("qk_ready")
        qk_free = sem("qk_free")
        vt_done = sem("vt_done")
        vt_ready = sem("vt_ready")
        c_done = [sem(f"causal_done{b}") for b in range(2)]
        c_free = [sem(f"causal_free{b}") for b in range(2)]
        qmax_ready = sem("qmax_ready")
        qexp_ready = sem("qexp_ready")
        ctr_done = [sem(f"ctr_done{b}") for b in range(2)]
        cT_ready = [sem(f"cT_ready{b}") for b in range(2)]
        co_done = sem("co_done")
        co_free = sem("co_free")
        ztail_done = sem("ztail_done")
        zb_ready = sem("zb_ready")
        m_done = sem("m_done")
        passed = sem("passed")

        T0 = Tokens(0, S, 1)
        T1 = Tokens(META, S, 1)

        def psum_of(b, tok, m=P):
            return ps[0:m, 2 * b:2 * b + tok.parts, 0:tok.width]

        T2 = Tokens(0, T, 2)
        ATT_PER, FF_PER, CONV_PER, GATE_PER, GREC_PER, MLA_PER, MIX_PER, FF2_PER, LAYER_PER = (LOOPS[x] for x in (
            "attention", "ff", "conv", "gates", "recurrence", "mla", "mix", "ff2", "layer"))

        def level_blocks(x, size, half):
            cols = T if 2 * size <= META else S
            return x[:, 0:cols].rearrange("p (n two b) -> p n two b", two=2, b=size)[:, :, half, :]

        def level_total(x, size, half):
            v = level_blocks(x, size, half)
            return v[:, :, size - 1:size].to_broadcast([P, v.shape[1], size])

        HEADS = ((True, 0), (True, 1), (False, 0), (False, 1))

        def key_blocks(banded, b):
            return range(max(0, b - 1), min(QB, b + 2)) if banded else range(QB)

        def copy_causal_tile(eng, n, i):
            tb = 0 if eng.engine == nc.scalar.engine else 1
            rows = P if i < QT - 1 else META
            eng.wait_ge(ctr_done[tb], n.next(ctr_done[tb]))
            whole = min(i + 1, QT - 1)
            last = None
            for keys, c0, c1 in ((P, 0, whole * rows),) + (((META, whole * rows, (whole + 1) * rows),) if i == QT - 1 else ()):
                dst, src = eT2[0:keys, tb, c0:c1], ps[0:keys, TRB[tb], c0:c1]
                last = eng.activation(dst, src, ACT.Copy) if tb == 0 else eng.tensor_copy(dst, src)
            last.then_inc(cT_ready[tb], 1)

        block = ctx.enter_context(nc.Block())

        @block.sync
        def _(sp):
            for j in range(STAGE):
                sp.dma_start(stage[:, j, :], w[j]).then_inc(stage_full[j], 16)
            with sp.Fori(1, (N1_CHUNKS + LAYERS * N2_CHUNKS + AHEAD) // STAGE) as i:
                for j in range(STAGE):
                    sp.wait_ge(stage_free[j], i)
                    sp.dma_start(stage[:, j, :], w[bass.ds(STAGE * i + j, 1)].rearrange("o p n -> p (o n)")).then_inc(stage_full[j], 16)

        @block.gpsimd
        def _(pool):
            pool.memset(ones[:, :], 1.0)
            pool.memset(ident[:, :], 0.0)
            pool.drain()
            pool.affine_select(out=ident[:, :], in_=ident[:, :], compare_op=ALU.not_equal, fill=1.0, base=0,
                               pattern=[[-1, P]], channel_multiplier=1)
            pool.drain().then_inc(consts, 1)
            n = Counts(pool)
            pool.wait_ge(brow_ready, 1)
            pool.dma_start(bias_dram, brow[:, :]).then_inc(brow_out, 16)
            pool.wait_ge(brow_out, 16)
            with n.loop(4, {"bw_used": 1}) as t:
                pool.wait_ge(bw_used, n.next(bw_used))
                for j, row in enumerate((t, t + 4, 2 * t + 8, 2 * t + 9)):
                    pool.dma_start(bw[:, j, :], bias_slide[bass.ds(row, 1)].rearrange("o p c -> p (o c)")).then_inc(bw_in, 16)

            def rest_of_weights(count):
                with n.loop(count // 2, {w_lead_ready.name: 2}):
                    for j in range(2):
                        pool.wait_ge(w_lead_ready, n.next(w_lead_ready))
                        pool.tensor_tensor(wl[:, j, :], stage[:, j, :], wh[:, j, :].bitcast(F32), ALU.subtract).then_inc(w_split, 1)
                        pool.drain().then_inc(stage_free[j], 1)

            rest_of_weights(KD + AHEAD)
            pool.wait_ge(h_ready, KD)
            pool.memset(M[:, :, META:], 0.0).then_inc(m_zero, 1)
            rest_of_weights(16 * FF_GROUPS + KD + 2)
            pool.wait_ge(h_ready, 3 * KD)
            pool.memset(amat, 0.0)
            pool.memset(atail, 0.0)
            pool.drain().then_inc(consts, 1)
            for dst, src in ((cosT, cosines), (sinT, sines), (triT, causal), (rotm[:, :], turn), (pairf, pairs),
                             (v2all[:, :, :], vec2)):
                pool.dma_start(dst, src).then_inc(consts2_in, 16)
            with n.loop(LAYERS, LAYER_PER) as layer:
                pool.wait_ge(layer_begun, n.next(layer_begun))
                pool.sem_inc(passed, 1)
                pool.memset(hc[:, :, 0:TAPS - 1], 0.0).then_inc(hc_padded, 1)
                rest_of_weights(8 + 24 + 4 - AHEAD)
                with n.loop(4, MLA_PER) as pair:
                    pool.wait_ge(mlaw_used, n.next(mlaw_used))
                    pool.dma_start(mlaw, w_mla[bass.ds(layer * 4 + pair, 1)].rearrange("o p c -> p (o c)")).then_inc(mlaw_in, 16)
                pool.wait_ge(mlaw_used, n.next(mlaw_used))
                pool.sem_inc(passed, 1)
                rest_of_weights(KD + 16 * FF_GROUPS + AHEAD)

        @block.tensor
        def _(pe):
            n = Counts(pe)
            at = {"chunk": 0, "unit": 0}

            def chunk():
                slot = at["chunk"] % STAGE
                at["chunk"] += 1
                pe.wait_ge(stage_full[slot], n.next(stage_full[slot], 16))
                return [stage[:, slot, j * P:(j + 1) * P] for j in range(8)]

            def split_chunk():
                slot = at["chunk"] % STAGE
                at["chunk"] += 1
                n.next(stage_full[slot], 16)
                pe.wait_ge(w_split, n.next(w_split))
                return [[half[:, slot, j * P:(j + 1) * P] for half in (wh, wl)] for j in range(8)]

            def unit(weights, acts, tok, m=P, ready=None, frees=None):
                b = at["unit"] % 2
                at["unit"] += 1
                pe.wait_ge(unit_free[b], n.next(unit_free[b]))
                for k, (wt, a) in enumerate(zip(weights, acts)):
                    if ready is not None:
                        pe.wait_ge(ready, n.next(ready))
                    for h in range(tok.parts):
                        mm = pe.matmul(ps[0:m, 2 * b + h, 0:tok.width], wt, tok.part(a, h),
                                       start=(k == 0), stop=(k == len(acts) - 1))
                        if frees is not None and k == 0 and h == 0:
                            mm.then_inc(frees, 1)
                mm.then_inc(unit_done[b], 1)

            def split_unit(weights, acts, tok, ready=None):
                b = at["unit"] % 2
                at["unit"] += 1
                pe.wait_ge(unit_free[b], n.next(unit_free[b]))
                for k, ((w_lead, w_rest), (a_lead, a_rest)) in enumerate(zip(weights, acts)):
                    if ready is not None:
                        pe.wait_ge(ready, n.next(ready))
                    for h in range(tok.parts):
                        dst = ps[:, 2 * b + h, 0:tok.width]
                        pe.matmul(dst, w_lead, tok.part(a_lead, h), start=(k == 0), stop=False)
                        pe.matmul(dst, w_lead, tok.part(a_rest, h), start=False, stop=False)
                        mm = pe.matmul(dst, w_rest, tok.part(a_lead, h), start=False, stop=(k == len(acts) - 1))
                mm.then_inc(unit_done[b], 1)

            def project(acts, tok, count, ready=None):
                for m in range(count):
                    frees = stage_free[(at["chunk"] - 1) % STAGE] if m > 0 else None
                    unit(chunk(), acts, tok, ready=ready if m == 0 else None, frees=frees)
                pe.drain().then_inc(stage_free[(at["chunk"] - 1) % STAGE], 1)

            def split_project(acts, tok, count, ready=None):
                for m in range(count):
                    split_unit(split_chunk(), acts, tok, ready=ready if m == 0 else None)

            def keep_warm(bank, count):
                for _ in range(count):
                    pe.matmul(ps[:, bank, 0:2 * P], ident[:, :], ones[:, 0:1].to_broadcast([P, 2 * P]), start=True, stop=True)

            def sums_into(bank, srcs, tok, m=P, ready=None, warm=0):
                keep_warm(bank, warm)
                for k, src in enumerate(srcs):
                    if ready is not None:
                        pe.wait_ge(ready, n.next(ready))
                    for i in range(tok.tiles):
                        c = tok.start + i * tok.rows
                        mm = pe.matmul(ps[0:tok.rows, bank, i:i + 1], src[0:m, c:c + tok.rows], ones[0:m, 0:1],
                                       start=(k == i == 0), stop=(k == len(srcs) - 1 and i == tok.tiles - 1))
                return mm

            def spread_into(bank, tok, side=0, m=P, warm=0):
                keep_warm(bank, warm)
                pe.wait_ge(inv_ready, n.next(inv_ready))
                each = tok.tiles // tok.parts
                for i in range(tok.tiles):
                    mm = pe.matmul(ps[0:m, bank + i // each, i % each * tok.rows:(i % each + 1) * tok.rows],
                                   inverses[0:tok.rows, side, i:i + 1].to_broadcast([tok.rows, m]),
                                   ident[0:tok.rows, 0:tok.rows], start=True, stop=True)
                return mm

            def as_unit(make, *args, **kwargs):
                b = at["unit"] % 2
                at["unit"] += 1
                pe.wait_ge(unit_free[b], n.next(unit_free[b]))
                make(2 * b, *args, **kwargs).then_inc(unit_done[b], 1)

            def inverse_rms(srcs, tok, ready=sq_ready):
                as_unit(sums_into, srcs, tok, ready=ready)
                as_unit(spread_into, tok)

            def sum_squares(tok, count=KD):
                n.next(sq_ready, count)
                inverse_rms([HID[:, 0, :]], tok, ready=sum_ready)

            Uk = [U[:, k, :] for k in range(KD)]
            U1k = [(Uh[:, k, :], Ul1[:, k, :]) for k in range(KD)]
            U2k = [(Uh[:, k, :], Ul2[:, k, :]) for k in range(KD)]
            HIDk = [(HIDh[:, k, :], HIDl[:, k, :]) for k in range(KD)]
            pe.wait_ge(consts, 1)
            pe.wait_ge(bias_in, 48)
            for h in range(2):
                b = at["unit"] % 2
                at["unit"] += 1
                pe.wait_ge(unit_free[b], n.next(unit_free[b]))
                pe.matmul(ps[0:16, 2 * b, 0:512], tab[:, :], oneh[:, h * 512:(h + 1) * 512],
                          start=True, stop=True).then_inc(unit_done[b], 1)

            sum_squares(T1)
            project(Uk, T1, 1, ready=u_ready)
            project(Uk, T1, 1)
            tr = [0]

            def transposed(b, blocks):
                for j, src in enumerate(blocks):
                    mm = pe.transpose(ps[0:src.shape[-1], 1 + 2 * b, j * P:j * P + src.shape[0]], src, ident[0:src.shape[0], 0:src.shape[0]])
                mm.then_inc(tr_done[b], 1)

            def transpose_values(src):
                for b in range(2):
                    transposed(b, [src[:, (2 * b + j) * P:(2 * b + j + 1) * P] for j in range(2)])
                for b in range(2):
                    pe.wait_ge(eT_ready[b], n.next(eT_ready[b]))

            pe.wait_ge(qkv_ready, n.next(qkv_ready, 2))
            transpose_values(vaT)
            assert at["unit"] % 2 == 0

            def scores(hd):
                banded, half = HEADS[hd]
                q, k = (qa, ka) if banded else (qb, kb)
                rows = slice(64 * half, 64 * half + 64)
                for b in range(QB):
                    u = (hd * QB + b) % 3
                    keys = key_blocks(banded, b)
                    pe.wait_ge(s_free[u], n.next(s_free[u]))
                    pe.matmul(ps[:, 4 + u, 0:len(keys) * P], q[rows, b * P:(b + 1) * P],
                              k[rows, keys[0] * P:(keys[-1] + 1) * P], start=True, stop=True).then_inc(s_done[u], 1)

            def transpose_exps(hd, b):
                keys = key_blocks(HEADS[hd][0], b)
                transposed(b % 2, [ss[:, hd % 2, b, j * P:(j + 1) * P] for j in range(len(keys))])

            def weigh(hd, b):
                banded, half = HEADS[hd]
                v = va if banded else vb
                keys = key_blocks(banded, b)
                pe.wait_ge(eT_ready[b % 2], n.next(eT_ready[b % 2]))
                for j, kblock in enumerate(keys):
                    mm = pe.matmul(ps[:, 7, b * DH:(b + 1) * DH], eT[:, b % 2, j * P:(j + 1) * P],
                                   v[:, kblock, 64 * half:64 * half + 64], start=(j == 0), stop=(j == len(keys) - 1))
                return mm

            def attend(hd):
                pe.wait_ge(exp_ready, n.next(exp_ready))
                transpose_exps(hd, 0)
                pe.wait_ge(o_free, n.next(o_free))
                for b in range(QB):
                    if b + 1 < QB:
                        transpose_exps(hd, b + 1)
                    mm = weigh(hd, b)
                mm.then_inc(o_done, 1)

            def heads(following):
                pe.wait_ge(qkv_ready, n.next(qkv_ready, 4))
                transpose_values(vbT)
                scores(0)
                scores(1)
                if following:
                    project(Uk, T1, 1)
                attend(0)
                scores(2)
                attend(1)
                scores(3)
                if following:
                    project(Uk, T1, 1)
                attend(2)
                if following:
                    project(Uk, T1, 1)
                attend(3)
                if following:
                    project(Uk, T1, 1)

            project(Uk, T1, 4)
            with n.loop(3, ATT_PER):
                heads(True)
            heads(False)

            pe.wait_ge(on_ready, n.next(on_ready))
            for f in range(KD):
                if f >= 2:
                    pe.wait_ge(oT_ready[f % 2], n.next(oT_ready[f % 2]))
                transposed(f % 2, [otok[:, b, f * P:(f + 1) * P] for b in range(QB)])
            split_project(U1k, T1, KD, ready=u_ready)
            sum_squares(T1)

            sum_squares(T1)
            first = True
            split_project(U1k, T1, KD, ready=u_ready)
            split_project(HIDk, T1, KD, ready=hid_ready)
            with n.loop(FF_GROUPS - 1, FF_PER):
                split_project(U1k, T1, KD)
                split_project(HIDk, T1, KD, ready=hid_ready)
            sum_squares(T1)

            split_project(U1k, T1, KD, ready=u_ready)
            pe.wait_ge(pt_ready, 1)
            for m in range(KD):
                if m % 4 == 0:
                    tiles = split_chunk()
                split_unit(tiles[2 * (m % 4):2 * (m % 4) + 2], [(pth[:, k, :], ptl[:, k, :]) for k in range(2)], T0)
            sum_squares(T1)

            ZA, ZB, ZC = ([z[:, k, :] for k in range(4)] for z in (za, zb, zc))

            def pair_products(level):
                b = level % 2
                lhs, rhs = (kk, qg_) if level == 0 else (lk[level % 2], lq[level % 2])
                pe.wait_ge(pair_free[b], n.next(pair_free[b]))
                if level > 0:
                    pe.wait_ge(level_ready, n.next(level_ready))
                if level <= 4:
                    pe.matmul(ps[0:META, 6, level * META:(level + 1) * META], lhs[:, S:T], rhs[:, S:T], start=True, stop=True)
                for c in range(CHUNKS_G):
                    mm = pe.matmul(ps[:, 4 + b, c * GCH:(c + 1) * GCH], lhs[:, c * GCH:(c + 1) * GCH],
                                   rhs[:, c * GCH:(c + 1) * GCH], start=True, stop=True)
                mm.then_inc(pair_done[b], 1)

            pe.wait_ge(consts, 2)
            pe.wait_ge(consts2_in, 16 * 6)
            with n.loop(LAYERS, LAYER_PER) as layer:
                sum_squares(T2)
                split_project(U2k, T2, 8, ready=u_ready)
                with n.loop(6, GATE_PER):
                    split_project(U2k, T2, 4)
                split_project(U2k, T2, 4)
                unit([ones[:, :]] * 4, ZA, T2, ready=conv_ready)
                sum_squares(T2, 4)
                inverse_rms([Hs[4], Hs[5]], T2)
                inverse_rms([Hs[6]], T2)
                pe.wait_ge(u_ready, n.next(u_ready, KD))
                pe.sem_inc(passed, 1)
                def recur(following):
                    pe.wait_ge(v_ready, n.next(v_ready))
                    for c in range(CHUNKS_G):
                        pe.transpose(ps[:, 7, c * GCH:(c + 1) * GCH], vT[:, c * GCH:(c + 1) * GCH], ident[:, :])
                    pe.transpose(ps[0:META, 6, 2 * P:3 * P], vT[:, S:T], ident[:, :]).then_inc(vtr_done, 1)
                    pe.wait_ge(vtok_ready, n.next(vtok_ready))
                    pe.wait_ge(qg_ready, n.next(qg_ready))
                    pair_products(0)
                    for level in range(1, LEVELS + 1):
                        pair_products(level)
                        if following and level in (2, 5):
                            project(Uk, T2, 1)
                    pe.wait_ge(a_ready, n.next(a_ready))
                    for c in range(CHUNKS_G):
                        mm = pe.transpose(ps[:, 7, c * GCH:(c + 1) * GCH], kfull[:, c * GCH:(c + 1) * GCH], ident[:, :])
                    mm.then_inc(kft_done, 1)
                    if following:
                        project(Uk, T2, 1)
                    pe.wait_ge(kft_ready, n.next(kft_ready))
                    for c in range(CHUNKS_G):
                        mm = pe.matmul(ps[:, 6, c * GCH:(c + 1) * GCH], kft[:, c, :], vtok[:, c, :], start=True, stop=True)
                    mm.then_inc(upd_done, 1)
                    pe.wait_ge(state_ready, n.next(state_ready))
                    for c in range(CHUNKS_G + 1):
                        rows, cols = (GCH, slice(c * GCH, (c + 1) * GCH)) if c < CHUNKS_G else (META, slice(S, T))
                        dst = ps[:, 4, cols] if c < CHUNKS_G else ps[:, 5, 0:META]
                        inner = amat[:, c, :] if c < CHUNKS_G else atail
                        mm = pe.matmul(dst, vtok[0:rows, c, :], inner, start=True, stop=(c == 0))
                        if c > 0:
                            mm = pe.matmul(dst, state[:, c, :], qfull[:, cols], start=False, stop=True)
                    mm.then_inc(go_done, 1)
                    if following:
                        project(Uk, T2, 1)
                    keep_warm(7, 2)
                    pe.wait_ge(go_copied, n.next(go_copied))
                    sums_into(6, [gsq], T2).then_inc(gss_done, 1)
                    spread_into(6, T2).then_inc(spread_done, 1)

                project(Uk, T2, 4)
                with n.loop(HEADS_G - 1, GREC_PER):
                    recur(True)
                recur(False)

                def causal_scores(hd):
                    for i in range(QT - 1):
                        b = i % 2
                        pe.wait_ge(c_free[b], n.next(c_free[b]))
                        pe.matmul(ps[:, 4 + b, 0:(i + 1) * P], qh_of[hd][:, i * P:(i + 1) * P],
                                  kh_of[hd][:, 0:(i + 1) * P], start=True, stop=True).then_inc(c_done[b], 1)
                    for b in range(2):
                        pe.wait_ge(c_free[b], n.next(c_free[b]))
                        pe.matmul(ps[0:META, 4 + b, 0:T2.width], qh_of[hd][:, S:T], T2.part(kh_of[hd], b),
                                  start=True, stop=True).then_inc(c_done[b], 1)

                def causal_transpose(hd, i):
                    tb = (hd * QT + i) % 2
                    rows = P if i < QT - 1 else META
                    e = exps_of(hd, i)
                    for j in range(i + 1):
                        keys = P if j < QT - 1 else META
                        mm = pe.transpose(ps[0:keys, TRB[tb], j * rows:(j + 1) * rows], e[:, j * P:j * P + keys], ident[0:rows, 0:rows])
                    mm.then_inc(ctr_done[tb], 1)

                def causal_weigh(hd, i):
                    tb = (hd * QT + i) % 2
                    rows = P if i < QT - 1 else META
                    pe.wait_ge(cT_ready[tb], n.next(cT_ready[tb]))
                    for j in range(i + 1):
                        keys = P if j < QT - 1 else META
                        mm = pe.matmul(ps[0:rows, 6, i * DH:(i + 1) * DH], eT2[0:keys, tb, j * rows:(j + 1) * rows],
                                       vt[0:keys, j, hd * DH:(hd + 1) * DH], start=(j == 0), stop=(j == i))
                    return mm

                pe.wait_ge(c_ready, n.next(c_ready))
                pe.wait_ge(zc_ready, n.next(zc_ready))
                pe.sem_inc(passed, 1)
                def tile(j):
                    return mlaw[:, j * P:(j + 1) * P]

                def raw_queries_keys(hd):
                    unit([tile(3 * hd)[:, 0:QK], tile(3 * hd + 1)[:, 0:QK]], [cq[:, 0, :], cq[:, 1, :]], T2, m=QK)
                    unit([tile(3 * hd + 2)[:, 0:NOPE]], [ckv], T2, m=NOPE)

                def sums_and_rotations():
                    as_unit(sums_into, [qsq], T2, m=QK, ready=qk_raw, warm=2)
                    unit([rotm[:, :]], [qgain], T2, m=QK)
                    as_unit(sums_into, [ksq], T2, m=QK, ready=qk_raw, warm=1)
                    unit([rotm[:, :]], [kgain], T2, m=QK)
                    for side in range(2):
                        as_unit(spread_into, T2, side, m=QK, warm=1 if side == 0 else 0)

                def values():
                    pe.wait_ge(c_free[0], n.now(c_free[0]) + 1)
                    for j in range(QT):
                        rows = P if j < QT - 1 else META
                        dst = ps[0:rows, 7, j * P:(j + 1) * P] if j < QT - 1 else ps[0:rows, 4, 0:P]
                        mm = pe.matmul(dst, ckv[:, j * P:j * P + rows], tile(6), start=True, stop=True)
                    mm.then_inc(vt_done, 1)
                    pe.drain().then_inc(mlaw_used, 1)

                def all_scores(following):
                    pe.wait_ge(vt_ready, n.next(vt_ready))
                    pe.wait_ge(qk_ready, n.next(qk_ready, 2))
                    causal_scores(0)
                    if following:
                        pe.wait_ge(mlaw_in, n.next(mlaw_in, 16))
                        raw_queries_keys(0)
                    causal_scores(1)

                def causal_attend(hd):
                    pe.wait_ge(qexp_ready, n.next(qexp_ready))
                    if hd == 0:
                        pe.wait_ge(c_free[1], n.now(c_free[1]) + 1)
                    keep_warm(TRB[0], 3)
                    causal_transpose(hd, 0)
                    pe.wait_ge(co_free, n.next(co_free))
                    for i in range(QT):
                        if i + 1 < QT:
                            causal_transpose(hd, i + 1)
                        mm = causal_weigh(hd, i)
                    mm.then_inc(co_done, 1)

                pe.wait_ge(mlaw_in, n.next(mlaw_in, 16))
                for hd in range(2):
                    raw_queries_keys(hd)
                    sums_and_rotations()
                values()
                with n.loop(3, MLA_PER):
                    all_scores(True)
                    causal_attend(0)
                    sums_and_rotations()
                    raw_queries_keys(1)
                    causal_attend(1)
                    sums_and_rotations()
                    values()
                all_scores(False)
                causal_attend(0)
                causal_attend(1)

                pe.wait_ge(co_free, n.now(co_free) + 1)
                for f in range(4):
                    tb = f % 2
                    if f >= 2:
                        pe.wait_ge(cT_ready[tb], n.next(cT_ready[tb]))
                    for j in range(QT - 1):
                        mm = pe.transpose(ps[:, TRB[tb], j * P:(j + 1) * P], otok2[:, j, f * P:(f + 1) * P], ident[:, :])
                    mm.then_inc(ctr_done[tb], 1)
                    mm = pe.transpose(ps[:, 6, f * META:(f + 1) * META], otok2[0:META, QT - 1, f * P:(f + 1) * P], ident[0:META, 0:META])
                mm.then_inc(ztail_done, 1)
                for tb in range(2):
                    pe.wait_ge(cT_ready[tb], n.next(cT_ready[tb]))
                pe.wait_ge(zb_ready, n.next(zb_ready))
                pe.sem_inc(passed, 1)
                with n.loop(4, MIX_PER):
                    for j in range(2):
                        tiles = chunk()
                        unit(tiles[0:4], ZA, T2, frees=stage_free[1] if j > 0 else None)
                        unit(tiles[4:8], ZB, T2)
                        tiles = chunk()
                        unit(tiles[0:4], ZC, T2, frees=stage_free[0])
                    pe.drain().then_inc(stage_free[1], 1)
                pe.wait_ge(m_done, n.next(m_done, 1))
                split_project([(Mh[:, k, :], Ml[:, k, :]) for k in range(KD)], T2, KD)
                sum_squares(T2)
                split_project(U2k, T2, KD, ready=u_ready)
                split_project(HIDk, T2, KD, ready=hid_ready)
                with n.loop(FF_GROUPS - 1, FF2_PER):
                    split_project(U2k, T2, KD)
                    split_project(HIDk, T2, KD, ready=hid_ready)

        @block.scalar
        def _(act):
            n = Counts(act)
            at = {"unit": 0, "chunk": 0}

            def take():
                b = at["unit"] % 2
                at["unit"] += 1
                return b, n.next(unit_done[b])

            def pass_chunks(count):
                for _ in range(count):
                    n.next(stage_full[at["chunk"] % STAGE], 16)
                    at["chunk"] += 1

            def split_weights():
                slot = at["chunk"] % STAGE
                at["chunk"] += 1
                act.wait_ge(stage_full[slot], n.next(stage_full[slot], 16))
                act.activation(wh[:, slot, :], stage[:, slot, :], ACT.Copy).then_inc(w_lead_ready, 1)

            def used_up(split=True):
                b, done = take()
                act.wait_ge(unit_done[b], done)
                if split:
                    split_weights()
                return b

            def split_inputs(src, tok):
                for k in range(KD):
                    act.wait_ge(whole_ready, n.next(whole_ready))
                    act.activation(tok.of(Uh[:, k, :]), tok.of(src[:, k, :]), ACT.Copy).then_inc(lead_ready, 1)

            act.dma_start(v1[:, :], vec1).then_inc(vec_in, 16)
            act.dma_start(sinks[:, :], sink.to_broadcast([P, 8])).then_inc(vec_in, 16)
            act.dma_start(tab[:, :], table).then_inc(bias_in, 16)
            act.dma_start(oneh[:, :], onehot).then_inc(bias_in, 16)
            act.dma_start(addm[:, :], addmask).then_inc(bias_in, 16)
            act.dma_start(H[:, :, META:], xT).then_inc(x_in, 16)
            act.dma_start(H[:, :, 0:META], metaT).then_inc(x_in, 16)
            act.dma_start(pt[:, :, :], pT).then_inc(x_in, 16)

            def root_mean(tok, count, side=0):
                b, done = take()
                act.wait_ge(unit_done[b], done)
                act.activation(roots[0:tok.rows, side, 0:tok.tiles], ps[0:tok.rows, 2 * b, 0:tok.tiles], ACT.Sqrt,
                               bias=EPS, scale=1.0 / count).then_inc(unit_free[b], 1)
                act.drain().then_inc(rms_ready, 1)
                take()

            def squares(src, tok, ready=None, free=None):
                for k in range(KD):
                    if ready is not None:
                        act.wait_ge(ready, n.next(ready))
                    act.activation(tok.of(HID[:, k, :]), tok.of(src[:, k, :]), ACT.Square).then_inc(sq_ready, 1)

            act.wait_ge(x_in, 48)
            take()
            take()
            squares(H, T1)
            root_mean(T1, D)

            def evacuate(dst, tok, func=ACT.Copy, bias=0.0, flip=False, ready=None, split=False):
                b = used_up(split)
                src = psum_of(b, tok)
                if flip:
                    src = ps[:, 2 * b, :].rearrange("p (b q) -> p b q", q=P)[:, :, ::-1]
                    dst = dst.rearrange("p (b q) -> p b q", q=P)
                else:
                    dst = tok.of(dst)
                act.activation(dst, src, func, bias=bias).then_inc(unit_free[b], 1)
                if ready is not None:
                    act.drain().then_inc(ready, 1)

            pass_chunks(2)
            evacuate(ka, T0, ready=qkv_ready)
            evacuate(vaT, T0, ready=qkv_ready)

            def copy_values(dst):
                act.wait_ge(tr_done[0], n.next(tr_done[0]))
                act.activation(dst[:, 0:2, :], ps[:, 1, 0:2 * P].rearrange("p (j d) -> p j d", d=P), ACT.Copy).then_inc(eT_ready[0], 1)

            copy_values(va)

            def exps(hd):
                banded, half = HEADS[hd]
                act.wait_ge(max_ready, n.next(max_ready))
                for b in range(QB):
                    e = ss[:, hd % 2, b, 0:len(key_blocks(banded, b)) * P]
                    act.activation(e, e, ACT.Exp, bias=(nms if banded else nmax)[:, hd % 2, b:b + 1],
                                   accum_out=den[:, hd % 2, b:b + 1])
                if banded:
                    act.activation(esink[:, hd % 2, :], srel[:, hd % 2, :], ACT.Exp)
                act.drain().then_inc(exp_ready, 1)

            def copy_exps(hd):
                for b in (0, 2):
                    act.wait_ge(tr_done[0], n.next(tr_done[0]))
                    wd = len(key_blocks(HEADS[hd][0], b)) * P
                    act.activation(eT[:, 0, 0:wd], ps[:, 1, 0:wd], ACT.Copy).then_inc(eT_ready[0], 1)

            def heads(following):
                copy_values(vb)
                exps(0)
                exps(1)
                copy_exps(0)
                if following:
                    pass_chunks(4)
                    evacuate(qa, T0, flip=True, ready=qkv_ready)
                exps(2)
                copy_exps(1)
                exps(3)
                copy_exps(2)
                if following:
                    evacuate(qb, T0, flip=True, ready=qkv_ready)
                copy_exps(3)
                if following:
                    evacuate(kb, T0, ready=qkv_ready)
                    evacuate(vbT, T0, ready=qkv_ready)

            pass_chunks(4)
            evacuate(qa, T0, flip=True, ready=qkv_ready)
            evacuate(qb, T0, flip=True, ready=qkv_ready)
            evacuate(kb, T0, ready=qkv_ready)
            evacuate(vbT, T0, ready=qkv_ready)
            with n.loop(3, ATT_PER):
                heads(True)
            heads(False)

            act.wait_ge(o_free, 1 + 16)
            for b in range(QB):
                for half in range(2):
                    act.activation(ss[:, half, b, :], otok[:, b, half * 512:(half + 1) * 512], ACT.Square,
                                   accum_out=ss8[:, 2 * b + half:2 * b + half + 1])
            act.drain()
            act.activation(rms8[:, :], ss8[:, :], ACT.Sqrt, bias=EPS, scale=1.0 / 512)
            act.drain().then_inc(osq_ready, 1)
            for _ in range(AHEAD):
                split_weights()
            for f in range(KD):
                if f % 2 == 0:
                    act.wait_ge(tr_done[0], n.next(tr_done[0]))
                    act.activation(HID[:, f, META:].rearrange("p (b q) -> p b q", q=P),
                                   ps[:, 1, :].rearrange("p (b q) -> p b q", q=P)[:, :, ::-1], ACT.Copy,
                                   scale=v1[:, V1["g_out"] + f:V1["g_out"] + f + 1]).then_inc(oT_ready[0], 1)
                    act.drain()
                else:
                    act.wait_ge(whole_ready, n.next(whole_ready))
                act.activation(T1.of(Uh[:, f, :]), T1.of(HID[:, f, :]), ACT.Copy).then_inc(lead_ready, 1)

            def out_and_squares(tok):
                for m in range(KD):
                    b = used_up()
                    act.activation(tok.of(M[:, m, :]), psum_of(b, tok), ACT.Copy)
                    act.activation(tok.of(HID[:, m, :]), psum_of(b, tok), ACT.Square).then_inc(unit_free[b], 1)
                    act.drain().then_inc(sq_ready, 1)

            out_and_squares(T1)
            root_mean(T1, D)
            squares(H, T1, ready=h_ready)
            root_mean(T1, D)
            split_inputs(HID, T1)
            with n.loop(FF_GROUPS, FF_PER):
                for m in range(KD):
                    used_up()
                for m in range(KD):
                    used_up()
            for k in range(2):
                act.activation(pth[:, k, :], pt[:, k, :], ACT.Copy)
            act.drain().then_inc(pt_lead, 1)
            squares(M, T1, ready=m_ready)
            root_mean(T1, D)
            split_inputs(H, T1)
            for m in range(KD):
                b = used_up()
                act.activation(T1.of(HID[:, m, :]), psum_of(b, T1), ACT.Sigmoid,
                               bias=v1[:, V1["b_gate"] + m:V1["b_gate"] + m + 1]).then_inc(unit_free[b], 1)
                act.drain().then_inc(gate_ready, 1)
            for m in range(KD):
                used_up(m % 4 == 3)
            squares(M, T1, ready=m_ready)
            root_mean(T1, D)
            n.next(h_ready, 2 * KD)

            with n.loop(LAYERS, LAYER_PER) as layer:
                act.wait_ge(layer_begun, n.next(layer_begun))
                act.wait_ge(lb_max_ready, n.next(lb_max_ready))
                act.activation(lb_e, lb_e, ACT.Exp).then_inc(lb_exp_ready, 1)
                squares(H, T2)
                root_mean(T2, D)
                split_inputs(HID, T2)
                with n.loop(2, CONV_PER):
                    for j in range(2):
                        evacuate(relu[:, j, :], T2, func=ACT.Sigmoid, ready=sig_ready, split=True)
                        used_up()
                with n.loop(6, GATE_PER) as g:
                    for j in range(4):
                        b = used_up()
                        act.activation(gates[:, bass.ds(4 * g + j, 1), :].rearrange("p o (h n) -> p (o h) n", h=2),
                                       psum_of(b, T2), ACT.Sigmoid).then_inc(unit_free[b], 1)
                for i, (dst, rows) in enumerate(((cq[:, 0, :], slice(0, P)), (cq[:, 1, :], slice(0, P)),
                                                 (ckv, slice(0, P)), (kraw, slice(NOPE, QK)))):
                    b = used_up(i < 4 - AHEAD)
                    act.activation(T2.of(dst[rows]), ps[rows, 2 * b:2 * b + 2, 0:T2.width], ACT.Copy).then_inc(unit_free[b], 1)
                b = used_up(False)
                act.activation(T2.of(mu), psum_of(b, T2), ACT.Copy, scale=1.0 / 512).then_inc(unit_free[b], 1)
                act.drain().then_inc(mean_ready, 1)
                act.wait_ge(centred, n.next(centred))
                for src, dst in ((za[:, 0, :], 0), (za[:, 1, :], 1), (za[:, 2, :], 2), (za[:, 3, :], 3),
                                 (cq[:, 0, :], 4), (cq[:, 1, :], 5), (ckv, 6)):
                    act.activation(Hs[dst], src, ACT.Square).then_inc(sq_ready, 1)
                root_mean(T2, 512)
                root_mean(T2, 256, side=1)
                root_mean(T2, P, side=2)
                act.wait_ge(ln_ready, n.next(ln_ready))
                for k in range(4):
                    act.activation(Hs[k], za[:, k, :], ACT.Sigmoid, bias=v2[:, V2["ln_b"] + k:V2["ln_b"] + k + 1])
                act.drain().then_inc(lnsig_ready, 1)

                def keep_sigmoid(dst):
                    b = used_up(False)
                    act.activation(T2.of(dst), psum_of(b, T2), ACT.Sigmoid)
                    act.drain().then_inc(sig_ready, 1)

                def forget_and_queries():
                    pass_chunks(4)
                    b = used_up(False)
                    act.activation(T2.of(relu[:, 0, :]), psum_of(b, T2), ACT.Sigmoid, scale=-1.0).then_inc(unit_free[b], 1)
                    act.drain().then_inc(f_sig, 1)
                    evacuate(relu[:, 1, :], T2, ready=q_ready)

                def recur(following):
                    act.wait_ge(vtr_done, n.next(vtr_done))
                    act.activation(vtok[:, 0:CHUNKS_G, :], ps[:, 7, :].rearrange("p (c d) -> p c d", d=P), ACT.Copy)
                    act.activation(vtok[0:META, CHUNKS_G, :], ps[0:META, 6, 2 * P:3 * P], ACT.Copy)
                    act.drain().then_inc(vtok_ready, 1)
                    if following:
                        forget_and_queries()
                    act.wait_ge(kft_done, n.next(kft_done))
                    act.activation(kft, ps[:, 7, :].rearrange("p (c d) -> p c d", d=P), ACT.Copy).then_inc(kft_ready, 1)
                    if following:
                        keep_sigmoid(Hs[6])
                    act.wait_ge(go_done, n.next(go_done))
                    for dst, func in ((oT, ACT.Copy), (gsq, ACT.Square)):
                        act.activation(dst[:, 0:S], ps[:, 4, :], func)
                        act.activation(dst[:, S:T], ps[:, 5, 0:META], func)
                    act.drain().then_inc(go_copied, 1)
                    if following:
                        keep_sigmoid(Hs[5])
                    act.wait_ge(gss_done, n.next(gss_done))
                    act.activation(roots[0:T2.rows, 0, :], ps[0:T2.rows, 6, 0:T2.tiles], ACT.Sqrt, bias=EPS, scale=1.0 / P)
                    act.drain().then_inc(rms_ready, 1)

                forget_and_queries()
                keep_sigmoid(Hs[6])
                keep_sigmoid(Hs[5])
                with n.loop(HEADS_G - 1, GREC_PER):
                    recur(True)
                recur(False)

                def causal_exps(hd):
                    act.wait_ge(qmax_ready, n.next(qmax_ready))
                    for i in range(QT):
                        rows = P if i < QT - 1 else META
                        e = exps_of(hd, i)[:, 0:min((i + 1) * P, T)]
                        act.activation(e, e, ACT.Exp, bias=qmax[0:rows, hd, i:i + 1], accum_out=qden[0:rows, hd, i:i + 1])
                    act.drain().then_inc(qexp_ready, 1)

                def copy_causal(hd):
                    for i in range(QT):
                        if (hd * QT + i) % 2 == 0:
                            copy_causal_tile(act, n, i)

                def copy_vt():
                    act.wait_ge(vt_done, n.next(vt_done))
                    act.activation(vt[:, 0:QT - 1, :], ps[:, 7, :].rearrange("p (c d) -> p c d", d=P), ACT.Copy)
                    act.activation(vt[0:META, QT - 1, :], ps[0:META, 4, 0:P], ACT.Copy)
                    act.drain().then_inc(vt_ready, 1)

                def raw_queries_keys():
                    act.wait_ge(qk_free, n.next(qk_free))
                    b = used_up(False)
                    act.activation(T2.of(qsq), psum_of(b, T2, QK), ACT.Square)
                    act.activation(T2.of(qgain), psum_of(b, T2, QK), ACT.Copy, scale=v2[0:QK, V2["q_norm"]:V2["q_norm"] + 1]).then_inc(unit_free[b], 1)
                    act.drain().then_inc(qk_raw, 1)
                    b = used_up(False)
                    act.activation(T2.of(kraw[0:NOPE]), psum_of(b, T2, NOPE), ACT.Copy).then_inc(unit_free[b], 1)
                    act.drain()
                    act.activation(ksq, kraw[0:QK], ACT.Square)
                    act.activation(kgain, kraw[0:QK], ACT.Copy, scale=v2[0:QK, V2["k_norm"]:V2["k_norm"] + 1])
                    act.drain().then_inc(qk_raw, 1)

                def qk_roots():
                    for side in range(2):
                        root_mean(T2, QK, side=side)
                    take()
                    take()

                for hd in range(2):
                    raw_queries_keys()
                    qk_roots()
                copy_vt()
                with n.loop(3, MLA_PER):
                    causal_exps(0)
                    raw_queries_keys()
                    copy_causal(0)
                    causal_exps(1)
                    qk_roots()
                    raw_queries_keys()
                    copy_causal(1)
                    qk_roots()
                    copy_vt()
                causal_exps(0)
                causal_exps(1)
                copy_causal(0)
                copy_causal(1)
                for f in (0, 2):
                    act.wait_ge(ctr_done[0], n.next(ctr_done[0]))
                    act.activation(zb[:, f, 0:S], ps[:, TRB[0], :], ACT.Copy).then_inc(cT_ready[0], 1)
                act.wait_ge(ztail_done, n.next(ztail_done))
                act.activation(zb[:, :, S:T], ps[:, 6, 0:4 * META].rearrange("p (f t) -> p f t", f=4), ACT.Copy).then_inc(zb_ready, 1)
                with n.loop(4, MIX_PER):
                    pass_chunks(4)
                    for _ in range(6):
                        take()
                for _ in range(AHEAD):
                    split_weights()
                for _ in range(KD):
                    used_up()
                squares(H, T2, ready=h_ready)
                root_mean(T2, D)
                split_inputs(HID, T2)
                with n.loop(FF_GROUPS, FF2_PER):
                    for m in range(KD):
                        used_up()
                    for m in range(KD):
                        used_up()
            act.wait_ge(layer_begun, n.next(layer_begun))
            act.dma_start(out, H[:, :, META:]).then_inc(out_done, 16)
            act.wait_ge(out_done, 16)

        @block.vector
        def _(dve):
            n = Counts(dve)
            at = {"unit": 0}
            for b in range(2):
                dve.sem_inc(unit_free[b], 1)
            for b in range(3):
                dve.sem_inc(s_free[b], 1)
            dve.sem_inc(o_free, 1)
            dve.sem_inc(bw_used, 1)
            for b in range(2):
                dve.sem_inc(pair_free[b], 1)
                dve.sem_inc(c_free[b], 1)
            dve.sem_inc(co_free, 1)
            dve.sem_inc(qk_free, 1)

            def take():
                b = at["unit"] % 2
                at["unit"] += 1
                return b, n.next(unit_done[b])

            def col(name, k):
                return v1[:, V1[name] + k:V1[name] + k + 1]

            def rest_of_input(src, rest, tok, k):
                dve.wait_ge(lead_ready, n.next(lead_ready))
                dve.tensor_tensor(tok.of(rest[:, k, :]), tok.of(src[:, k, :]), tok.of(Uh[:, k, :].bitcast(F32)),
                                  ALU.subtract).then_inc(u_ready, 1)

            def invert(tok, side=0, root=0):
                dve.wait_ge(rms_ready, n.next(rms_ready))
                dve.reciprocal(inverses[0:tok.rows, side, 0:tok.tiles], roots[0:tok.rows, root, 0:tok.tiles])
                dve.drain().then_inc(inv_ready, 1)

            def inverse_rms(tok, root=0, squares=KD):
                if root == 0:
                    dve.wait_ge(sq_ready, n.next(sq_ready))
                    total = tok.of(HID[:, 0, :])
                    for k in range(1, squares):
                        dve.wait_ge(sq_ready, n.next(sq_ready))
                        dve.tensor_tensor(total, total, tok.of(HID[:, k, :]), ALU.add)
                        dve.drain()
                    dve.drain().then_inc(sum_ready, 1)
                take()
                invert(tok, root=root)
                b, done = take()
                dve.wait_ge(unit_done[b], done)
                return b

            def norm(gains, tok, dst, rest=None, keep=False):
                b = inverse_rms(tok)
                for k in range(KD):
                    ins = dve.scalar_tensor_tensor(tok.of(dst[:, k, :]), tok.of(H[:, k, :]), gains(k), psum_of(b, tok),
                                                   ALU.mult, ALU.mult)
                    ins.then_inc(u_ready if rest is None else whole_ready, 1)
                    if rest is not None and k > 0:
                        rest_of_input(dst, rest, tok, k - 1)
                if keep:
                    dve.tensor_copy(tok.of(rstd), psum_of(b, tok))
                dve.drain().then_inc(unit_free[b], 1)
                if rest is not None:
                    rest_of_input(dst, rest, tok, KD - 1)

            def hidden(b, done, m, tok):
                x = tok.of(relu[:, m % 2, :])
                dve.wait_ge(unit_done[b], done)
                dve.tensor_scalar(x, psum_of(b, tok), 0.0, None, ALU.max).then_inc(unit_free[b], 1)
                dve.drain()
                dve.tensor_tensor(x, x, x, ALU.mult)
                dve.drain()
                dve.tensor_copy(tok.of(HIDh[:, m, :]), x)
                dve.drain()
                dve.tensor_tensor(tok.of(HIDl[:, m, :]), x, tok.of(HIDh[:, m, :].bitcast(F32)), ALU.subtract).then_inc(hid_ready, 1)
                n.next(hid_ready)

            def norm_and_add(gain, tok):
                b = inverse_rms(tok)
                for k in range(KD):
                    dve.scalar_tensor_tensor(tok.of(M[:, k, :]), tok.of(M[:, k, :]), col(gain, k), psum_of(b, tok),
                                             ALU.mult, ALU.mult)
                dve.drain().then_inc(unit_free[b], 1)
                for k in range(KD):
                    dve.tensor_tensor(tok.of(H[:, k, :]), tok.of(H[:, k, :]), tok.of(M[:, k, :]), ALU.add).then_inc(h_ready, 1)

            dve.wait_ge(vec_in, 32)
            dve.tensor_scalar(nsinks[:, :], sinks[:, :], -1.0, None, ALU.mult)
            dve.wait_ge(bias_in, 48)
            for h in range(2):
                b, done = take()
                dve.wait_ge(unit_done[b], done)
                dve.tensor_tensor(brow[:, h * 512:(h + 1) * 512], ps[0:16, 2 * b, :], addm[:, h * 512:(h + 1) * 512],
                                  ALU.add).then_inc(unit_free[b], 1)
            dve.drain().then_inc(brow_ready, 1)
            dve.wait_ge(x_in, 48)
            norm(lambda k: col("g_pre_mix", k), T1, U)
            take()
            take()

            def copy_values(dst):
                dve.wait_ge(tr_done[1], n.next(tr_done[1]))
                dve.tensor_copy(dst[:, 2:4, :], ps[:, 3, 0:2 * P].rearrange("p (j d) -> p j d", d=P)).then_inc(eT_ready[1], 1)

            copy_values(va)

            def maxima(hd, t):
                banded, half = HEADS[hd]
                i = hd % 2
                for b in range(QB):
                    u = (hd * QB + b) % 3
                    keys = key_blocks(banded, b)
                    wd = len(keys) * P
                    c = 384 - P * b + keys[0] * P
                    dve.wait_ge(s_done[u], n.next(s_done[u]))
                    dve.scalar_tensor_tensor(ss[:, i, b, 0:wd], ps[:, 4 + u, 0:wd], DH ** -0.5, bw[:, hd, c:c + wd],
                                             ALU.mult, ALU.add).then_inc(s_free[u], 1)
                dve.drain()
                for b in range(QB):
                    wd = len(key_blocks(banded, b)) * P
                    dve.tensor_reduce(nmax[:, i, b:b + 1], ss[:, i, b, 0:wd], AX, ALU.max, negate=True)
                if banded:
                    dve.drain()
                    dve.tensor_tensor(nms[:, i, :], nmax[:, i, :], nsinks[:, bass.ds(t + 4 * half, 1)].to_broadcast([P, 4]), ALU.min)
                    dve.drain()
                    dve.tensor_tensor(srel[:, i, :], nms[:, i, :], sinks[:, bass.ds(t + 4 * half, 1)].to_broadcast([P, 4]), ALU.add)
                dve.drain().then_inc(max_ready, 1)

            def outputs(hd, t):
                banded, half = HEADS[hd]
                i = hd % 2
                for b in (1, 3):
                    wd = len(key_blocks(banded, b)) * P
                    dve.wait_ge(tr_done[1], n.next(tr_done[1]))
                    dve.tensor_copy(eT[:, 1, 0:wd], ps[:, 3, 0:wd]).then_inc(eT_ready[1], 1)
                dve.wait_ge(exp_ready, n.next(exp_ready))
                total = den
                if banded:
                    dve.tensor_tensor(den2[:, i, :], den[:, i, :], esink[:, i, :], ALU.add)
                    total = den2
                    dve.drain()
                dve.reciprocal(rinv[:, i, :], total[:, i, :])
                dve.drain()
                dve.wait_ge(o_done, n.next(o_done))
                at_col = t * DH + 256 * half if banded else t * P + 512 + DH * half
                dve.tensor_tensor(otok[:, :, bass.ds(at_col, DH)], ps[:, 7, 0:QB * DH].rearrange("p (b d) -> p b d", d=DH),
                                  rinv[:, i, :].unsqueeze(2).to_broadcast([P, QB, DH]), ALU.mult).then_inc(o_free, 1)

            with n.loop(4, ATT_PER) as t:
                for _ in range(4):
                    take()
                copy_values(vb)
                dve.wait_ge(bw_in, n.next(bw_in, 64))
                maxima(0, t)
                maxima(1, t)
                outputs(0, t)
                maxima(2, t)
                outputs(1, t)
                maxima(3, t)
                dve.drain().then_inc(bw_used, 1)
                outputs(2, t)
                outputs(3, t)

            dve.wait_ge(osq_ready, 1)
            dve.reciprocal(r8[:, :], rms8[:, :])
            dve.drain()
            for b in range(QB):
                for half in range(2):
                    o = otok[:, b, half * 512:(half + 1) * 512]
                    dve.tensor_scalar(o, o, r8[:, 2 * b + half:2 * b + half + 1], None, ALU.mult)
            dve.drain().then_inc(on_ready, 1)
            for f in range(1, KD, 2):
                dve.wait_ge(tr_done[1], n.next(tr_done[1]))
                dve.tensor_scalar(HID[:, f, META:].rearrange("p (b q) -> p b q", q=P),
                                  ps[:, 3, :].rearrange("p (b q) -> p b q", q=P)[:, :, ::-1],
                                  col("g_out", f), None, ALU.mult).then_inc(oT_ready[1], 1)
                dve.drain().then_inc(whole_ready, 1)
                rest_of_input(HID, Ul1, T1, f - 1)
                rest_of_input(HID, Ul1, T1, f)
            for m in range(KD):
                take()
            norm_and_add("g_post_mix", T1)
            norm(lambda k: col("g_pre_mlp", k), T1, HID, Ul1)
            dve.wait_ge(m_zero, 1)
            with n.loop(FF_GROUPS, FF_PER):
                for m in range(KD):
                    hidden(*take(), m, T1)
                for m in range(KD):
                    b, done = take()
                    dve.wait_ge(unit_done[b], done)
                    dve.tensor_tensor(T1.of(M[:, m, :]), T1.of(M[:, m, :]), psum_of(b, T1), ALU.add).then_inc(unit_free[b], 1)
                dve.drain()
            for m in range(KD):
                dve.sem_inc(m_ready, 1)
            norm_and_add("g_post_mlp", T1)
            dve.drain()
            for k in range(KD):
                dve.sem_inc(whole_ready, 1)
            for k in range(KD):
                rest_of_input(H, Ul1, T1, k)
            dve.wait_ge(pt_lead, 1)
            for k in range(2):
                dve.tensor_tensor(ptl[:, k, :], pt[:, k, :], pth[:, k, :].bitcast(F32), ALU.subtract)
            dve.drain().then_inc(pt_ready, 1)
            for m in range(KD):
                take()
            for m in range(KD):
                b, done = take()
                dve.wait_ge(gate_ready, n.next(gate_ready))
                dve.wait_ge(unit_done[b], done)
                dve.tensor_tensor(T1.of(M[:, m, :]), psum_of(b, T1), T1.of(HID[:, m, :]), ALU.mult).then_inc(unit_free[b], 1)
                dve.drain().then_inc(m_ready, 1)
            norm_and_add("g_post_ple", T1)

            def col2(name, k=0, rows=P):
                return v2[0:rows, V2[name] + k:V2[name] + k + 1]

            def gated(dst, sig):
                b, done = take()
                dve.wait_ge(unit_done[b], done)
                dve.wait_ge(sig_ready, n.next(sig_ready))
                dve.tensor_tensor(dst, psum_of(b, T2), T2.of(sig), ALU.mult).then_inc(unit_free[b], 1)

            pairm3 = pairm[:, :].rearrange("p (l t) -> p l t", t=GCH)

            def level_operands(level):
                size, i = 2 ** (level - 1), level % 2
                dve.tensor_tensor(level_blocks(lq[i], size, 1), level_blocks(qg_, size, 1), level_blocks(pre, size, 1), ALU.mult)
                dve.tensor_tensor(level_blocks(lk[i], size, 0), level_blocks(kk, size, 0), level_blocks(suf, size, 0), ALU.mult)
                dve.drain().then_inc(level_ready, 1)

            def level_up(level):
                size = 2 ** (level - 1)
                dve.tensor_tensor(level_blocks(suf, size, 0), level_blocks(suf, size, 0), level_total(pre, size, 1), ALU.mult)
                dve.drain()
                dve.tensor_tensor(level_blocks(pre, size, 1), level_blocks(pre, size, 1), level_total(pre, size, 0), ALU.mult)
                dve.drain()

            def select_pairs(level):
                b = level % 2
                dve.drain()
                mask = pairm3[:, level, :].unsqueeze(1).to_broadcast([P, CHUNKS_G, GCH])
                dve.wait_ge(pair_done[b], n.next(pair_done[b]))
                dve.sem_inc(passed, 1)
                dve.copy_predicated(amat, mask, ps[:, 4 + b, :].rearrange("p (c t) -> p c t", t=GCH)).then_inc(pair_free[b], 1)

            def select_tails():
                for level in range(5):
                    dve.drain()
                    dve.copy_predicated(atail, pairm3[0:META, level, 0:META], ps[0:META, 6, level * META:(level + 1) * META])

            dve.wait_ge(consts2_in, 96)
            dve.tensor_copy(pairm[:, :], pairf)
            dve.drain()
            with n.loop(LAYERS, LAYER_PER) as layer:
                dve.tensor_copy(v2[:, :], v2all[:, bass.ds(layer, 1), :].rearrange("p o c -> p (o c)"))
                dve.drain().then_inc(layer_begun, 1)
                lb01 = v2[:, V2["lb0"]:V2["lb0"] + 8].rearrange("p (l h) -> p l h", l=2)
                dve.tensor_tensor(lb_max, lb01[:, 0, :], lb01[:, 1, :], ALU.max)
                dve.drain()
                dve.tensor_tensor(lb_e, lb01, lb_max.unsqueeze(1).to_broadcast([P, 2, 4]), ALU.subtract)
                dve.drain().then_inc(lb_max_ready, 1)
                dve.wait_ge(lb_exp_ready, n.next(lb_exp_ready))
                dve.tensor_tensor(lb_sum, lb_e[:, 0, :], lb_e[:, 1, :], ALU.add)
                dve.drain()
                dve.reciprocal(lb_sum, lb_sum)
                dve.drain()
                dve.tensor_tensor(lb_e, lb_e, lb_sum.unsqueeze(1).to_broadcast([P, 2, 4]), ALU.mult)
                dve.drain()
                dve.scalar_tensor_tensor(oml, lb_e[:, 1, :], col2("second"), lb_e[:, 0, :], ALU.mult, ALU.add)
                dve.drain()
                dve.tensor_tensor(oml, oml, lb_e[:, 0, :], ALU.subtract)
                dve.drain()
                dve.tensor_scalar(oml, oml, -1.0, 1.0, ALU.mult, ALU.add)

                dve.drain()
                norm(lambda k: col2("norm1", k), T2, HID, Ul2, keep=True)
                with n.loop(2, CONV_PER) as c:
                    for j in range(2):
                        take()
                        gated(hc[:, bass.ds(2 * c + j, 1), TAPS - 1:].rearrange("p o (h n) -> p (o h) n", h=2), relu[:, j, :])
                dve.drain()
                dve.wait_ge(hc_padded, n.next(hc_padded))
                for k in range(TAPS):
                    for t in range(CONV_TILES):
                        x, wk = hc[:, t, k:k + T], col2("conv_w", t * TAPS + k)
                        if k == 0:
                            ins = dve.tensor_scalar(za[:, t, :], x, wk, col2("conv_b", t), ALU.mult, ALU.add)
                        else:
                            ins = dve.scalar_tensor_tensor(za[:, t, :], x, wk, za[:, t, :], ALU.mult, ALU.add)
                        if k == TAPS - 1:
                            ins.then_inc(conv_ready, 1)
                    dve.drain()
                with n.loop(6, GATE_PER):
                    for _ in range(4):
                        take()
                for _ in range(4):
                    b, done = take()
                dve.wait_ge(unit_done[b], done)
                for k in range(KD):
                    dve.scalar_tensor_tensor(U[:, k, :], H[:, k, :], col2("norm1", k), rstd[:, :], ALU.mult, ALU.mult).then_inc(u_ready, 1)
                take()
                dve.wait_ge(mean_ready, n.next(mean_ready))
                for t in range(CONV_TILES):
                    dve.tensor_tensor(za[:, t, :], za[:, t, :], mu, ALU.subtract)
                dve.drain().then_inc(centred, 1)
                b = inverse_rms(T2, squares=CONV_TILES)
                n.next(sq_ready, 3)
                for t in range(CONV_TILES):
                    dve.scalar_tensor_tensor(T2.of(za[:, t, :]), T2.of(za[:, t, :]), col2("ln_g", t), psum_of(b, T2),
                                             ALU.mult, ALU.mult)
                dve.drain().then_inc(unit_free[b], 1)
                dve.drain().then_inc(ln_ready, 1)
                for root, count, names in ((1, 2, "q_a"), (2, 1, "kv_a")):
                    b = inverse_rms(T2, root)
                    for k in range(count):
                        x = T2.of(cq[:, k, :] if count == 2 else ckv)
                        dve.scalar_tensor_tensor(x, x, col2(names, k), psum_of(b, T2), ALU.mult, ALU.mult)
                    dve.drain().then_inc(unit_free[b], 1)
                dve.drain().then_inc(c_ready, 1)
                dve.wait_ge(lnsig_ready, n.next(lnsig_ready))
                for t in range(CONV_TILES):
                    dve.scalar_tensor_tensor(za[:, t, :], za[:, t, :], col2("ln_b", t), Hs[t], ALU.add, ALU.mult)

                def values():
                    take()
                    take()
                    gated(T2.of(vT), Hs[6])

                def one_of(x, i):
                    return x[:, i:i + 1] if isinstance(i, int) else x[:, bass.ds(i, 1)]

                def recur(h, following):
                    dve.drain()
                    dve.tensor_copy(headcol[:, 0:1], one_of(oml, h))
                    dve.tensor_copy(headcol[:, 1:2], one_of(v2, h + V2["hgrn_g"]))
                    dve.memset(suf, 1.0)
                    dve.drain()
                    dve.wait_ge(f_sig, n.next(f_sig))
                    dve.tensor_scalar(kk, relu[:, 0, :], headcol[:, 0:1], None, ALU.mult)
                    dve.drain()
                    dve.tensor_scalar(pre, kk, CLAMP, -1.0, ALU.min, ALU.mult)
                    dve.drain()
                    dve.tensor_scalar(pre, pre, 1.0, None, ALU.add)
                    dve.drain()
                    dve.wait_ge(q_ready, n.next(q_ready))
                    dve.tensor_copy(qg_, relu[:, 1, :])
                    dve.drain().then_inc(qg_ready, 1)
                    level_operands(1)
                    level_up(1)
                    level_operands(2)
                    level_up(2)
                    select_pairs(0)
                    select_pairs(1)
                    level_operands(3)
                    level_up(3)
                    for level in range(4, LEVELS + 1):
                        select_pairs(level - 2)
                        level_operands(level)
                        level_up(level)
                        if level == 6:
                            select_tails()
                    dve.tensor_tensor(qfull, qg_, pre, ALU.mult)
                    dve.tensor_tensor(kfull[:, 0:S], kk[:, 0:S], suf[:, 0:S], ALU.mult)
                    select_pairs(LEVELS - 1)
                    select_pairs(LEVELS)
                    dve.drain().then_inc(a_ready, 1)
                    dve.wait_ge(upd_done, n.next(upd_done))
                    dve.tensor_copy(state[:, 1, :], ps[:, 6, 0:GCH])
                    for c in range(1, CHUNKS_G):
                        dve.drain()
                        dve.scalar_tensor_tensor(state[:, c + 1, :], state[:, c, :], pre[:, (c + 1) * GCH - 1:(c + 1) * GCH],
                                                 ps[:, 6, c * GCH:(c + 1) * GCH], ALU.mult, ALU.add)
                    dve.drain().then_inc(state_ready, 1)
                    if following:
                        values()
                    invert(T2)
                    dve.wait_ge(spread_done, n.next(spread_done))
                    dve.scalar_tensor_tensor(T2.of(oT), T2.of(oT), headcol[:, 1:2], ps[:, 6:8, 0:T2.width], ALU.mult, ALU.mult)
                    if following:
                        dve.drain().then_inc(v_ready, 1)
                    else:
                        dve.drain()
                    dst = zc[:, h, :] if isinstance(h, int) else zc[:, bass.ds(h, 1), :].rearrange("p o t -> p (o t)")
                    dve.tensor_tensor(dst, oT, gs, ALU.mult)
                    if following:
                        dve.drain()
                        gated(T2.of(gs), Hs[5])

                values()
                dve.drain().then_inc(v_ready, 1)
                gated(T2.of(gs), Hs[5])
                with n.loop(HEADS_G - 1, GREC_PER) as h:
                    recur(h, True)
                recur(HEADS_G - 1, False)

                dve.drain().then_inc(zc_ready, 1)
                dve.drain().then_inc(mlaw_used, 1)

                def rotated(src, dst, side):
                    take()
                    dve.tensor_tensor(dst, src, cosT, ALU.mult)
                    invert(T2, side, root=side)
                    b, done = take()
                    dve.wait_ge(unit_done[b], done)
                    dve.tensor_tensor(T2.of(rot1), psum_of(b, T2, QK), T2.of(sinT), ALU.mult).then_inc(unit_free[b], 1)
                    dve.drain()
                    dve.tensor_tensor(dst, dst, rot1, ALU.add)
                    dve.drain()

                def divided(dst):
                    b, done = take()
                    dve.wait_ge(unit_done[b], done)
                    dve.tensor_tensor(T2.of(dst), T2.of(dst), psum_of(b, T2, QK), ALU.mult).then_inc(unit_free[b], 1)

                def causal_maxima(hd):
                    for i in range(QT):
                        e = exps_of(hd, i)
                        if i < QT - 1:
                            b, wd = i % 2, (i + 1) * P
                            dve.wait_ge(c_done[b], n.next(c_done[b]))
                            dve.scalar_tensor_tensor(e[:, 0:wd], ps[:, 4 + b, 0:wd], QK ** -0.5, triT[:, S - i * P:S + P],
                                                     ALU.mult, ALU.add).then_inc(c_free[b], 1)
                        else:
                            for b in range(2):
                                dve.wait_ge(c_done[b], n.next(c_done[b]))
                                dve.scalar_tensor_tensor(T2.part(e, b), ps[0:META, 4 + b, 0:T2.width], QK ** -0.5,
                                                         triT[0:META, b * T2.width:(b + 1) * T2.width],
                                                         ALU.mult, ALU.add).then_inc(c_free[b], 1)
                    dve.drain()
                    for i in range(QT):
                        e = exps_of(hd, i)[:, 0:min((i + 1) * P, T)]
                        rows = P if i < QT - 1 else META
                        dve.tensor_reduce(qmax[0:rows, hd, i:i + 1], e, AX, ALU.max, negate=True)
                    dve.drain().then_inc(qmax_ready, 1)

                def causal_outputs(hd, at_col):
                    for i in range(QT):
                        if (hd * QT + i) % 2 == 1:
                            copy_causal_tile(dve, n, i)
                    dve.wait_ge(qexp_ready, n.next(qexp_ready))
                    dve.reciprocal(qinv[:, hd, 0:QT - 1], qden[:, hd, 0:QT - 1])
                    dve.reciprocal(qinv[0:META, hd, QT - 1:QT], qden[0:META, hd, QT - 1:QT])
                    dve.drain()
                    dve.wait_ge(co_done, n.next(co_done))
                    cols = bass.ds(at_col + hd * DH, DH)
                    dve.tensor_tensor(otok2[:, 0:QT - 1, cols], ps[:, 6, 0:(QT - 1) * DH].rearrange("p (b d) -> p b d", d=DH),
                                      qinv[:, hd, 0:QT - 1].unsqueeze(2).to_broadcast([P, QT - 1, DH]), ALU.mult)
                    dve.tensor_scalar(otok2[0:META, QT - 1, cols], ps[0:META, 6, (QT - 1) * DH:QT * DH],
                                      qinv[0:META, hd, QT - 1:QT], None, ALU.mult)
                    dve.drain().then_inc(co_free, 1)

                def finish_queries_keys(hd):
                    take()
                    take()
                    dve.wait_ge(qk_raw, n.next(qk_raw, 2))
                    rotated(qgain, qh_of[hd], 0)
                    rotated(kgain, kh_of[hd], 1)
                    divided(qh_of[hd])
                    divided(kh_of[hd])
                    dve.drain().then_inc(qk_ready, 1)
                    dve.drain().then_inc(qk_free, 1)

                finish_queries_keys(0)
                finish_queries_keys(1)
                with n.loop(3, MLA_PER) as pair:
                    causal_maxima(0)
                    causal_maxima(1)
                    causal_outputs(0, pair * P)
                    finish_queries_keys(0)
                    causal_outputs(1, pair * P)
                    finish_queries_keys(1)
                causal_maxima(0)
                causal_maxima(1)
                causal_outputs(0, 3 * P)
                causal_outputs(1, 3 * P)
                for f in (1, 3):
                    dve.wait_ge(ctr_done[1], n.next(ctr_done[1]))
                    dve.tensor_copy(zb[:, f, 0:S], ps[:, TRB[1], :]).then_inc(cT_ready[1], 1)

                def gate_of(branch, m):
                    return gates[:, bass.ds(m + branch * KD, 1), :].rearrange("p o (h n) -> p (o h) n", h=2)

                def tile_of(x, m):
                    return x[:, bass.ds(m, 1), :].rearrange("p o (h n) -> p (o h) n", h=2)

                with n.loop(4, MIX_PER) as i:
                    for j in range(2):
                        m = 2 * i + j
                        mix, parts = T2.of(mixed), [T2.of(x) for x in (mixed, relu[:, 0, :], relu[:, 1, :])]
                        for branch in range(3):
                            b, done = take()
                            dve.wait_ge(unit_done[b], done)
                            dve.tensor_tensor(parts[branch], psum_of(b, T2), gate_of(branch, m), ALU.mult).then_inc(unit_free[b], 1)
                        for part in parts[1:]:
                            dve.drain()
                            dve.tensor_tensor(mix, mix, part, ALU.add)
                        dve.drain()
                        dve.tensor_copy(tile_of(Mh, m), mix)
                        dve.drain()
                        dve.tensor_tensor(tile_of(Ml, m), mix, tile_of(Mh, m).bitcast(F32), ALU.subtract)
                        dve.drain()
                dve.drain().then_inc(m_done, 1)
                for m in range(KD):
                    b, done = take()
                    dve.wait_ge(unit_done[b], done)
                    dve.tensor_tensor(T2.of(H[:, m, :]), T2.of(H[:, m, :]), psum_of(b, T2), ALU.add).then_inc(unit_free[b], 1)
                    dve.drain().then_inc(h_ready, 1)
                norm(lambda k: col2("norm2", k), T2, HID, Ul2)
                with n.loop(FF_GROUPS, FF2_PER):
                    for m in range(KD):
                        hidden(*take(), m, T2)
                    for m in range(KD):
                        b, done = take()
                        dve.wait_ge(unit_done[b], done)
                        dve.tensor_tensor(T2.of(H[:, m, :]), T2.of(H[:, m, :]), psum_of(b, T2), ALU.add).then_inc(unit_free[b], 1)
                    dve.drain()
            dve.drain().then_inc(layer_begun, 1)


def tiles_of(wt):
    k, m = wt.shape
    return wt.reshape(k // P, P, m // P, P).transpose(2, 1, 0, 3).reshape(m // P, P, k)


def columns(v):
    return np.ascontiguousarray(v.reshape(-1, P).T)


def layout_first(a):
    w_in = a["w_in"][0]
    head = lambda base, h: w_in[:, base + h * DH:base + (h + 1) * DH]
    q_a = tiles_of(np.concatenate([head(0, h) for t in range(4) for h in (t, t + 4)], axis=1))
    ka, va = tiles_of(w_in[:, 512:640]), tiles_of(w_in[:, 640:768])
    q_b, k_b, v_b = (tiles_of(w_in[:, 768 + 512 * i:1280 + 512 * i]) for i in range(3))
    chunks = [ka[0], va[0]]
    for t in range(4):
        chunks += [q_a[t], q_b[t], k_b[t], v_b[t]]
    chunks += list(tiles_of(a["w_o"][0]))
    up, down = tiles_of(a["w_up"][0]), a["w_down"][0]
    for g in range(FF_GROUPS):
        chunks += list(up[8 * g:8 * g + 8]) + list(tiles_of(down[D * g:D * (g + 1)]))
    chunks += list(tiles_of(a["w_ple_gate"][0]))
    ple = tiles_of(a["w_ple_proj"][0])
    chunks += [np.concatenate(list(ple[4 * i:4 * i + 4]), axis=1) for i in range(2)]
    assert len(chunks) == N1_CHUNKS
    return chunks


def layout_second(a):
    ring_chunks, head_chunks = [], []
    for l in range(LAYERS):
        wt = tiles_of(np.concatenate([a["w_in_2"][l][:, :1408], np.zeros((D, NOPE), np.float32), a["w_in_2"][l][:, 1408:1440],
                                      np.zeros((D, P - QK), np.float32), a["w_in_2"][l][:, 1440:]], axis=1))
        value, gate, latent, rec, gates = wt[0:4], wt[4:8], wt[8:12], wt[12:28], wt[28:52]
        for t in range(4):
            ring_chunks += [gate[t], value[t]]
        ring_chunks += list(gates) + list(latent)
        q, f, i, g = (rec[4 * k:4 * k + 4] for k in range(4))
        for h in range(HEADS_G):
            ring_chunks += [f[h], q[h], i[h], g[h]]
        uq, ukv = a["w_uq_2"][l], a["w_ukv_2"][l]
        for pair in range(4):
            c = np.zeros((P, 8, P), np.float32)
            for j in range(2):
                h = 2 * pair + j
                c[:, 3 * j:3 * j + 2, :QK] = uq[:, h * QK:(h + 1) * QK].reshape(2, P, QK).transpose(1, 0, 2)
                c[:, 3 * j + 2, :NOPE] = ukv[:, h * P:h * P + NOPE]
                c[:, 6, j * DH:(j + 1) * DH] = ukv[:, h * P + NOPE:(h + 1) * P]
            head_chunks.append(c.reshape(P, CH))
        conv, att, rec = (tiles_of(a[k][l]) for k in ("w_conv_out_2", "w_attn_out_2", "w_hgrn_out_2"))
        for m in range(KD):
            ring_chunks += [np.concatenate([conv[m], att[m]], axis=1),
                            np.concatenate([rec[m], np.zeros((P, 512), np.float32)], axis=1)]
        ring_chunks += list(tiles_of(a["w_out_2"][l]))
        up, down = tiles_of(a["w_ff1_2"][l]), a["w_ff2_2"][l]
        for g in range(FF_GROUPS):
            ring_chunks += list(up[8 * g:8 * g + 8]) + list(tiles_of(down[D * g:D * (g + 1)]))
    assert len(ring_chunks) == LAYERS * N2_CHUNKS
    return ring_chunks, head_chunks


def vectors_second(a):
    out = []
    for l in range(LAYERS):
        pad = lambda v: np.concatenate([v, np.zeros(P - QK, np.float32)])
        out.append(np.concatenate([
            columns(a["norm1_g_2"][l]),
            a["conv_w_2"][l].T.reshape(CONV_TILES, P, TAPS).transpose(1, 0, 2).reshape(P, -1),
            columns(a["conv_b_2"][l]), columns(a["conv_ln_g_2"][l]), columns(a["conv_ln_b_2"][l]),
            columns(a["q_a_norm_g_2"][l]), columns(a["kv_a_norm_g_2"][l]), columns(pad(a["q_norm_g_2"][l])),
            columns(pad(a["k_norm_g_2"][l])), columns(a["hgrn_lb_logits_2"][0]), columns(a["hgrn_lb_logits_2"][1]),
            np.full((P, 1), float(l), np.float32), columns(a["hgrn_norm_g_2"][l]), columns(a["norm2_g_2"][l])], axis=1))
    return np.stack(out, axis=1)


def rotary_constants():
    half = ROPE // 2
    freq = np.float32(10000.0) ** (-np.arange(half, dtype=np.float32) / np.float32(half))
    ang = (np.arange(T, dtype=np.float32)[None, :] * freq[:, None]).astype(np.float32)
    cosines, sines = np.ones((QK, T), np.float32), np.zeros((QK, T), np.float32)
    cosines[NOPE:] = np.concatenate([np.cos(ang)] * 2)
    sines[NOPE:] = np.concatenate([np.sin(ang)] * 2)
    turn = np.zeros((QK, QK), np.float32)
    for j in range(half):
        turn[NOPE + half + j, NOPE + j] = -1.0
        turn[NOPE + j, NOPE + half + j] = 1.0
    return cosines, sines, turn


def mask_constants():
    causal = np.zeros((P, 640), np.float32)
    causal[:, S:] = np.where(np.arange(P)[None, :] <= np.arange(P)[:, None], 0.0, NEG)
    s, t = np.arange(GCH)[:, None], np.arange(GCH)[None, :]
    masks = [s == t]
    for level in range(1, LEVELS + 1):
        size = 2 ** (level - 1)
        masks.append((s // (2 * size) == t // (2 * size)) & (s % (2 * size) < size) & (t % (2 * size) >= size))
    return causal, np.concatenate(masks, axis=1).astype(np.float32)


def distance_constants():
    rel = np.arange(REL) - 511
    n = np.abs(rel)
    large = 8 + (np.log(np.maximum(n, 1) / 8.0) / np.log(128.0) * 8).astype(np.int64)
    bucket = np.where(rel > 0, 16, 0) + np.where(n < 8, n, np.minimum(large, 15))
    onehot = (np.arange(32)[:, None] == bucket[None, :]).astype(np.float32)
    seen = np.zeros(REL)
    for window, dil in DILATED:
        seen += (rel % dil == 0) & (n <= window // 2)
    dilated = np.where(seen > 0, np.log(np.maximum(seen, 1)), NEG)
    banded = np.where(n <= WIN, 0.0, NEG)
    return onehot, np.stack([banded] * 8 + [dilated] * 8).astype(np.float32)


def kernel(**inputs):
    import concourse.bacc as _bacc
    from concourse.bass_utils import run_bass_kernel_spmd as _run

    a = {k: np.asarray(v) for k, v in inputs.items()}
    onehot, addmask = distance_constants()
    cosines, sines, turn = rotary_constants()
    causal, pairs = mask_constants()
    ring_chunks, head_chunks = layout_second(a)
    arrays = {
        "xT": a["x"][0].T.reshape(KD, P, S).transpose(1, 0, 2),
        "pT": a["p"][0, 0].T.reshape(2, P, S).transpose(1, 0, 2),
        "metaT": a["meta_2"].T.reshape(KD, P, META).transpose(1, 0, 2),
        "w": np.stack(layout_first(a) + ring_chunks + [np.zeros((P, CH), np.float32)] * AHEAD),
        "w_mla": np.stack(head_chunks),
        "vec1": np.concatenate([columns(v) for v in (
            a["g_pre_mix"][0], np.concatenate([a["g_out_a"][0], a["g_out_b"][0]]), a["g_post_mix"][0],
            a["g_pre_mlp"][0], a["g_post_mlp"][0], a["b_ple_gate"][0], a["g_post_ple"][0])], axis=1),
        "vec2": vectors_second(a),
        "table": a["rel_bias_table"],
        "onehot": onehot,
        "addmask": addmask,
        "sink": a["sink_a"],
        "cosines": cosines,
        "sines": sines,
        "turn": turn,
        "causal": causal,
        "pairs": pairs,
    }
    nc = _bacc.Bacc("TRN2", target_bir_lowering=False, num_devices=1)
    args = []
    for name, v in arrays.items():
        arrays[name] = np.ascontiguousarray(v)
        args.append(nc.dram_tensor(name, v.shape, F32, kind="ExternalInput").ap())
    out = nc.dram_tensor("out", (P, KD, S), F32, kind="ExternalOutput").ap()
    program(nc, *args, out)
    r = _run(nc, [arrays], core_ids=[0])
    got = r.results[0]["out"]
    return got.transpose(1, 0, 2).reshape(1, D, S).transpose(0, 2, 1)
```
